# Optimizing a Trainium2 kernel written in Bass

```python
import jax, jax.numpy as jnp
from jax import lax
import numpy as np

D_MODEL = 1024
BATCH = 1
SEQ = 4096
DEPTH = 1

CHUNK = 64
N_META = 16
WINDOW = 128
WIN_CHUNKS = WINDOW // CHUNK
HEAD_DIM = 64
N_Q_HEADS = 8
N_KV_HEADS = 2
Q_PER_KV = N_Q_HEADS // N_KV_HEADS
ATTN_WIDTH = N_Q_HEADS * HEAD_DIM
KV_WIDTH = N_KV_HEADS * HEAD_DIM
CONV_WIDTH = D_MODEL // 2
CONV_K = 3
N_BRANCH = 2
N_GROUPS = 4
EXPERTS_PER_GROUP = 8
N_EXPERTS = N_GROUPS * EXPERTS_PER_GROUP
TOP_K = 2
EXPERT_HIDDEN = D_MODEL // 2
LN_EPS = 1e-5
NEG_INF = -1e30
IN_WIDTHS = (ATTN_WIDTH, KV_WIDTH, KV_WIDTH, CONV_WIDTH, CONV_WIDTH, CONV_WIDTH, N_BRANCH * D_MODEL)
IN_COLS = sum(IN_WIDTHS)
IN_SPLITS = tuple(int(c) for c in np.cumsum(IN_WIDTHS)[:-1])

kernel_name = "hybrid_swa_sink_shortconv_hiermoe_deepnorm"

def _layernorm(x, g, b):
    xf = x.astype(jnp.float32)
    mu = jnp.mean(xf, axis=-1, keepdims=True)
    var = jnp.mean(jnp.square(xf - mu), axis=-1, keepdims=True)
    y = (xf - mu) * lax.rsqrt(var + LN_EPS) * g.astype(jnp.float32) + b.astype(jnp.float32)
    return y.astype(x.dtype)

def _alibi_slopes():
    s = 2.0 ** (-8.0 * (np.arange(N_Q_HEADS) + 1) / N_Q_HEADS)
    return jnp.asarray(s, dtype=jnp.float32).reshape(N_KV_HEADS, Q_PER_KV)

def _alibi_bias(qpos, kpos, valid):
    dist = jnp.abs(qpos[:, :, None] - kpos[:, None, :]).astype(jnp.float32)
    bias = -_alibi_slopes()[:, :, None, None, None] * dist
    return jnp.where(valid[:, None, :], bias, NEG_INF)

def _sink_attend(q, k, v, bias, sinks):
    s = jnp.einsum('bnqkgd,bnskd->bkgnqs', q.astype(jnp.float32), k.astype(jnp.float32))
    s = s * (HEAD_DIM ** -0.5) + bias
    sink = sinks.astype(jnp.float32).reshape(N_KV_HEADS, Q_PER_KV)[None, :, :, None, None, None]
    sink = jnp.broadcast_to(sink, s.shape[:-1] + (1,))
    p = jax.nn.softmax(jnp.concatenate([s, sink], axis=-1), axis=-1)[..., :-1]
    o = jnp.einsum('bkgnqs,bnskd->bnqkgd', p, v.astype(jnp.float32))
    return o.astype(q.dtype)

def _window_attention(q, k, v, sinks):
    B, L, _ = q.shape
    S = L - N_META
    nc = S // CHUNK
    q = q.reshape(B, L, N_KV_HEADS, Q_PER_KV, HEAD_DIM)
    k = k.reshape(B, L, N_KV_HEADS, HEAD_DIM)
    v = v.reshape(B, L, N_KV_HEADS, HEAD_DIM)
    qm, km, vm = q[:, :N_META], k[:, :N_META], v[:, :N_META]
    mpos = jnp.arange(N_META)
    bias_m = _alibi_bias(mpos[None], mpos[None], jnp.ones((1, N_META), dtype=bool))
    o_meta = _sink_attend(qm[:, None], km[:, None], vm[:, None], bias_m, sinks)[:, 0]
    qr = q[:, N_META:].reshape(B, nc, CHUNK, N_KV_HEADS, Q_PER_KV, HEAD_DIM)
    kr = k[:, N_META:].reshape(B, nc, CHUNK, N_KV_HEADS, HEAD_DIM)
    vr = v[:, N_META:].reshape(B, nc, CHUNK, N_KV_HEADS, HEAD_DIM)
    shifts = list(range(WIN_CHUNKS - 1, 0, -1))

    def _band(t, tm):
        pad = ((0, 0), (0, 0), (0, 0), (0, 0), (0, 0))
        parts = [jnp.broadcast_to(tm[:, None], (B, nc, N_META, N_KV_HEADS, HEAD_DIM))]
        for j in shifts:
            parts.append(jnp.pad(t, ((0, 0), (j, 0)) + pad[2:])[:, :nc])
        parts.append(t)
        return jnp.concatenate(parts, axis=2)

    kb, vb = _band(kr, km), _band(vr, vm)
    cidx = jnp.arange(nc)[:, None]
    cpos = N_META + cidx * CHUNK + jnp.arange(CHUNK)[None]
    kpos = jnp.concatenate([jnp.broadcast_to(mpos[None], (nc, N_META))]
                           + [cpos - j * CHUNK for j in shifts] + [cpos], axis=1)
    valid = jnp.concatenate([jnp.ones((nc, N_META), dtype=bool)]
                            + [jnp.broadcast_to(cidx >= j, (nc, CHUNK)) for j in shifts]
                            + [jnp.ones((nc, CHUNK), dtype=bool)], axis=1)
    o_real = _sink_attend(qr, kb, vb, _alibi_bias(cpos, kpos, valid), sinks)
    return jnp.concatenate([o_meta.reshape(B, N_META, ATTN_WIDTH),
                            o_real.reshape(B, S, ATTN_WIDTH)], axis=1)

def _causal_depthwise_conv(u, w):
    return lax.conv_general_dilated(u, w[:, None, :].astype(u.dtype), window_strides=(1,),
                                    padding=[(CONV_K - 1, 0)],
                                    dimension_numbers=('NWC', 'WIO', 'NWC'),
                                    feature_group_count=u.shape[-1])

def _mixer(h, w_in, sinks, conv_w, w_attn_out, w_conv_out, w_o):
    proj = h @ w_in
    q, k, v, cb, cc, ch, gates = jnp.split(proj, IN_SPLITS, axis=-1)
    y_attn = _window_attention(q, k, v, sinks) @ w_attn_out
    y_conv = (cb * _causal_depthwise_conv(cc * ch, conv_w)) @ w_conv_out
    g = jax.nn.sigmoid(gates.astype(jnp.float32)).astype(h.dtype)
    g_attn, g_conv = jnp.split(g, N_BRANCH, axis=-1)
    return (g_attn * y_attn + g_conv * y_conv) @ w_o

def _hier_moe(h, w_rg, b_rg, w_re, b_re, w_gate, w_up, w_down):
    B, L, D = h.shape
    xt = h.reshape(-1, D)
    T = xt.shape[0]
    g_prob = jax.nn.softmax((xt @ w_rg + b_rg).astype(jnp.float32), axis=-1)
    g_top, g_idx = lax.top_k(g_prob, 1)
    e_logits = (xt @ w_re + b_re).astype(jnp.float32).reshape(T, N_GROUPS, EXPERTS_PER_GROUP)
    sel = jnp.broadcast_to(g_idx[:, :, None], (T, 1, EXPERTS_PER_GROUP))
    e_in = jnp.take_along_axis(e_logits, sel, axis=1)[:, 0]
    e_top, e_loc = lax.top_k(e_in, TOP_K)
    weight = g_top * jax.nn.softmax(e_top, axis=-1)
    eid = (g_idx * EXPERTS_PER_GROUP + e_loc).reshape(-1)
    tok = jnp.repeat(jnp.arange(T), TOP_K)
    order = jnp.argsort(eid)
    sizes = jnp.bincount(eid, length=N_EXPERTS).astype(jnp.int32)
    tok_s = tok[order]
    xs = xt[tok_s]
    a = jax.nn.silu(lax.ragged_dot(xs, w_gate, sizes)) * lax.ragged_dot(xs, w_up, sizes)
    ys = lax.ragged_dot(a, w_down, sizes) * weight.reshape(-1)[order][:, None].astype(h.dtype)
    out = jnp.zeros_like(xt).at[tok_s].add(ys)
    return out.reshape(B, L, D)

def setup_inputs(seed: int = 0) -> dict:
    key = jax.random.key(seed)
    ks = jax.random.split(key, 24)
    f32 = jnp.float32
    beta = (8.0 * DEPTH) ** -0.25
    nrm = lambda k, shape, s: jax.random.normal(k, shape, f32) * s
    D = D_MODEL
    col_scale = np.ones((IN_COLS,), np.float32)
    v0 = ATTN_WIDTH + KV_WIDTH
    col_scale[v0:v0 + KV_WIDTH] = beta
    w_in = nrm(ks[2], (DEPTH, D, IN_COLS), D ** -0.5) * jnp.asarray(col_scale)
    return {
        "x": nrm(ks[0], (BATCH, SEQ, D), 1.0),
        "meta_tokens": nrm(ks[1], (N_META, D), 1.0),
        "ln0_g": 1.0 + nrm(ks[3], (D,), 0.02),
        "ln0_b": nrm(ks[4], (D,), 0.02),
        "w_in": w_in,
        "attn_sinks": nrm(ks[5], (DEPTH, N_Q_HEADS), 1.0),
        "conv_w": nrm(ks[6], (DEPTH, CONV_K, CONV_WIDTH), CONV_K ** -0.5),
        "w_attn_out": nrm(ks[7], (DEPTH, ATTN_WIDTH, D), beta * ATTN_WIDTH ** -0.5),
        "w_conv_out": nrm(ks[8], (DEPTH, CONV_WIDTH, D), beta * CONV_WIDTH ** -0.5),
        "w_o": nrm(ks[9], (DEPTH, D, D), beta * D ** -0.5),
        "ln1_g": 1.0 + nrm(ks[10], (DEPTH, D), 0.02),
        "ln1_b": nrm(ks[11], (DEPTH, D), 0.02),
        "w_router_group": nrm(ks[12], (DEPTH, D, N_GROUPS), D ** -0.5),
        "b_router_group": nrm(ks[13], (DEPTH, N_GROUPS), 0.01),
        "w_router_expert": nrm(ks[14], (DEPTH, D, N_EXPERTS), D ** -0.5),
        "b_router_expert": nrm(ks[15], (DEPTH, N_EXPERTS), 0.01),
        "w_exp_gate": nrm(ks[16], (DEPTH, N_EXPERTS, D, EXPERT_HIDDEN), D ** -0.5),
        "w_exp_up": nrm(ks[17], (DEPTH, N_EXPERTS, D, EXPERT_HIDDEN), D ** -0.5),
        "w_exp_down": nrm(ks[18], (DEPTH, N_EXPERTS, EXPERT_HIDDEN, D), beta * EXPERT_HIDDEN ** -0.5),
        "ln2_g": 1.0 + nrm(ks[19], (DEPTH, D), 0.02),
        "ln2_b": nrm(ks[20], (DEPTH, D), 0.02),
    }

def reference(x, meta_tokens, ln0_g, ln0_b, w_in, attn_sinks, conv_w, w_attn_out, w_conv_out,
              w_o, ln1_g, ln1_b, w_router_group, b_router_group, w_router_expert,
              b_router_expert, w_exp_gate, w_exp_up, w_exp_down, ln2_g, ln2_b):
    alpha = (2.0 * DEPTH) ** 0.25
    B = x.shape[0]
    meta = jnp.broadcast_to(meta_tokens[None].astype(x.dtype), (B, N_META, D_MODEL))
    h = _layernorm(jnp.concatenate([meta, x], axis=1), ln0_g, ln0_b)
    for l in range(DEPTH):
        mix = _mixer(h, w_in[l], attn_sinks[l], conv_w[l], w_attn_out[l], w_conv_out[l], w_o[l])
        h = _layernorm(alpha * h + mix, ln1_g[l], ln1_b[l])
        ffn = _hier_moe(h, w_router_group[l], b_router_group[l], w_router_expert[l],
                        b_router_expert[l], w_exp_gate[l], w_exp_up[l], w_exp_down[l])
        h = _layernorm(alpha * h + ffn, ln2_g[l], ln2_b[l])
    return h[:, N_META:]


_drawn_inputs = setup_inputs


def setup_inputs(seed=0):
    import zlib

    import numpy as np

    out = dict(_drawn_inputs(seed))
    spreads = {}
    factors = {'meta_tokens': 64.0,
     'attn_sinks': 33.031,
     'b_router_group': 27.268,
     'b_router_expert': 22.361,
     'ln2_g': 8.065,
     'ln2_b': 8.377,
     'w_attn_out': 4.239}
    for name, (base, spread) in spreads.items():
        noise = np.random.default_rng([zlib.crc32(name.encode()), seed]).standard_normal(out[name].shape)
        drawn = base * np.exp(spread * noise) if base else spread * noise
        out[name] = __import__('jax').numpy.asarray(drawn.astype(out[name].dtype))
    for name, factor in factors.items():
        out[name] = (out[name] * factor).astype(out[name].dtype)
    return out
```

```python
import concourse.bass as bass
from concourse import mybir
from contextlib import ExitStack
import math

FP32 = mybir.dt.float32
F32R = mybir.dt.float32r
I32 = mybir.dt.int32
ALU = mybir.AluOpType
ACT = mybir.ActivationFunctionType
AX = mybir.AxisListType.X

P = 128
ALPHA = 2.0 ** 0.25
LN_EPS = 1e-5
NEG_INF = -1e30
CHUNK = 64
HEAD = 64
HEADS = 8
PAIRS = HEADS // 2
TAPS = 3

TOK = 512
TILES = TOK // P


def hold(eng, sem, value):
    eng.wait_ge(sem, value)
    eng.nop(nofuse=True)


def layernorm_stats(v, rows, x, stats, moments, ln_step, step0, ln_moments):
    half = x.shape[1] // 2
    v.bn_stats(stats[0:rows, 0, :], x[:, 0:half])
    v.bn_stats(stats[0:rows, 1, :], x[:, half:2 * half]).then_inc(ln_step, 1)
    hold(v, ln_step, step0 + 1)
    v.bn_aggr(moments[0:rows, :], stats[0:rows, :, :]).then_inc(ln_moments, 1)


def rsqrt(po, rows, moments, rstd, minus_half, ln_rstd, count):
    po.tensor_scalar(rstd[0:rows, :], moments[0:rows, 1:2], LN_EPS, None, ALU.add).then_inc(ln_rstd, 1)
    po.wait_ge(ln_rstd, count + 1)
    po.tensor_tensor(rstd[0:rows, :], rstd[0:rows, :], minus_half[0:rows, :], ALU.pow).then_inc(ln_rstd, 1)


def mixer(nc, t, x, w_in, w_attn_out, w_conv_out, w_o, h1):
    D = x.shape[1]
    S = x.shape[0]
    KD = D // P
    BLOCKS = S // TOK
    AW = w_attn_out.shape[0]
    CW = w_conv_out.shape[0]
    KA, KC = AW // P, CW // P
    KVW = 128
    META = t["meta"].shape[0]
    PREV = META + CHUNK
    KEYS = PREV + P

    Q0, K0, V0 = 0, AW, AW + KVW
    CB0 = V0 + KVW
    CC0, CH0 = CB0 + CW, CB0 + 2 * CW
    GA0 = CB0 + 3 * CW
    GC0 = GA0 + D

    w_in_k = w_in.rearrange("(k p) n -> p k n", p=P)
    w_ao_k = w_attn_out.rearrange("(k p) n -> p k n", p=P)
    w_co_k = w_conv_out.rearrange("(k p) n -> p k n", p=P)
    w_o_k = w_o.rearrange("(k p) n -> p k n", p=P)

    strips = [("k", 0), ("v", 0)] + [("q", i) for i in range(PAIRS)]
    for i in range(KC):
        strips += [("cc", i), ("ch", i), ("cb", i)]
    for j in range(KD):
        strips += [("ga", j), ("gc", j), ("out", j)]
    for n in range(2):
        strips += [("wo", 4 * n + k) for k in range(4)]
    N = len(strips)
    RAW = 5
    assert N % RAW == 0 and N % 2 == 0
    CONV0 = 2 + PAIRS
    MIX0 = CONV0 + 3 * KC
    WO0 = MIX0 + 3 * KD
    UNITS = 2 * TILES
    base_col = {"k": K0, "v": V0, "cc": CC0, "ch": CH0, "cb": CB0, "ga": GA0, "gc": GC0}

    outputs = []
    for s, (kind, i) in enumerate(strips):
        if kind == "out":
            outputs += [(s, 0), (s, 1)]
        elif kind != "wo":
            outputs += [(s, 0)]
    NOUT = len(outputs)
    assert NOUT % 2 == 0
    out_no = {o: n for n, o in enumerate(outputs)}
    by_act = {"k", "v", "q", "cc", "ga", "gc"}
    act_outs = [o for o in outputs if strips[o[0]][0] in by_act]
    dve_outs = [o for o in outputs if strips[o[0]][0] not in by_act]

    def strip_dmas(kind, i, raw):
        full = raw.rearrange("p (k c) -> p k c", k=KD)
        if kind == "q":
            return [(full[:, :, g * HEAD:(g + 1) * HEAD],
                     w_in_k[:, :, Q0 + (i + 4 * g) * HEAD:Q0 + (i + 4 * g + 1) * HEAD]) for g in range(2)]
        if kind == "out":
            return [(full[:, 0:KA, :], w_ao_k[:, :, i * P:(i + 1) * P]),
                    (full[:, KA:KA + KC, :], w_co_k[:, :, i * P:(i + 1) * P])]
        if kind == "wo":
            n, k = i // 4, i % 4
            return [(raw.rearrange("p (k c) -> p k c", k=2),
                     w_o_k[:, 2 * k:2 * k + 2, n * TOK:(n + 1) * TOK])]
        c = base_col[kind] + i * P
        return [(full, w_in_k[:, :, c:c + P])]

    with ExitStack() as ctx:
        def sb(name, shape, dt=FP32):
            return ctx.enter_context(nc.sbuf_tensor(name, shape, dt))

        def sem(name):
            return ctx.enter_context(nc.semaphore(name))

        raw = sb("raw", [P, RAW, D])
        w_hi = sb("w_hi", [P, 2, D], F32R)
        w_lo = sb("w_lo", [P, 2, D], F32R)
        xs = sb("x_rows", [P, TILES, D])
        h = sb("h_rows", [P, TILES, D])
        hT_hi = sb("hT_hi", [P, KD, TOK], F32R)
        hT_lo = sb("hT_lo", [P, KD, TOK], F32R)
        kT = sb("kT", [P, CHUNK + TOK])
        vT = sb("vT", [P, CHUNK + TOK])
        kmT = sb("kmT", [P, META])
        vBT = sb("vBT", [P, TILES, PREV])
        bias = sb("bias", [P, HEADS, KEYS])
        bias_prev = sb("bias_prev", [P // 2, HEADS, CHUNK])
        meta_step = sb("meta_step", [P, HEADS, META])
        sinks = sb("sinks", [P, HEADS])
        oT_hi = sb("oT_hi", [P, KA, TOK], F32R)
        oT_lo = sb("oT_lo", [P, KA, TOK], F32R)
        zT_hi = sb("zT_hi", [P, KC, TOK], F32R)
        zT_lo = sb("zT_lo", [P, KC, TOK], F32R)
        work = [sb(f"work{i}", [P, TOK + 2]) for i in range(4)]
        u_tail = sb("u_tail", [P, KC, 2])
        cw = sb("conv_taps", [P, KC, TAPS])
        ident = sb("ident", [P, P])
        g0, b0 = sb("ln0_gain", [P, D]), sb("ln0_bias", [P, D])
        g1, b1 = sb("ln1_gain", [P, D]), sb("ln1_bias", [P, D])
        stats = sb("stats", [P, 2, 6])
        moments = sb("moments", [P, 2])
        rstd = sb("rstd", [P, 1])
        minus_half = sb("minus_half", [P, 1])
        top = sb("top", [P, 4])
        neg_top = sb("neg_top", [P, 2, 4])
        sink_gap = sb("sink_gap", [P, 2, 4])
        den = sb("den", [P, 2, HEADS])
        sink_e = sb("sink_e", [P, 2, HEADS])
        rden = sb("rden", [P, HEADS])
        shared = -(-nc.sbuf_base // 32) * 32
        arena = sb("arena", [P, 2 * KD * TOK])

        def place(at, name, shape, dt=FP32):
            size = 4 * math.prod(shape[1:])
            assert at[0] + size <= shared + 4 * 2 * KD * TOK
            placed = nc.alloc_sbuf_tensor_at(name, shape, dt, offset=at[0])
            at[0] += size
            return placed

        at = [shared]
        qT = place(at, "qT", [P, PAIRS, TOK])
        prob = place(at, "prob", [P, 2, 4, KEYS])
        pTa = place(at, "pTa", [P, 2, 4 * P])
        pTb = place(at, "pTb", [P, 2, 4 * P])
        o_rows = place(at, "o_rows", [P, AW])
        v_own = place(at, "v_own", [P, TILES, KVW])
        v_before = place(at, "v_before", [P, TILES, KVW])
        at = [shared]
        mT_hi = place(at, "mixT_hi", [P, KD, TOK], F32R)
        mT_lo = place(at, "mixT_lo", [P, KD, TOK], F32R)

        banks = [ctx.enter_context(nc.psum_tensor(f"bank{i}", [P, TOK], FP32)) for i in range(8)]
        pj = banks[0:2]
        quad = banks[2:6]
        tp = banks[6:8]

        with ExitStack() as c1, nc.Block() as block:
            def sem1(name):
                return c1.enter_context(nc.semaphore(name))
            meta_in, consts_in, x_in = sem1("meta_in"), sem1("consts_in"), sem1("x_in")
            raw_in = [sem1(f"meta_raw_in{i}") for i in range(RAW)]
            raw_used = sem1("meta_raw_used")
            ln_step, ln_moments, ln_rstd, ln_normed, ln_scaled, ln_done = (
                sem1("ln_step"), sem1("ln_moments"), sem1("ln_rstd"), sem1("ln_normed"),
                sem1("ln_scaled"), sem1("ln_done"))
            pool_step, dve_step = sem1("pool_step"), sem1("dve_step")
            ident_ready, dist_ready = sem1("ident_ready"), sem1("dist_ready")
            tp_ready, tp_taken_act, tp_taken_dve = sem1("tp_ready"), sem1("tp_taken_act"), sem1("tp_taken_dve")
            pj_ready, pj_taken = sem1("mpj_ready"), sem1("mpj_taken")

            meta_strips = [("k", 0), ("v", 0)] + [s for i in range(KC) for s in (("cc", i), ("ch", i))]
            hm = h[0:META, 0, :]
            hmT = work[0][:, 0:KD * META].rearrange("p (k m) -> p k m", k=KD)
            lns = [(META, hm)] + [(P, xs[:, i, :]) for i in range(TILES)]

            @block.sync
            def _(sp):
                sp.dma_start(hm, t["meta"]).then_inc(meta_in, 16)
                for dst, src in ((g0, t["ln0_g"]), (b0, t["ln0_b"]), (g1, t["ln1_g"]), (b1, t["ln1_b"])):
                    sp.dma_start(dst[:, :], src.unsqueeze(0).to_broadcast([P, D])).then_inc(consts_in, 16)
                sp.dma_start(rden[:, :], t["sinks"].unsqueeze(0).to_broadcast([P, HEADS])).then_inc(consts_in, 16)
                for k in range(TAPS):
                    sp.dma_start(cw[:, :, k], t["conv_w"][k].rearrange("(i p) -> p i", p=P),
                                 allow_slow_non_contiguous=True).then_inc(consts_in, 16)
                sp.dma_start(xs[:, :, :], x[0:TOK, :].rearrange("(t p) d -> p t d", p=P)).then_inc(x_in, 16)
                for n, (kind, i) in enumerate(meta_strips):
                    if n >= RAW:
                        sp.wait_ge(raw_used, n - RAW + 1)
                    for dst, src in strip_dmas(kind, i, raw[:, n % RAW, :]):
                        sp.dma_start(dst, src).then_inc(raw_in[n % RAW], 16)

            @block.gpsimd
            def _(po):
                steps = [0]

                def link(ins):
                    steps[0] += 1
                    ins.then_inc(pool_step, 1)
                    po.wait_ge(pool_step, steps[0])

                po.memset(minus_half[:, :], -0.5)
                link(po.memset(ident[:, :], 0.0))
                po.affine_select(out=ident[:, :], in_=ident[:, :], compare_op=ALU.not_equal, fill=1.0, base=0,
                                 pattern=[[-1, P]], channel_multiplier=1).then_inc(ident_ready, 1)
                dist = work[1]
                link(po.iota(dist[:, 0:META], pattern=[[-1, META]], base=META, channel_multiplier=1,
                             allow_small_or_imprecise_dtypes=True))
                po.iota(dist[:, META:KEYS], pattern=[[-1, CHUNK + P]], base=CHUNK, channel_multiplier=1,
                        allow_small_or_imprecise_dtypes=True).then_inc(dist_ready, 1)
                po.wait_ge(dist_ready, 2)
                for i in range(PAIRS):
                    for g in range(2):
                        slope = 2.0 ** (-8.0 * (i + 4 * g + 1) / HEADS)
                        hh = 2 * i + g
                        link(po.tensor_scalar(bias[:, hh, :], dist[:, 0:KEYS], -slope, None, ALU.mult))
                        link(po.memset(meta_step[:, hh, :], -slope * P))
                link(po.tensor_copy(bias_prev[:, :, :], bias[0:CHUNK, :, META:PREV]))
                link(po.memset(bias[:, :, META:PREV], NEG_INF))
                link(po.memset(bias[0:CHUNK, :, PREV + CHUNK:KEYS], NEG_INF))
                po.wait_ge(consts_in, 16 * (5 + TAPS))
                link(po.tensor_copy(sinks[:, :].rearrange("p (i g) -> p i g", g=2),
                                    rden[:, :].rearrange("p (g i) -> p i g", g=2)))
                for n, (rows, xx) in enumerate(lns):
                    po.wait_ge(ln_moments, n + 1)
                    rsqrt(po, rows, moments, rstd, minus_half, ln_rstd, 2 * n)
                    po.wait_ge(ln_normed, n + 1)
                    po.tensor_tensor(xx, xx, g0[0:rows, :], ALU.mult).then_inc(ln_scaled, 1)
                    po.wait_ge(ln_scaled, n + 1)
                    po.tensor_tensor(xx, xx, b0[0:rows, :], ALU.add).then_inc(ln_done, 1)

            @block.vector
            def _(v):
                v.wait_ge(dist_ready, 1)
                v.scalar_tensor_tensor(out=work[1][:, 0:KEYS], in0=work[1][:, 0:KEYS], scalar=-1.0,
                                       in1=work[1][:, 0:KEYS], op0=ALU.mult, op1=ALU.max).then_inc(dist_ready, 1)
                v.memset(kT[:, :], 0.0)
                v.memset(vT[:, :], 0.0)
                for n, (rows, xx) in enumerate(lns):
                    v.wait_ge(meta_in if n == 0 else x_in, 16)
                    layernorm_stats(v, rows, xx, stats, moments, ln_step, n, ln_moments)
                    v.wait_ge(ln_moments, n + 1)
                    v.wait_ge(ln_rstd, 2 * n + 2)
                    v.tensor_scalar(xx, xx, moments[0:rows, 0:1], rstd[0:rows, 0:1], ALU.subtract, ALU.mult)\
                     .then_inc(ln_normed, 1)
                    if n == 0:
                        v.wait_ge(tp_ready, 1)
                        v.tensor_copy(hmT, tp[0][:, 0:KD * META].rearrange("p (k m) -> p k m", k=KD))\
                         .then_inc(tp_taken_dve, 1)
                    else:
                        for half in range(2):
                            q = 2 * (n - 1) + half
                            v.wait_ge(tp_taken_act, q + 1)
                            dst = (slice(None), slice(4 * half, 4 * half + 4), slice((n - 1) * P, n * P))
                            v.tensor_tensor(hT_lo[dst], tp[q % 2][:, :].rearrange("p (k c) -> p k c", k=4),
                                            hT_hi[dst].bitcast(FP32), ALU.subtract).then_inc(tp_taken_dve, 1)
                v.memset(h[:, :, :], 0.0)
                for n, (kind, i) in enumerate(meta_strips):
                    v.wait_ge(pj_ready, n + 1)
                    got = pj[n % 2][:, 0:META]
                    if kind == "k":
                        v.tensor_copy(kmT[:, :], got).then_inc(pj_taken, 1)
                    elif kind == "v":
                        v.tensor_copy(vBT[:, :, 0:META], got.unsqueeze(1).to_broadcast([P, TILES, META]))\
                         .then_inc(pj_taken, 1)
                    elif kind == "cc":
                        v.tensor_copy(u_tail[:, i, :], got[:, META - 2:META]).then_inc(pj_taken, 1)
                    else:
                        v.wait_ge(pj_taken, n)
                        v.tensor_tensor(u_tail[:, i, :], u_tail[:, i, :], got[:, META - 2:META], ALU.mult)\
                         .then_inc(pj_taken, 1)

            @block.scalar
            def _(a):
                for n in range(1, len(lns)):
                    for half in range(2):
                        q = 2 * (n - 1) + half
                        a.wait_ge(tp_ready, q + 2)
                        a.activation(hT_hi[:, 4 * half:4 * half + 4, (n - 1) * P:n * P],
                                     tp[q % 2][:, :].rearrange("p (k c) -> p k c", k=4), ACT.Copy)\
                         .then_inc(tp_taken_act, 1)

            @block.tensor
            def _(pe):
                pe.wait_ge(ident_ready, 1)
                pe.wait_ge(ln_done, 1)
                for k in range(KD):
                    mm = pe.transpose(tp[0][:, k * META:(k + 1) * META], hm[:, k * P:(k + 1) * P],
                                      ident[0:META, 0:META])
                mm.then_inc(tp_ready, 1)
                for n in range(1, len(lns)):
                    pe.wait_ge(ln_done, n + 1)
                    for half in range(2):
                        q = 2 * (n - 1) + half
                        pe.wait_ge(tp_taken_dve, max(1, q))
                        for k in range(4):
                            mm = pe.transpose(tp[q % 2][:, k * P:(k + 1) * P],
                                              xs[:, n - 1, (4 * half + k) * P:(4 * half + k + 1) * P], ident[:, :])
                        mm.then_inc(tp_ready, 1)
                uses = [0] * RAW
                for n, (kind, i) in enumerate(meta_strips):
                    uses[n % RAW] += 16 * len(strip_dmas(kind, i, raw[:, 0, :]))
                    pe.wait_ge(raw_in[n % RAW], uses[n % RAW])
                    if n >= 2:
                        pe.wait_ge(pj_taken, n - 1)
                    for k in range(KD):
                        mm = pe.matmul(pj[n % 2][:, 0:META], raw[:, n % RAW, k * P:(k + 1) * P], hmT[:, k, :],
                                       start=(k == 0), stop=(k == KD - 1))
                    mm.then_inc(pj_ready, 1)
                    pe.wait_ge(pj_ready, n + 1)
                    pe.nop().then_inc(raw_used, 1)

        raw_in = [sem(f"raw_in{i}") for i in range(RAW)]
        x_in = [sem(f"x_in{i}") for i in range(TILES)]
        h1_out = [sem(f"h1_out{i}") for i in range(TILES)]
        hi_ready = sem("hi_ready")
        lo_ready = sem("lo_ready")
        strip_done = sem("strip_done")
        branch_ready = sem("branch_ready")
        pj_taken = [sem(f"pj_taken{i}") for i in range(2)]
        carried = sem("carried")
        vbt_ready = sem("vbt_ready")
        v_ready, v_taken = sem("v_ready"), sem("v_taken")
        s_ready, s_prep = sem("s_ready"), sem("s_prep")
        p_ready = sem("p_ready")
        pT_ready, pTa_taken, pTb_taken = sem("pT_ready"), sem("pTa_taken"), sem("pTb_taken")
        o_ready, o_taken = sem("o_ready"), sem("o_taken")
        oT_ready, oThi_ready, oTlo_ready = sem("oT_ready"), sem("oThi_ready"), sem("oTlo_ready")
        z_ready, zhi_ready, zlo_ready = sem("z_ready"), sem("zhi_ready"), sem("zlo_ready")
        m_ready, mhi_ready, mlo_ready = sem("m_ready"), sem("mhi_ready"), sem("mlo_ready")
        wo_ready, wo_taken = sem("wo_ready"), sem("wo_taken")
        hx_ready, hx_hi, hx_lo = sem("hx_ready"), sem("hx_hi"), sem("hx_lo")
        ln_step, ln_moments, ln_rstd, ln_normed, ln_scaled, ln_done = (
            sem("ln_step2"), sem("ln_moments2"), sem("ln_rstd2"), sem("ln_normed2"), sem("ln_scaled2"),
            sem("ln_done2"))
        h_copied = sem("h_copied")
        dve_step = sem("dve_step2")

        LN1_AT = {1 + i: i for i in range(TILES)}
        LN0_AT = {MIX0 + 2 + 3 * i: i for i in range(TILES)}
        HX_AT = {WO0 + i: i for i in range(2 * TILES)}
        LNS = 2 * TILES

        def raw_uses(s, b):
            per = lambda ss: 16 * len(strip_dmas(*strips[ss], raw[:, 0, :]))
            slot = s % RAW
            in_block = sum(per(q) for q in range(slot, N, RAW))
            return b * in_block + sum(per(q) for q in range(slot, s + 1, RAW))

        with nc.Block() as block:
            @block.sync
            def _(sp):
                with sp.Fori(0, BLOCKS) as b:
                    for s, (kind, i) in enumerate(strips):
                        hold(sp, lo_ready, b * N + s + 1)
                        for dst, src in strip_dmas(kind, i, raw[:, s % RAW, :]):
                            sp.dma_start(dst, src).then_inc(raw_in[s % RAW], 16)
                        if s - 3 in LN1_AT:
                            i1 = LN1_AT[s - 3]
                            hold(sp, ln_done, b * LNS + i1 + 1)
                            sp.dma_start(h1[bass.ds(b * TOK + i1 * P, P), :], h[:, i1, :]).then_inc(h1_out[i1], 16)
                        if s - 8 in LN1_AT:
                            i1 = LN1_AT[s - 8]
                            hold(sp, h_copied, b * TILES + i1 + 1)
                            nxt = (b + 1) % BLOCKS
                            sp.dma_start(xs[:, i1, :], x[bass.ds(nxt * TOK + i1 * P, P), :]).then_inc(x_in[i1], 16)
                for i1 in range(TILES):
                    sp.wait_ge(ln_done, BLOCKS * LNS + i1 + 1)
                    sp.dma_start(h1[BLOCKS * TOK + i1 * P:BLOCKS * TOK + (i1 + 1) * P, :], h[:, i1, :])\
                      .then_inc(h1_out[i1], 16)
                for i1 in range(TILES):
                    sp.wait_ge(h1_out[i1], 16 * (BLOCKS + 1))

            @block.gpsimd
            def _(po):
                def scale(n, i1, rows, gain, shift):
                    hold(po, ln_moments, n + 1)
                    rsqrt(po, P, moments, rstd, minus_half, ln_rstd, 2 * n)
                    po.wait_ge(ln_normed, n + 1)
                    po.tensor_tensor(rows[:, i1, :], rows[:, i1, :], gain[:, :], ALU.mult).then_inc(ln_scaled, 1)
                    po.wait_ge(ln_scaled, n + 1)
                    po.tensor_tensor(rows[:, i1, :], rows[:, i1, :], shift[:, :], ALU.add).then_inc(ln_done, 1)

                with po.Fori(0, BLOCKS) as b:
                    for i1 in range(TILES):
                        scale(b * LNS + i1, i1, h, g1, b1)
                    for i1 in range(TILES):
                        hold(po, h1_out[i1], 16 * b + 16)
                        po.tensor_copy(h[:, i1, :], xs[:, i1, :]).then_inc(h_copied, 1)
                    for i1 in range(TILES):
                        scale(b * LNS + TILES + i1, i1, xs, g0, b0)
                for i1 in range(TILES):
                    scale(BLOCKS * LNS + i1, i1, h, g1, b1)

            @block.scalar
            def _(a):
                def split_hi(b, s):
                    a.wait_ge(raw_in[s % RAW], raw_uses(s, b))
                    a.wait_ge(strip_done, b * N + s + 1)
                    a.activation(w_hi[:, s % 2, :], raw[:, s % RAW, :], ACT.Copy).then_inc(hi_ready, 1)

                def take(b, s):
                    kind, i = strips[s]
                    n = out_no[(s, 0)]
                    got, taken_act = pj[n % 2][:, :], pj_taken[n % 2]
                    if kind in ("k", "v"):
                        a.wait_ge(carried, b + 1)
                    a.wait_ge(strip_done, b * N + s + 3)
                    if kind == "k":
                        a.activation(kT[:, CHUNK:], got, ACT.Copy).then_inc(taken_act, 1)
                    elif kind == "v":
                        a.activation(vT[:, CHUNK:], got, ACT.Copy).then_inc(taken_act, 1)
                    elif kind == "q":
                        a.activation(qT[:, i, :], got, ACT.Copy).then_inc(taken_act, 1)
                    elif kind == "cc":
                        a.activation(work[0][:, 0:TOK], got, ACT.Copy).then_inc(taken_act, 1)
                    elif kind in ("ga", "gc"):
                        w = work[0] if kind == "ga" else work[1]
                        a.activation(w[:, 0:TOK], got, ACT.Sigmoid).then_inc(taken_act, 1)

                with a.Fori(0, BLOCKS) as b:
                    split_hi(b, 0)
                    for s, (kind, i) in enumerate(strips):
                        n = s - CONV0
                        if s == CONV0:
                            a.wait_ge(v_ready, b * 2 + 1)
                            a.activation(v_own[:, :, :], tp[0][:, :].rearrange("p (t c) -> p t c", t=TILES),
                                         ACT.Copy).then_inc(v_taken, 1)
                            a.wait_ge(v_ready, b * 2 + 2)
                            a.activation(v_before[0:PREV, :, :],
                                         tp[1][0:PREV, :].rearrange("p (t c) -> p t c", t=TILES),
                                         ACT.Copy).then_inc(v_taken, 1)
                        if n >= 4 and n % 2 == 0 and (n - 4) // 2 < TILES:
                            tt = (n - 4) // 2
                            a.wait_ge(oT_ready, b * TILES + tt + 1)
                            a.activation(oT_hi[:, :, tt * P:(tt + 1) * P],
                                         quad[3][:, :].rearrange("p (k c) -> p k c", k=KA),
                                         ACT.Copy).then_inc(oThi_ready, 1)
                        if 0 <= n < UNITS:
                            a.wait_ge(s_prep, b * UNITS + n + 1)
                            tt, half = n // 2, n % 2
                            for q in range(4):
                                hh = 4 * half + q
                                head = hh // 2 + 4 * (hh % 2)
                                a.activation(prob[:, n % 2, q, :], prob[:, n % 2, q, :], ACT.Exp,
                                             bias=neg_top[:, n % 2, q:q + 1],
                                             accum_out=den[:, tt % 2, head:head + 1])
                            a.activation(sink_e[:, tt % 2, :].rearrange("p (g i) -> p i g", g=2)
                                         [:, 2 * half:2 * half + 2, :],
                                         sink_gap[:, n % 2, :].rearrange("p (i g) -> p i g", g=2), ACT.Exp)\
                             .then_inc(p_ready, 1)
                        if s + 1 < N:
                            split_hi(b, s + 1)
                        if kind in by_act:
                            take(b, s)
                        if kind == "cb":
                            a.wait_ge(z_ready, b * KC + i + 1)
                            a.activation(zT_hi[:, i, :], work[3][:, 0:TOK], ACT.Copy).then_inc(zhi_ready, 1)
                        if kind == "out":
                            a.wait_ge(m_ready, b * KD + i + 1)
                            a.activation(mT_hi[:, i, :], work[2][:, 0:TOK], ACT.Copy).then_inc(mhi_ready, 1)
                        if 1 <= n <= UNITS:
                            a.wait_ge(pT_ready, b * UNITS + n)
                            a.activation(pTa[:, (n - 1) % 2, :], tp[0][:, :], ACT.Copy).then_inc(pTa_taken, 1)
                        if s in HX_AT:
                            q = HX_AT[s]
                            a.wait_ge(hx_ready, b * 2 * TILES + q + 1)
                            a.activation(hT_hi[:, 4 * (q % 2):4 * (q % 2) + 4, (q // 2) * P:(q // 2 + 1) * P],
                                         tp[q % 2][:, :].rearrange("p (k c) -> p k c", k=4), ACT.Copy)\
                             .then_inc(hx_hi, 1)

            DVE_STEPS = 3 * UNITS + 1 + TILES + 2 * TILES + 4 * KC

            @block.vector
            def _(v):
                def layernorm(n, i1, rows):
                    layernorm_stats(v, P, rows[:, i1, :], stats, moments, ln_step, n, ln_moments)
                    v.wait_ge(ln_moments, n + 1)
                    v.wait_ge(ln_rstd, 2 * n + 2)
                    v.tensor_scalar(rows[:, i1, :], rows[:, i1, :], moments[:, 0:1], rstd[:, 0:1],
                                    ALU.subtract, ALU.mult).then_inc(ln_normed, 1)

                v.sem_inc(lo_ready, RAW)
                v.sem_inc(strip_done, 2)
                v.sem_inc(pj_taken[0], 1)
                v.sem_inc(pj_taken[1], 1)
                v.sem_inc(wo_taken, 1)
                v.sem_inc(hx_lo, 1)
                with v.Fori(0, BLOCKS) as b:
                    steps = [0]

                    def link(ins):
                        steps[0] += 1
                        ins.then_inc(dve_step, 1)
                        v.wait_ge(dve_step, b * DVE_STEPS + steps[0])

                    def split_lo(s):
                        v.wait_ge(hi_ready, b * N + s + 1)
                        v.tensor_tensor(w_lo[:, s % 2, :], raw[:, s % RAW, :], w_hi[:, s % 2, :].bitcast(FP32),
                                        ALU.subtract).then_inc(lo_ready, 1)

                    def output(s, part=0):
                        n = out_no[(s, part)]
                        if strips[s][0] == "out" and part == 0:
                            v.wait_ge(branch_ready, b * KD + strips[s][1] + 1)
                        else:
                            v.wait_ge(strip_done, b * N + s + 3)
                        return pj[n % 2][:, :], pj_taken[n % 2], b * (NOUT // 2) + n // 2 + 2

                    def taken_by_act(s):
                        n = out_no[(s, 0)]
                        v.wait_ge(pj_taken[n % 2], b * (NOUT // 2) + n // 2 + 2)

                    v.tensor_copy(kT[:, 0:CHUNK], kT[:, TOK:TOK + CHUNK])
                    v.tensor_copy(vT[:, 0:CHUNK], vT[:, TOK:TOK + CHUNK]).then_inc(carried, 1)
                    split_lo(0)
                    for s, (kind, i) in enumerate(strips):
                        n = s - CONV0
                        if s in LN1_AT:
                            if s == 1:
                                v.wait_ge(wo_taken, b * 2 * TILES + 1)
                            layernorm(b * LNS + LN1_AT[s], LN1_AT[s], h)
                        if s in LN0_AT:
                            v.wait_ge(x_in[LN0_AT[s]], b * 16 + 16)
                            layernorm(b * LNS + TILES + LN0_AT[s], LN0_AT[s], xs)
                        if n >= 4 and n % 2 == 0 and (n - 4) // 2 < TILES:
                            tt = (n - 4) // 2
                            v.wait_ge(oThi_ready, b * TILES + tt + 1)
                            v.tensor_tensor(oT_lo[:, :, tt * P:(tt + 1) * P],
                                            quad[3][:, :].rearrange("p (k c) -> p k c", k=KA),
                                            oT_hi[:, :, tt * P:(tt + 1) * P].bitcast(FP32),
                                            ALU.subtract).then_inc(oTlo_ready, 1)
                        if 0 <= n < UNITS:
                            tt, half = n // 2, n % 2
                            v.wait_ge(s_ready, b * UNITS + n + 1)
                            for g in range(2):
                                ins = v.scalar_tensor_tensor(
                                    out=prob[:, n % 2, g:4:2, :],
                                    in0=quad[g][:, 0:2 * KEYS].rearrange("p (q c) -> p q c", q=2),
                                    scalar=HEAD ** -0.5, in1=bias[:, 4 * half + g:4 * half + 4:2, :],
                                    op0=ALU.mult, op1=ALU.add)
                            link(ins)
                            link(v.tensor_reduce(top[:, :], prob[:, n % 2, :, :], AX, ALU.max))
                            link(v.tensor_tensor(top[:, :], top[:, :], sinks[:, 4 * half:4 * half + 4], ALU.max))
                            v.tensor_tensor(sink_gap[:, n % 2, :], sinks[:, 4 * half:4 * half + 4], top[:, :],
                                            ALU.subtract)
                            v.tensor_scalar(neg_top[:, n % 2, :], top[:, :], -1.0, None, ALU.mult)\
                             .then_inc(s_prep, 1)
                            if n == 1:
                                link(v.tensor_copy(bias[0:CHUNK, :, META:PREV], bias_prev[:, :, :]))
                            if half == 1:
                                link(v.tensor_tensor(bias[:, :, 0:META], bias[:, :, 0:META], meta_step[:, :, :],
                                                     ALU.add))
                        if 3 <= n <= UNITS + 1 and n % 2 == 1:
                            tt = (n - 3) // 2
                            v.wait_ge(o_ready, b * TILES + tt + 1)
                            link(v.tensor_tensor(rden[:, :], den[:, tt % 2, :], sink_e[:, tt % 2, :], ALU.add))
                            link(v.reciprocal(rden[:, :], rden[:, :]))
                            v.tensor_tensor(o_rows[:, :].rearrange("p (h c) -> p h c", h=HEADS),
                                            quad[2][:, :].rearrange("p (h c) -> p h c", h=HEADS),
                                            rden[:, :].unsqueeze(2).to_broadcast([P, HEADS, HEAD]), ALU.mult)\
                             .then_inc(o_taken, 1)
                        if s + 1 < N:
                            split_lo(s + 1)
                        if s == 2:
                            taken_by_act(1)
                            v.tensor_copy(vBT[:, :, META:PREV],
                                          vT[:, 0:TOK].rearrange("p (t c) -> p t c", t=TILES)[:, :, 0:CHUNK])\
                             .then_inc(vbt_ready, 1)
                        if kind == "ch":
                            taken_by_act(s - 1)
                            v.tensor_copy(work[2][:, 0:2], u_tail[:, i, :])
                            got, taken, count = output(s)
                            v.tensor_tensor(work[2][:, 2:TOK + 2], got, work[0][:, 0:TOK], ALU.mult).then_inc(taken, 1)
                            v.wait_ge(taken, count)
                            link(v.tensor_scalar(work[1][:, 0:TOK], work[2][:, 0:TOK], cw[:, i, 0:1], None, ALU.mult))
                            for k in (1, 2):
                                link(v.scalar_tensor_tensor(
                                    out=work[1][:, 0:TOK], in0=work[2][:, k:k + TOK], scalar=cw[:, i, k:k + 1],
                                    in1=work[1][:, 0:TOK], op0=ALU.mult, op1=ALU.add))
                            link(v.tensor_copy(u_tail[:, i, :], work[2][:, TOK:TOK + 2]))
                        if kind == "cb":
                            got, taken, count = output(s)
                            v.tensor_tensor(work[3][:, 0:TOK], got, work[1][:, 0:TOK], ALU.mult).then_inc(taken, 1)
                            v.wait_ge(taken, count)
                            v.sem_inc(z_ready, 1)
                            v.wait_ge(zhi_ready, b * KC + i + 1)
                            v.tensor_tensor(zT_lo[:, i, :], work[3][:, 0:TOK], zT_hi[:, i, :].bitcast(FP32),
                                            ALU.subtract).then_inc(zlo_ready, 1)
                        if kind == "out":
                            taken_by_act(s - 1)
                            got, taken, _ = output(s, 0)
                            v.tensor_tensor(work[2][:, 0:TOK], got, work[0][:, 0:TOK], ALU.mult).then_inc(taken, 1)
                            got, taken, count = output(s, 1)
                            v.tensor_tensor(work[3][:, 0:TOK], got, work[1][:, 0:TOK], ALU.mult).then_inc(taken, 1)
                            v.wait_ge(taken, count)
                            v.tensor_tensor(work[2][:, 0:TOK], work[2][:, 0:TOK], work[3][:, 0:TOK], ALU.add)\
                             .then_inc(m_ready, 1)
                            v.wait_ge(mhi_ready, b * KD + i + 1)
                            v.tensor_tensor(mT_lo[:, i, :], work[2][:, 0:TOK], mT_hi[:, i, :].bitcast(FP32),
                                            ALU.subtract).then_inc(mlo_ready, 1)
                        if 1 <= n <= UNITS:
                            v.wait_ge(pT_ready, b * UNITS + n)
                            v.tensor_copy(pTb[0:PREV, (n - 1) % 2, :], tp[1][0:PREV, :]).then_inc(pTb_taken, 1)
                        if s in HX_AT:
                            q = HX_AT[s]
                            v.wait_ge(hx_hi, b * 2 * TILES + q + 1)
                            dst = (slice(None), slice(4 * (q % 2), 4 * (q % 2) + 4),
                                   slice((q // 2) * P, (q // 2 + 1) * P))
                            v.tensor_tensor(hT_lo[dst], tp[q % 2][:, :].rearrange("p (k c) -> p k c", k=4),
                                            hT_hi[dst].bitcast(FP32), ALU.subtract).then_inc(hx_lo, 1)
                        if kind == "wo" and i % 4 == 3:
                            half = i // 4
                            if half == 0:
                                v.wait_ge(h_copied, b * TILES + TILES)
                            for tt in range(TILES):
                                if tt == TILES - 1:
                                    v.wait_ge(strip_done, b * N + s + 3)
                                else:
                                    v.wait_ge(wo_ready, (b * 2 + half) * (TILES - 1) + tt + 1)
                                part = h[:, tt, half * TOK:(half + 1) * TOK]
                                v.scalar_tensor_tensor(out=part, in0=part, scalar=ALPHA, in1=quad[tt][:, :],
                                                       op0=ALU.mult, op1=ALU.add).then_inc(wo_taken, 1)
                    assert steps[0] == DVE_STEPS
                v.wait_ge(wo_taken, BLOCKS * 2 * TILES + 1)
                for i1 in range(TILES):
                    layernorm(BLOCKS * LNS + i1, i1, h)

            @block.tensor
            def _(pe):
                def product(out, hi, lo, x_hi, x_lo, first, last):
                    pe.matmul(out, hi, x_hi, start=first, stop=False)
                    pe.matmul(out, hi, x_lo, start=False, stop=False)
                    return pe.matmul(out, lo, x_hi, start=False, stop=last)

                with pe.Fori(0, BLOCKS) as b:
                    pe.wait_ge(hx_lo, b * 2 * TILES + 1)
                    for s, (kind, i) in enumerate(strips):
                        n = s - CONV0
                        if s == CONV0:
                            taken = out_no[(s - 1, 0)]
                            pe.wait_ge(pj_taken[taken % 2], b * (NOUT // 2) + taken // 2 + 2)
                            for tt in range(TILES):
                                mm = pe.transpose(tp[0][:, tt * KVW:(tt + 1) * KVW],
                                                  vT[:, CHUNK + tt * P:CHUNK + (tt + 1) * P], ident[:, :])
                            mm.then_inc(v_ready, 1)
                            pe.wait_ge(vbt_ready, b + 1)
                            for tt in range(TILES):
                                mm = pe.transpose(tp[1][0:PREV, tt * KVW:(tt + 1) * KVW], vBT[:, tt, :], ident[:, :])
                            mm.then_inc(v_ready, 1)
                            pe.wait_ge(carried, b + 1)
                            pe.wait_ge(wo_taken, b * 2 * TILES + 1)
                        if n >= 4 and n % 2 == 0 and (n - 4) // 2 < TILES:
                            tt = (n - 4) // 2
                            pe.wait_ge(o_taken, b * TILES + tt + 1)
                            if tt:
                                pe.wait_ge(oTlo_ready, b * TILES + tt)
                            for k in range(KA):
                                mm = pe.transpose(quad[3][:, k * P:(k + 1) * P], o_rows[:, k * P:(k + 1) * P],
                                                  ident[:, :])
                            mm.then_inc(oT_ready, 1)
                        if 0 <= n < UNITS:
                            tt, half = n // 2, n % 2
                            if n:
                                pe.wait_ge(s_prep, b * UNITS + n)
                            for q in range(2):
                                for g in range(2):
                                    rows = slice(g * HEAD, (g + 1) * HEAD)
                                    qh = qT[rows, 2 * half + q, tt * P:(tt + 1) * P]
                                    pe.matmul(quad[g][:, q * KEYS:q * KEYS + META], qh, kmT[rows, :],
                                              start=True, stop=True)
                                    mm = pe.matmul(quad[g][:, q * KEYS + META:(q + 1) * KEYS], qh,
                                                   kT[rows, tt * P:tt * P + CHUNK + P], start=True, stop=True)
                            mm.then_inc(s_ready, 1)
                        if 2 <= n <= UNITS + 1:
                            tt, half, buf = (n - 2) // 2, n % 2, n % 2
                            pe.wait_ge(pTa_taken, b * UNITS + n - 1)
                            pe.wait_ge(pTb_taken, b * UNITS + n - 1)
                            if half == 0 and tt:
                                pe.wait_ge(o_taken, b * TILES + tt)
                            for q in range(4):
                                hh = 4 * half + q
                                g = hh % 2
                                head = hh // 2 + 4 * g
                                out = quad[2][:, head * HEAD:(head + 1) * HEAD]
                                cols = slice(g * HEAD, (g + 1) * HEAD)
                                pe.matmul(out, pTb[0:PREV, buf, q * P:(q + 1) * P], v_before[0:PREV, tt, cols],
                                          start=True, stop=False)
                                mm = pe.matmul(out, pTa[:, buf, q * P:(q + 1) * P], v_own[:, tt, cols],
                                               start=False, stop=True)
                            if half == 1:
                                mm.then_inc(o_ready, 1)
                        pe.wait_ge(lo_ready, b * N + RAW + s + 1)
                        if kind == "out" and i == 0:
                            pe.wait_ge(oTlo_ready, b * TILES + TILES)
                            pe.wait_ge(zlo_ready, b * KC + KC)
                        if kind == "wo":
                            half, kk = i // 4, i % 4
                            if half == 0:
                                pe.wait_ge(mlo_ready, b * KD + 2 * kk + 2)
                            for tt in range(TILES):
                                if half == 1 and kk == 0:
                                    pe.wait_ge(wo_taken, b * 2 * TILES + tt + 2)
                                toks = slice(tt * P, (tt + 1) * P)
                                for k in range(2):
                                    w = slice(k * TOK, (k + 1) * TOK)
                                    mm = product(quad[tt][:, :], mT_hi[:, 2 * kk + k, toks], mT_lo[:, 2 * kk + k, toks],
                                                 w_hi[:, s % 2, w], w_lo[:, s % 2, w],
                                                 kk == 0 and k == 0, kk == 3 and k == 1)
                                if tt == TILES - 1:
                                    mm.then_inc(strip_done, 1)
                                elif kk == 3:
                                    mm.then_inc(wo_ready, 1)
                        else:
                            if kind == "out":
                                parts = [(oT_hi, oT_lo, 0, KA), (zT_hi, zT_lo, KA, KC)]
                            else:
                                parts = [(hT_hi, hT_lo, 0, KD)]
                            for part, (x_hi, x_lo, k0, ks) in enumerate(parts):
                                no = out_no[(s, part)]
                                pe.wait_ge(pj_taken[no % 2], b * (NOUT // 2) + no // 2 + 1)
                                for k in range(ks):
                                    w = slice((k0 + k) * P, (k0 + k + 1) * P)
                                    mm = product(pj[no % 2][:, :], w_hi[:, s % 2, w], w_lo[:, s % 2, w],
                                                 x_hi[:, k, :], x_lo[:, k, :], k == 0, k == ks - 1)
                                mm.then_inc(strip_done if part == len(parts) - 1 else branch_ready, 1)
                        if 1 <= n <= UNITS:
                            buf = (n - 1) % 2
                            pe.wait_ge(p_ready, b * UNITS + n)
                            if n == 1:
                                pe.wait_ge(v_taken, b * 2 + 2)
                            else:
                                pe.wait_ge(pTa_taken, b * UNITS + n - 1)
                                pe.wait_ge(pTb_taken, b * UNITS + n - 1)
                            for q in range(4):
                                pe.transpose(tp[0][:, q * P:(q + 1) * P], prob[:, buf, q, PREV:KEYS], ident[:, :])
                                mm = pe.transpose(tp[1][0:PREV, q * P:(q + 1) * P], prob[:, buf, q, 0:PREV],
                                                  ident[:, :])
                            mm.then_inc(pT_ready, 1)
                        if s in HX_AT:
                            q = HX_AT[s]
                            pe.wait_ge(ln_done, b * LNS + TILES + q // 2 + 1)
                            if q >= 2:
                                pe.wait_ge(hx_lo, b * 2 * TILES + q)
                            for k in range(4):
                                c = (4 * (q % 2) + k) * P
                                mm = pe.transpose(tp[q % 2][:, k * P:(k + 1) * P], xs[:, q // 2, c:c + P], ident[:, :])
                            mm.then_inc(hx_ready, 1)
def route(nc, t, h1, keep):
    S, D = h1.shape[0] - TOK, h1.shape[1]
    KD = D // P
    NT = S // P
    G, E = t["w_rg"].shape[1], t["w_re"].shape[1]
    EG = E // G
    L = G + E
    slot1, slot2, weight1, weight2, slot_token, bounds, slot_tiles = keep
    MT = slot_tiles
    RING = 4
    assert NT % RING == 0

    with ExitStack() as ctx:
        def sb(name, shape, dt=FP32):
            return ctx.enter_context(nc.sbuf_tensor(name, shape, dt))

        def sem(name):
            return ctx.enter_context(nc.semaphore(name))

        rows = sb("r_rows", [P, RING, D])
        rowsT = sb("r_rowsT", [P, 2, KD, P])
        w_r = sb("r_weights", [P, KD, L])
        b_r = sb("r_bias", [P, L])
        ident = sb("r_ident", [P, P])
        before = sb("r_before", [P, P])
        ones = sb("r_ones", [P, P])
        logits = sb("r_logits", [P, NT, L])
        desc = sb("r_desc", [P, E])
        count_up = sb("r_count_up", [P, P])
        token = sb("r_token", [P, NT])
        gmax, gsum, gtop = sb("r_gmax", [P, NT]), sb("r_gsum", [P, NT]), sb("r_gtop", [P, NT])
        gdiff, gexp = sb("r_gdiff", [P, NT, G]), sb("r_gexp", [P, NT, G])
        group, penalty = sb("r_group", [P, NT, G]), sb("r_penalty", [P, NT, G])
        inside, tie = sb("r_inside", [P, NT, E]), sb("r_tie", [P, NT, E])
        hot1, hot2, both = sb("r_hot1", [P, NT, E]), sb("r_hot2", [P, NT, E]), sb("r_both", [P, NT, E])
        best1, best2, tied = sb("r_best1", [P, NT]), sb("r_best2", [P, NT]), sb("r_tied", [P, NT])
        gap, gap_exp = sb("r_gap", [P, NT]), sb("r_gap_exp", [P, NT])
        earlier = sb("r_earlier", [P, NT, E])
        total = sb("r_total", [P, E])
        tiles_i, tiles_f = sb("r_tiles_i", [P, E], I32), sb("r_tiles_f", [P, E])
        upto, first = sb("r_upto", [P, E]), sb("r_first", [P, E])
        slot_f, slot_i = sb("r_slot_f", [P, 2, NT]), sb("r_slot_i", [P, 2, NT], I32)
        in_tile_i, tile_of_i = sb("r_in_tile_i", [P, 2 * NT], I32), sb("r_tile_of_i", [P, 2 * NT], I32)
        in_tile, tile_of = sb("r_in_tile", [P, 2 * NT]), sb("r_tile_of", [P, 2 * NT])
        OH = 4
        hot_lo, hot_hi = sb("r_hot_lo", [P, OH, P]), sb("r_hot_hi", [P, OH, MT])
        tp = [ctx.enter_context(nc.psum_tensor(f"r_tp{i}", [P, TOK], FP32)) for i in range(2)]
        lg = [ctx.enter_context(nc.psum_tensor(f"r_lg{i}", [P, L], FP32)) for i in range(2)]
        ranks = [ctx.enter_context(nc.psum_tensor(f"r_rank{i}", [P, TOK], FP32)) for i in range(2)]
        totals = [ctx.enter_context(nc.psum_tensor(f"r_totals{i}", [P, TOK], FP32)) for i in range(2)]
        listed = lg[0]

        rows_in = [sem(f"r_rows_in{i}") for i in range(RING)]
        weights_in = sem("r_weights_in")
        tpT_ready, tpT_act, tpT_dve = sem("r_tp_ready"), sem("r_tp_act"), sem("r_tp_dve")
        lg_ready, lg_taken = sem("r_lg_ready"), sem("r_lg_taken")
        tables = sem("r_tables")
        po_step, step = sem("r_po_step"), sem("r_step")
        gdiff_ready, gexp_ready, gap_ready, gap_exp_ready = (
            sem("r_gdiff_ready"), sem("r_gexp_ready"), sem("r_gap_ready"), sem("r_gap_exp_ready"))
        both_ready, counted = sem("r_both_ready"), sem("r_counted")
        places_ready, lo_made, hi_made, listed_up, hots_used = (
            sem("r_places_ready"), sem("r_lo_made"), sem("r_hi_made"), sem("r_listed_up"), sem("r_hots_used"))

        with nc.Block() as block:
            @block.sync
            def _(sp):
                with nc.allow_non_contiguous_dma(reason="the router's 36 columns"):
                    sp.dma_start(w_r[:, :, 0:G], t["w_rg"].rearrange("(k p) n -> p k n", p=P)).then_inc(weights_in, 16)
                    sp.dma_start(w_r[:, :, G:L], t["w_re"].rearrange("(k p) n -> p k n", p=P)).then_inc(weights_in, 16)
                sp.dma_start(b_r[:, 0:G], t["b_rg"].unsqueeze(0).to_broadcast([P, G])).then_inc(weights_in, 16)
                sp.dma_start(b_r[:, G:L], t["b_re"].unsqueeze(0).to_broadcast([P, E])).then_inc(weights_in, 16)
                with sp.Fori(0, NT // RING) as i:
                    for u in range(RING):
                        hold(sp, tpT_ready, i * 2 * RING + 2 * u + 2)
                        sp.dma_start(rows[:, u, :], h1[bass.ds(i * RING * P + TOK + u * P, P), :]).then_inc(rows_in[u], 16)

            @block.gpsimd
            def _(po):
                steps = [0]

                def link(ins):
                    steps[0] += 1
                    ins.then_inc(po_step, 1)
                    po.wait_ge(po_step, steps[0])

                link(po.memset(ident[:, :], 0.0))
                link(po.memset(before[:, :], 1.0))
                po.affine_select(out=ident[:, :], in_=ident[:, :], compare_op=ALU.not_equal, fill=1.0, base=0,
                                 pattern=[[-1, P]], channel_multiplier=1).then_inc(tables, 1)
                po.affine_select(out=before[:, :], in_=before[:, :], compare_op=ALU.is_gt, fill=0.0, base=0,
                                 pattern=[[1, P]], channel_multiplier=-1).then_inc(tables, 1)
                po.iota(desc[:, :], pattern=[[-1, E]], base=E, channel_multiplier=0,
                        allow_small_or_imprecise_dtypes=True).then_inc(tables, 1)
                po.iota(count_up[:, :], pattern=[[1, P]], base=0, channel_multiplier=0,
                        allow_small_or_imprecise_dtypes=True).then_inc(tables, 1)
                po.iota(token[:, :], pattern=[[P, NT]], base=TOK, channel_multiplier=1,
                        allow_small_or_imprecise_dtypes=True).then_inc(tables, 1)
                po.wait_ge(tables, 5)
                po.wait_ge(places_ready, 2)
                for j in range(2 * NT):
                    if j >= OH:
                        po.wait_ge(hots_used, j - OH + 1)
                    po.tensor_scalar(hot_hi[:, j % OH, :], count_up[:, 0:MT], tile_of[:, j:j + 1],
                                     token[:, j % NT:j % NT + 1], ALU.is_equal, ALU.mult).then_inc(hi_made, 1)

            @block.scalar
            def _(a):
                with a.Fori(0, NT // RING) as i:
                    for u in range(RING):
                        a.wait_ge(tpT_ready, i * 2 * RING + 2 * RING + 2 * u + 1)
                        a.activation(rowsT[:, u % 2, 0:4, :], tp[0][:, :].rearrange("p (k c) -> p k c", k=4), ACT.Copy)\
                         .then_inc(tpT_act, 1)
                a.wait_ge(gdiff_ready, 1)
                a.activation(gexp[:, :, :], gdiff[:, :, :], ACT.Exp).then_inc(gexp_ready, 1)
                a.wait_ge(gap_ready, 1)
                a.activation(gap_exp[:, :], gap[:, :], ACT.Exp).then_inc(gap_exp_ready, 1)

            @block.vector
            def _(v):
                steps = [0]

                def link(ins):
                    steps[0] += 1
                    ins.then_inc(step, 1)
                    v.wait_ge(step, steps[0])

                v.sem_inc(tpT_ready, 2 * RING)
                v.sem_inc(tpT_act, 1)
                v.sem_inc(tpT_dve, 1)
                v.sem_inc(lg_taken, 2)
                v.memset(ones[:, :], 1.0)
                v.wait_ge(weights_in, 64)
                with v.Fori(0, NT // RING) as i:
                    for u in range(RING):
                        v.wait_ge(tpT_ready, i * 2 * RING + 2 * RING + 2 * u + 2)
                        v.tensor_copy(rowsT[:, u % 2, 4:8, :], tp[1][:, :].rearrange("p (k c) -> p k c", k=4))\
                         .then_inc(tpT_dve, 1)
                        v.wait_ge(lg_ready, i * RING + u + 1)
                        v.tensor_tensor(logits[:, bass.ds(i * RING + u, 1), :], lg[u % 2][:, :].unsqueeze(1),
                                        b_r[:, :].unsqueeze(1), ALU.add).then_inc(lg_taken, 1)
                v.wait_ge(lg_taken, NT + 2)
                v.wait_ge(tables, 5)

                def over(ap, n):
                    return ap.unsqueeze(2).to_broadcast([P, NT, n])

                def first_best(values, best, n, hot):
                    link(v.tensor_tensor(tie[:, :, 0:n], values, over(best[:, :], n), ALU.is_equal))
                    link(v.tensor_tensor(tie[:, :, 0:n], tie[:, :, 0:n],
                                         desc[:, E - n:E].unsqueeze(1).to_broadcast([P, NT, n]), ALU.mult))
                    link(v.tensor_reduce(tied[:, :], tie[:, :, 0:n], AX, ALU.max))
                    link(v.tensor_tensor(hot[:, :, :], tie[:, :, 0:n], over(tied[:, :], n), ALU.is_equal))

                g_logits, e_logits = logits[:, :, 0:G], logits[:, :, G:L]
                link(v.tensor_reduce(gmax[:, :], g_logits, AX, ALU.max))
                v.tensor_tensor(gdiff[:, :, :], g_logits, over(gmax[:, :], G), ALU.subtract).then_inc(gdiff_ready, 1)
                first_best(g_logits, gmax, G, group)
                v.wait_ge(gexp_ready, 1)
                link(v.tensor_reduce(gsum[:, :], gexp[:, :, :], AX, ALU.add))
                link(v.reciprocal(gtop[:, :], gsum[:, :]))
                link(v.tensor_scalar(penalty[:, :, :], group[:, :, :], -NEG_INF, NEG_INF, ALU.mult, ALU.add))
                by_group = lambda ap: ap.rearrange("p t (g e) -> p t g e", g=G)
                spread = lambda ap: ap.unsqueeze(3).to_broadcast([P, NT, G, EG])
                link(v.tensor_tensor(by_group(inside[:, :, :]), by_group(e_logits), spread(group[:, :, :]), ALU.mult))
                link(v.tensor_tensor(by_group(inside[:, :, :]), by_group(inside[:, :, :]), spread(penalty[:, :, :]),
                                     ALU.add))
                link(v.tensor_reduce(best1[:, :], inside[:, :, :], AX, ALU.max))
                first_best(inside[:, :, :], best1, E, hot1)
                link(v.scalar_tensor_tensor(out=inside[:, :, :], in0=hot1[:, :, :], scalar=3 * NEG_INF,
                                            in1=inside[:, :, :], op0=ALU.mult, op1=ALU.add))
                link(v.tensor_reduce(best2[:, :], inside[:, :, :], AX, ALU.max))
                v.tensor_tensor(gap[:, :], best2[:, :], best1[:, :], ALU.subtract).then_inc(gap_ready, 1)
                first_best(inside[:, :, :], best2, E, hot2)
                v.tensor_tensor(both[:, :, :], hot1[:, :, :], hot2[:, :, :], ALU.add).then_inc(both_ready, 1)
                v.wait_ge(gap_exp_ready, 1)
                link(v.tensor_scalar(weight1[:, :], gap_exp[:, :], 1.0, None, ALU.add))
                link(v.reciprocal(weight1[:, :], weight1[:, :]))
                link(v.tensor_tensor(weight1[:, :], weight1[:, :], gtop[:, :], ALU.mult))
                link(v.tensor_tensor(weight2[:, :], weight1[:, :], gap_exp[:, :], ALU.mult))
                v.wait_ge(counted, 1)
                half = NT // 2
                tot = lambda q: totals[q // half][:, (q % half) * E:(q % half + 1) * E]
                link(v.memset(earlier[:, 0, :], 0.0))
                for q in range(1, NT):
                    link(v.tensor_tensor(earlier[:, q, :], earlier[:, q - 1, :], tot(q - 1), ALU.add))
                link(v.tensor_tensor(total[:, :], earlier[:, NT - 1, :], tot(NT - 1), ALU.add))
                link(v.tensor_scalar(tiles_i[:, :], total[:, :], float(P - 1), None, ALU.add))
                link(v.tensor_scalar(tiles_i[:, :], tiles_i[:, :], P.bit_length() - 1, None, ALU.arith_shift_right))
                link(v.tensor_copy(tiles_f[:, :], tiles_i[:, :]))
                link(v.tensor_scalar(tiles_f[:, :], tiles_f[:, :], 1.0, None, ALU.max))
                link(v.tensor_tensor_scan(upto[:, :], ones[:, 0:E], tiles_f[:, :], 0.0, ALU.mult, ALU.add))
                link(v.tensor_tensor(first[:, :], upto[:, :], tiles_f[:, :], ALU.subtract))
                v.tensor_copy(bounds[:, 0, :], first[:, :])
                v.tensor_copy(bounds[:, 1, :], upto[:, :])
                v.tensor_scalar(bounds[:, 2, 0:E - 1], upto[:, 0:E - 1], -1.0, None, ALU.add)
                v.memset(bounds[:, 2, E - 1:E], MT)
                v.tensor_scalar(bounds[:, 3, :], upto[:, E - 1:E].to_broadcast([P, E]), -16.0, 16.0 * MT,
                                ALU.mult, ALU.add)
                link(v.tensor_scalar(first[:, :], first[:, :], float(P), None, ALU.mult))
                for q in range(2):
                    part = slice(q * half, (q + 1) * half)
                    link(v.tensor_tensor(earlier[:, part, :], earlier[:, part, :],
                                         ranks[q][:, :].rearrange("p (t e) -> p t e", e=E), ALU.add))
                link(v.tensor_tensor(earlier[:, :, :], earlier[:, :, :],
                                     first[:, :].unsqueeze(1).to_broadcast([P, NT, E]), ALU.add))
                for q, hot in enumerate((hot1, hot2)):
                    link(v.tensor_tensor(hot[:, :, :], hot[:, :, :], earlier[:, :, :], ALU.mult))
                    link(v.tensor_reduce(slot_f[:, q, :], hot[:, :, :], AX, ALU.add))
                v.tensor_copy(slot1[:, :], slot_f[:, 0, :])
                v.tensor_copy(slot2[:, :], slot_f[:, 1, :])
                link(v.tensor_copy(slot_i[:, :, :], slot_f[:, :, :]))
                flat = slot_i[:, :, :].rearrange("p k t -> p (k t)")
                link(v.tensor_scalar(in_tile_i[:, :], flat, P - 1, None, ALU.bitwise_and))
                link(v.tensor_scalar(tile_of_i[:, :], flat, P.bit_length() - 1, None, ALU.arith_shift_right))
                v.tensor_copy(in_tile[:, :], in_tile_i[:, :]).then_inc(places_ready, 1)
                v.tensor_copy(tile_of[:, :], tile_of_i[:, :]).then_inc(places_ready, 1)
                v.wait_ge(places_ready, 2)
                for j in range(2 * NT):
                    if j >= OH:
                        v.wait_ge(hots_used, j - OH + 1)
                    v.tensor_scalar(hot_lo[:, j % OH, :], count_up[:, :], in_tile[:, j:j + 1], None, ALU.is_equal)\
                     .then_inc(lo_made, 1)
                v.wait_ge(listed_up, 1)
                v.tensor_copy(slot_token[:, :], ranks[0][:, 0:MT])

            @block.tensor
            def _(pe):
                pe.wait_ge(tables, 1)
                pe.wait_ge(weights_in, 64)
                with pe.Fori(0, NT // RING) as i:
                    for u in range(RING):
                        pe.wait_ge(rows_in[u], i * 16 + 16)
                        for half, taken in ((0, tpT_act), (1, tpT_dve)):
                            pe.wait_ge(taken, i * RING + u + 1)
                            for k in range(4):
                                c = (4 * half + k) * P
                                mm = pe.transpose(tp[half][:, k * P:(k + 1) * P], rows[:, u, c:c + P], ident[:, :])
                            mm.then_inc(tpT_ready, 1)
                        pe.wait_ge(tpT_act, i * RING + u + 2)
                        pe.wait_ge(tpT_dve, i * RING + u + 2)
                        pe.wait_ge(lg_taken, i * RING + u + 1)
                        for k in range(KD):
                            mm = pe.matmul(lg[u % 2][:, :], rowsT[:, u % 2, k, :], w_r[:, k, :],
                                           start=(k == 0), stop=(k == KD - 1))
                        mm.then_inc(lg_ready, 1)
                pe.wait_ge(tables, 5)
                pe.wait_ge(both_ready, 1)
                flat = both[:, :, :].rearrange("p t e -> p (t e)")
                for q in range(2):
                    pe.matmul(ranks[q][:, :], before[:, :], flat[:, q * TOK:(q + 1) * TOK], start=True, stop=True)
                    mm = pe.matmul(totals[q][:, :], ones[:, :], flat[:, q * TOK:(q + 1) * TOK], start=True, stop=True)
                mm.then_inc(counted, 1)
                for j in range(2 * NT):
                    pe.wait_ge(lo_made, j + 1)
                    pe.wait_ge(hi_made, j + 1)
                    mm = pe.matmul(ranks[0][:, 0:MT], hot_lo[:, j % OH, :], hot_hi[:, j % OH, :],
                                   start=(j == 0), stop=(j == 2 * NT - 1))
                    if j < 2 * NT - 1:
                        mm.then_inc(hots_used, 1)
                mm.then_inc(listed_up, 1)


def experts(nc, t, h1, ys, keep):
    D = h1.shape[1]
    E, _, F = t["w_gate"].shape
    KD, KF = D // P, F // P
    slot1, slot2, weight1, weight2, slot_token, bounds, MT = keep
    GC = KD * F // D
    CH = 3 * GC
    KC = KD // GC

    def chunk(e, c):
        if c < 2 * GC:
            w, j = (t["w_gate"], c) if c < GC else (t["w_up"], c - GC)
            return w[bass.ds(e, 1), j * KC * P:(j + 1) * KC * P, :].rearrange("o (k p) n -> p (o k) n", p=P)
        j = c - 2 * GC
        return t["w_down"][bass.ds(e, 1), j * P:(j + 1) * P, :].rearrange("o p n -> p (o n)")

    with ExitStack() as ctx:
        def sb(name, shape, dt=FP32):
            return ctx.enter_context(nc.sbuf_tensor(name, shape, dt))

        def sem(name):
            return ctx.enter_context(nc.semaphore(name))

        raw = sb("e_raw", [P, CH, D])
        w_hi, w_lo = sb("e_w_hi", [P, CH, D], F32R), sb("e_w_lo", [P, CH, D], F32R)
        rows = sb("e_rows", [P, D])
        xT_hi, xT_lo = sb("e_xT_hi", [P, KD, P], F32R), sb("e_xT_lo", [P, KD, P], F32R)
        act = sb("e_act", [P, F])
        prod = sb("e_prod", [P, F])
        aT_hi, aT_lo = sb("e_aT_hi", [P, KF, P], F32R), sb("e_aT_lo", [P, KF, P], F32R)
        y = sb("e_y", [P, D])
        index = sb("e_index", [P, 1], I32)
        filler = sb("e_filler", [P, D])
        ident = sb("e_ident", [P, P])
        bank = [ctx.enter_context(nc.psum_tensor(f"e_bank{i}", [P, TOK], FP32)) for i in range(8)]
        gate_p, up_p, aT_p, tp, yp = bank[0], bank[1], bank[2:4], bank[4:6], bank[6:8]

        raw_in = [sem(f"e_raw_in{c}") for c in range(CH)]
        hi_ready, lo_ready = sem("e_hi_ready"), sem("e_lo_ready")
        gate_ready = sem("e_gate_ready")
        up_ready = sem("e_up_ready")
        act_ready = sem("e_act_ready")
        prod_ready = sem("e_prod_ready")
        aT_up, aT_himade, a_ready = sem("e_aT_up"), sem("e_aT_himade"), sem("e_a_ready")
        rows_in, index_set = sem("e_rows_in"), sem("e_index_set")
        t_ready = sem("e_t_ready")
        t_hi, t_lo = sem("e_t_hi"), sem("e_t_lo")
        y_ready = sem("e_y_ready")
        y_act, y_dve = sem("e_y_act"), sem("e_y_dve")
        y_out = sem("e_y_out")
        filled = sem("e_filled")
        ident_ready = sem("e_ident_ready")

        def tiles_of(eng, e):
            return [eng.value_load(bounds[0:1, q, bass.ds(e, 1)], min_val=0, max_val=top)
                    for q, top in ((0, MT - 1), (1, MT - 1), (2, MT))]

        with nc.Block() as block:
            @block.sync
            def _(sp):
                def load(e, c):
                    dst = raw[:, c, :]
                    if c < 2 * GC:
                        dst = dst.rearrange("p (k n) -> p k n", k=KC)
                    sp.dma_start(dst, chunk(e, c)).then_inc(raw_in[c], 16)

                for c in range(CH):
                    load(0, c)

                def stores(e):
                    lo, hi, _ = tiles_of(sp, e)
                    with sp.Fori(lo, hi) as g:
                        hold(sp, y_act, g + 2)
                        hold(sp, y_dve, g + 2)
                        sp.dma_start(ys[bass.ds(g * P, P), :], y[:, :]).then_inc(y_out, 16)

                with sp.Fori(0, E - 1) as e:
                    for c in range(CH):
                        hold(sp, lo_ready, e * CH + c + 1)
                        load(e + 1, c)
                    stores(e)
                stores(E - 1)
                total = sp.value_load(bounds[0:1, 1, E - 1:E], min_val=1, max_val=MT - 1)
                hold(sp, y_out, total * 16 + 16)

            @block.gpsimd
            def _(po):
                po.memset(filler[:, :], 0.0)
                po.memset(ident[:, :], 0.0).then_inc(ident_ready, 1)
                po.wait_ge(ident_ready, 1)
                po.affine_select(out=ident[:, :], in_=ident[:, :], compare_op=ALU.not_equal, fill=1.0, base=0,
                                 pattern=[[-1, P]], channel_multiplier=1).then_inc(ident_ready, 1)
                total = po.value_load(bounds[0:1, 1, E - 1:E], min_val=1, max_val=MT - 1)
                unfilled = po.value_load(bounds[0:1, 3, 0:1], min_val=16, max_val=16 * MT)

                def gather(g):
                    hold(po, t_ready, g * 2 + 2)
                    po.tensor_copy(index[:, :], slot_token[:, bass.ds(g, 1)]).then_inc(index_set, 1)
                    hold(po, index_set, g + 1)
                    po.indirect_dma_start(out=rows[:, :], out_offset=None, in_=h1[:, :],
                                          in_offset=bass.IndirectOffsetOnAxis(ap=index[:, 0:1], axis=0))\
                      .then_inc(rows_in, 16)
                    hold(po, rows_in, g * 16 + 16)

                with po.Fori(0, total + 1) as g:
                    gather(g)
                with po.Fori(total, MT) as g:
                    po.dma_start(ys[bass.ds(g * P, P), :], filler[:, :]).then_inc(filled, 16)
                hold(po, filled, unfilled)

            @block.scalar
            def _(a):
                def evacuate(count):
                    for half in range(2):
                        a.wait_ge(t_ready, count + half + 1)
                        a.activation(xT_hi[:, 4 * half:4 * half + 4, :],
                                     tp[half][:, :].rearrange("p (k c) -> p k c", k=4), ACT.Copy).then_inc(t_hi, 1)

                def split_hi(e, c):
                    a.wait_ge(raw_in[c], e * 16 + 16)
                    a.activation(w_hi[:, c, :], raw[:, c, :], ACT.Copy).then_inc(hi_ready, 1)

                for c in range(GC):
                    a.wait_ge(raw_in[c], 16)
                    a.activation(w_hi[:, c, :], raw[:, c, :], ACT.Copy).then_inc(hi_ready, 1)
                evacuate(2)
                with a.Fori(0, E) as e:
                    lo, hi, swap = tiles_of(a, e)
                    a.wait_ge(up_ready, lo + 1)
                    for c in range(GC, 2 * GC):
                        split_hi(e, c)
                    a.wait_ge(y_ready, lo * 2 + 2)
                    for c in range(2 * GC, CH):
                        split_hi(e, c)
                    with a.Fori(lo, hi) as g:
                        a.wait_ge(gate_ready, g + 1)
                        a.activation(act[:, :], gate_p[:, :], ACT.Silu).then_inc(act_ready, 1)
                        with a.If(g == swap):
                            for c in range(GC):
                                split_hi(e + 1, c)
                        for j in range(KF):
                            a.wait_ge(aT_up, g * KF + j + 1)
                            a.activation(aT_hi[:, j, :], aT_p[j % 2][:, 0:P], ACT.Copy).then_inc(aT_himade, 1)
                        evacuate(g * 2 + 4)
                        a.wait_ge(y_ready, g * 2 + 3)
                        a.wait_ge(y_out, g * 16 + 16)
                        a.activation(y[:, 0:TOK], yp[0][:, :], ACT.Copy).then_inc(y_act, 1)

            @block.vector
            def _(v):
                def evacuate(hi_count):
                    for half in range(2):
                        v.wait_ge(t_hi, hi_count + half + 1)
                        part = slice(4 * half, 4 * half + 4)
                        v.tensor_tensor(xT_lo[:, part, :], tp[half][:, :].rearrange("p (k c) -> p k c", k=4),
                                        xT_hi[:, part, :].bitcast(FP32), ALU.subtract).then_inc(t_lo, 1)

                def split_lo(e, c):
                    v.wait_ge(hi_ready, e * CH + c + 1)
                    v.tensor_tensor(w_lo[:, c, :], raw[:, c, :], w_hi[:, c, :].bitcast(FP32), ALU.subtract)\
                     .then_inc(lo_ready, 1)

                v.sem_inc(up_ready, 1)
                v.sem_inc(act_ready, 1)
                v.sem_inc(t_ready, 2)
                v.sem_inc(y_ready, 2)
                v.sem_inc(y_act, 1)
                v.sem_inc(y_dve, 1)
                v.sem_inc(y_out, 16)
                for c in range(GC):
                    split_lo(0, c)
                evacuate(0)
                with v.Fori(0, E) as e:
                    lo, hi, swap = tiles_of(v, e)
                    for c in range(GC, CH):
                        split_lo(e, c)
                    with v.Fori(lo, hi) as g:
                        with v.If(g == swap):
                            for c in range(GC):
                                split_lo(e + 1, c)
                        v.wait_ge(act_ready, g + 2)
                        v.wait_ge(up_ready, g + 2)
                        for j in range(KF):
                            part = slice(j * P, (j + 1) * P)
                            v.tensor_tensor(prod[:, part], up_p[:, part], act[:, part], ALU.mult).then_inc(prod_ready, 1)
                        for j in range(KF):
                            v.wait_ge(aT_himade, g * KF + j + 1)
                            v.tensor_tensor(aT_lo[:, j, :], aT_p[j % 2][:, 0:P], aT_hi[:, j, :].bitcast(FP32),
                                            ALU.subtract).then_inc(a_ready, 1)
                        evacuate(g * 2 + 2)
                        v.wait_ge(y_ready, g * 2 + 4)
                        v.wait_ge(y_out, g * 16 + 16)
                        v.tensor_copy(y[:, TOK:2 * TOK], yp[1][:, :]).then_inc(y_dve, 1)

            @block.tensor
            def _(pe):
                def product(out, hi, lo, x_hi, x_lo, first, last):
                    pe.matmul(out, hi, x_hi, start=first, stop=False)
                    pe.matmul(out, hi, x_lo, start=False, stop=False)
                    return pe.matmul(out, lo, x_hi, start=False, stop=last)

                def transposes(rows_count):
                    pe.wait_ge(rows_in, rows_count)
                    for half in range(2):
                        for k in range(4):
                            c = (4 * half + k) * P
                            mm = pe.transpose(tp[half][:, k * P:(k + 1) * P], rows[:, c:c + P], ident[:, :])
                        mm.then_inc(t_ready, 1)

                pe.wait_ge(ident_ready, 2)
                transposes(16)
                with pe.Fori(0, E) as e:
                    lo, hi, _ = tiles_of(pe, e)
                    with pe.Fori(lo, hi) as g:
                        pe.wait_ge(t_lo, g * 2 + 2)
                        pe.wait_ge(act_ready, g + 1)
                        for out, c0, ready in ((gate_p, 0, gate_ready), (up_p, GC, up_ready)):
                            for k in range(KD):
                                c = c0 + k // KC
                                w = slice((k % KC) * F, (k % KC + 1) * F)
                                if k % KC == 0:
                                    pe.wait_ge(lo_ready, e * CH + c + 1)
                                mm = product(out[:, :], xT_hi[:, k, :], xT_lo[:, k, :], w_hi[:, c, w], w_lo[:, c, w],
                                             k == 0, k == KD - 1)
                            mm.then_inc(ready, 1)
                        transposes(g * 16 + 32)
                        pe.wait_ge(y_act, g + 1)
                        pe.wait_ge(y_dve, g + 1)
                        for q in range(KF + 1):
                            if q < KF:
                                pe.wait_ge(prod_ready, g * KF + q + 1)
                                part = slice(q * P, (q + 1) * P)
                                pe.transpose(aT_p[q % 2][:, 0:P], prod[:, part], ident[:, :]).then_inc(aT_up, 1)
                            if q:
                                j = q - 1
                                pe.wait_ge(lo_ready, e * CH + 2 * GC + j + 1)
                                pe.wait_ge(a_ready, g * KF + j + 1)
                                for half in range(2):
                                    w = slice(half * TOK, (half + 1) * TOK)
                                    mm = product(yp[half][:, :], aT_hi[:, j, :], aT_lo[:, j, :],
                                                 w_hi[:, 2 * GC + j, w], w_lo[:, 2 * GC + j, w], j == 0, j == KF - 1)
                                    if j == KF - 1:
                                        mm.then_inc(y_ready, 1)


def combine(nc, t, h1, ys, out, keep):
    S, D = out.shape
    NT = S // P
    slot1, slot2, weight1, weight2, slot_token, bounds, MT = keep
    RING = 4

    with ExitStack() as ctx:
        def sb(name, shape, dt=FP32):
            return ctx.enter_context(nc.sbuf_tensor(name, shape, dt))

        def sem(name):
            return ctx.enter_context(nc.semaphore(name))

        y1, y2 = sb("c_y1", [P, RING, D]), sb("c_y2", [P, RING, D])
        h = sb("c_h", [P, RING, D])
        gain, shift = sb("c_gain", [P, D]), sb("c_bias", [P, D])
        stats, moments, rstd = sb("c_stats", [P, 2, 6]), sb("c_moments", [P, 2]), sb("c_rstd", [P, 1])
        minus_half = sb("c_minus_half", [P, 1])
        index = sb("c_index", [P, RING, 2], I32)
        consts_in = sem("c_consts_in")
        h_in = [sem(f"c_h_in{i}") for i in range(RING)]
        y_in = [sem(f"c_y_in{i}") for i in range(RING)]
        stored = [sem(f"c_stored{i}") for i in range(RING)]
        index_set, summed = sem("c_index_set"), sem("c_summed")
        scaled_h, sum1 = sem("c_scaled_h"), sem("c_sum1")
        ln_step, ln_moments, ln_rstd, ln_normed, ln_scaled, ln_done = (
            sem("c_ln_step"), sem("c_ln_moments"), sem("c_ln_rstd"), sem("c_ln_normed"), sem("c_ln_scaled"),
            sem("c_ln_done"))
        half_set = sem("c_half_set")

        with nc.Block() as block:
            @block.sync
            def _(sp):
                sp.dma_start(gain[:, :], t["ln2_g"].unsqueeze(0).to_broadcast([P, D])).then_inc(consts_in, 16)
                sp.dma_start(shift[:, :], t["ln2_b"].unsqueeze(0).to_broadcast([P, D])).then_inc(consts_in, 16)
                with sp.Fori(0, NT // RING) as i:
                    for u in range(RING):
                        hold(sp, stored[u], i * 16 + 16)
                        sp.dma_start(h[:, u, :], h1[bass.ds(i * RING * P + TOK + u * P, P), :]).then_inc(h_in[u], 16)

            @block.scalar
            def _(a):
                with a.Fori(0, NT // RING) as i:
                    for u in range(RING):
                        a.wait_ge(h_in[u], i * 16 + 16)
                        a.activation(h[:, u, :], h[:, u, :], ACT.Copy, scale=ALPHA).then_inc(scaled_h, 1)
                        if u:
                            a.wait_ge(ln_done, i * RING + u)
                            a.dma_start(out[bass.ds(i * RING * P + (u - 1) * P, P), :], h[:, u - 1, :])\
                             .then_inc(stored[u - 1], 16)
                    a.wait_ge(ln_done, i * RING + RING)
                    a.dma_start(out[bass.ds(i * RING * P + (RING - 1) * P, P), :], h[:, RING - 1, :])\
                     .then_inc(stored[RING - 1], 16)
                for u in range(RING):
                    a.wait_ge(stored[u], (NT // RING + 1) * 16)

            @block.gpsimd
            def _(po):
                def gather(i, u, n):
                    hold(po, summed, n + 1)
                    for q, slot in enumerate((slot1, slot2)):
                        po.tensor_copy(index[:, u, q:q + 1], slot[:, bass.ds(i * RING + u, 1)]).then_inc(index_set, 1)
                    hold(po, index_set, 2 * n + 2)
                    for q, y in enumerate((y1, y2)):
                        po.indirect_dma_start(out=y[:, u, :], out_offset=None, in_=ys[:, :],
                                              in_offset=bass.IndirectOffsetOnAxis(ap=index[:, u, q:q + 1], axis=0))\
                          .then_inc(y_in[u], 16)

                po.memset(minus_half[:, :], -0.5).then_inc(half_set, 1)
                po.wait_ge(half_set, 1)
                po.wait_ge(consts_in, 32)
                with po.Fori(0, NT // RING) as i:
                    for u in range(RING):
                        gather(i, u, i * RING + u)
                    for u in range(RING):
                        n = i * RING + u
                        hold(po, ln_moments, n + 1)
                        po.tensor_scalar(rstd[:, :], moments[:, 1:2], LN_EPS, None, ALU.add).then_inc(ln_rstd, 1)
                        po.wait_ge(ln_rstd, 2 * n + 1)
                        po.tensor_tensor(rstd[:, :], rstd[:, :], minus_half[:, :], ALU.pow).then_inc(ln_rstd, 1)
                        po.wait_ge(ln_normed, n + 1)
                        po.tensor_tensor(h[:, u, :], h[:, u, :], gain[:, :], ALU.mult).then_inc(ln_scaled, 1)
                        po.wait_ge(ln_scaled, n + 1)
                        po.tensor_tensor(h[:, u, :], h[:, u, :], shift[:, :], ALU.add).then_inc(ln_done, 1)

            @block.vector
            def _(v):
                v.sem_inc(summed, RING)
                for u in range(RING):
                    v.sem_inc(stored[u], 16)
                with v.Fori(0, NT // RING) as i:
                    for u in range(RING):
                        n = i * RING + u
                        v.wait_ge(scaled_h, n + 1)
                        v.wait_ge(y_in[u], i * 32 + 32)
                        tile = bass.ds(n, 1)
                        v.scalar_tensor_tensor(out=h[:, u, :], in0=y1[:, u, :], scalar=weight1[:, tile],
                                               in1=h[:, u, :], op0=ALU.mult, op1=ALU.add).then_inc(sum1, 1)
                        v.wait_ge(sum1, n + 1)
                        v.scalar_tensor_tensor(out=h[:, u, :], in0=y2[:, u, :], scalar=weight2[:, tile],
                                               in1=h[:, u, :], op0=ALU.mult, op1=ALU.add).then_inc(summed, 1)
                        v.wait_ge(summed, n + RING + 1)
                        layernorm_stats(v, P, h[:, u, :], stats, moments, ln_step, n, ln_moments)
                        v.wait_ge(ln_moments, n + 1)
                        v.wait_ge(ln_rstd, 2 * n + 2)
                        v.tensor_scalar(h[:, u, :], h[:, u, :], moments[:, 0:1], rstd[:, 0:1],
                                        ALU.subtract, ALU.mult).then_inc(ln_normed, 1)


def encoder_block(nc, x, meta_tokens, ln0_g, ln0_b, w_in, attn_sinks, conv_w, w_attn_out, w_conv_out, w_o,
                  ln1_g, ln1_b, w_router_group, b_router_group, w_router_expert, b_router_expert,
                  w_exp_gate, w_exp_up, w_exp_down, ln2_g, ln2_b, out):
    x2, out2 = x[0], out[0]
    S, D = x2.shape
    E = w_router_expert.shape[2]
    NT = S // P
    slot_tiles = 2 * NT + E + 1
    slot_tiles += slot_tiles % 2
    t = dict(meta=meta_tokens, ln0_g=ln0_g, ln0_b=ln0_b, ln1_g=ln1_g[0], ln1_b=ln1_b[0], ln2_g=ln2_g[0],
             ln2_b=ln2_b[0], sinks=attn_sinks[0], conv_w=conv_w[0], w_rg=w_router_group[0],
             b_rg=b_router_group[0], w_re=w_router_expert[0], b_re=b_router_expert[0],
             w_gate=w_exp_gate[0], w_up=w_exp_up[0], w_down=w_exp_down[0])
    h1 = nc.dram_tensor("h1_rows", [TOK + S, D], FP32).ap()
    ys = nc.dram_tensor("expert_rows", [slot_tiles * P, D], FP32).ap()
    mixer(nc, t, x2, w_in[0], w_attn_out[0], w_conv_out[0], w_o[0], h1)
    with ExitStack() as ctx:
        def sb(name, shape, dt=FP32):
            return ctx.enter_context(nc.sbuf_tensor(name, shape, dt))
        keep = (sb("slot1", [P, NT], I32), sb("slot2", [P, NT], I32), sb("weight1", [P, NT]),
                sb("weight2", [P, NT]), sb("slot_token", [P, slot_tiles], I32), sb("bounds", [P, 4, E], I32),
                slot_tiles)
        route(nc, t, h1, keep)
        experts(nc, t, h1, ys, keep)
        combine(nc, t, h1, ys, out2, keep)


_INS = ["x", "meta_tokens", "ln0_g", "ln0_b", "w_in", "attn_sinks", "conv_w", "w_attn_out", "w_conv_out", "w_o",
        "ln1_g", "ln1_b", "w_router_group", "b_router_group", "w_router_expert", "b_router_expert",
        "w_exp_gate", "w_exp_up", "w_exp_down", "ln2_g", "ln2_b"]


def kernel(**inputs):
    import numpy as _np
    import concourse.bacc as _bacc
    from concourse import mybir as _mybir
    from concourse.bass_utils import run_bass_kernel_spmd as _run

    nc = _bacc.Bacc("TRN2", target_bir_lowering=False, num_devices=1)
    arrays, args = {}, []
    for name in _INS:
        a = _np.ascontiguousarray(inputs[name])
        arrays[f"in_{name}_dram"] = a
        args.append(nc.dram_tensor(f"in_{name}_dram", a.shape, _mybir.dt.from_np(a.dtype), kind="ExternalInput").ap())
    shape = arrays["in_x_dram"].shape
    args.append(nc.dram_tensor("out_0_dram", shape, _mybir.dt.float32, kind="ExternalOutput").ap())
    encoder_block(nc, *args)
    r = _run(nc, [arrays], core_ids=[0])
    return r.results[0]["out_0_dram"]
```

```python
import concourse.bass as bass
from concourse import mybir
from contextlib import ExitStack
import math

FP32 = mybir.dt.float32
F32R = mybir.dt.float32r
I32 = mybir.dt.int32
ALU = mybir.AluOpType
ACT = mybir.ActivationFunctionType
AX = mybir.AxisListType.X

P = 128
ALPHA = 2.0 ** 0.25
LN_EPS = 1e-5
NEG_INF = -1e30
CHUNK = 64
HEAD = 64
HEADS = 8
PAIRS = HEADS // 2
TAPS = 3

TOK = 512
TILES = TOK // P


def hold(eng, sem, value):
    eng.wait_ge(sem, value)
    eng.nop(nofuse=True)


def layernorm_stats(v, rows, x, stats, moments, ln_step, step0, ln_moments):
    half = x.shape[1] // 2
    v.bn_stats(stats[0:rows, 0, :], x[:, 0:half])
    v.bn_stats(stats[0:rows, 1, :], x[:, half:2 * half]).then_inc(ln_step, 1)
    hold(v, ln_step, step0 + 1)
    v.bn_aggr(moments[0:rows, :], stats[0:rows, :, :]).then_inc(ln_moments, 1)


def rsqrt(po, rows, moments, rstd, minus_half, ln_rstd, count):
    po.tensor_scalar(rstd[0:rows, :], moments[0:rows, 1:2], LN_EPS, None, ALU.add).then_inc(ln_rstd, 1)
    po.wait_ge(ln_rstd, count + 1)
    po.tensor_tensor(rstd[0:rows, :], rstd[0:rows, :], minus_half[0:rows, :], ALU.pow).then_inc(ln_rstd, 1)


def mixer(nc, t, x, w_in, w_attn_out, w_conv_out, w_o, h1, logits):
    D = x.shape[1]
    S = x.shape[0]
    KD = D // P
    BLOCKS = S // TOK
    AW = w_attn_out.shape[0]
    CW = w_conv_out.shape[0]
    KA, KC = AW // P, CW // P
    KVW = 128
    META = t["meta"].shape[0]
    PREV = META + CHUNK
    KEYS = PREV + P
    G, E = t["w_rg"].shape[1], t["w_re"].shape[1]
    L = G + E

    Q0, K0, V0 = 0, AW, AW + KVW
    CB0 = V0 + KVW
    CC0, CH0 = CB0 + CW, CB0 + 2 * CW
    GA0 = CB0 + 3 * CW
    GC0 = GA0 + D

    w_in_k = w_in.rearrange("(k p) n -> p k n", p=P)
    w_ao_k = w_attn_out.rearrange("(k p) n -> p k n", p=P)
    w_co_k = w_conv_out.rearrange("(k p) n -> p k n", p=P)
    w_o_k = w_o.rearrange("(k p) n -> p k n", p=P)

    strips = [("k", 0), ("v", 0)] + [("q", i) for i in range(PAIRS)]
    for i in range(KC):
        strips += [("cc", i), ("ch", i), ("cb", i)]
    for j in range(KD):
        strips += [("ga", j), ("gc", j), ("out", j)]
    for n in range(2):
        strips += [("wo", 4 * n + k) for k in range(4)]
    N = len(strips)
    RAW = 5
    assert N % RAW == 0 and N % 2 == 0
    CONV0 = 2 + PAIRS
    MIX0 = CONV0 + 3 * KC
    WO0 = MIX0 + 3 * KD
    UNITS = 2 * TILES
    base_col = {"k": K0, "v": V0, "cc": CC0, "ch": CH0, "cb": CB0, "ga": GA0, "gc": GC0}

    outputs = []
    for s, (kind, i) in enumerate(strips):
        if kind == "out":
            outputs += [(s, 0), (s, 1)]
        elif kind != "wo":
            outputs += [(s, 0)]
    NOUT = len(outputs)
    assert NOUT % 2 == 0
    out_no = {o: n for n, o in enumerate(outputs)}
    by_act = {"k", "v", "q", "cc", "ga", "gc"}

    def strip_dmas(kind, i, raw):
        full = raw.rearrange("p (k c) -> p k c", k=KD)
        if kind == "q":
            return [(full[:, :, g * HEAD:(g + 1) * HEAD],
                     w_in_k[:, :, Q0 + (i + 4 * g) * HEAD:Q0 + (i + 4 * g + 1) * HEAD]) for g in range(2)]
        if kind == "out":
            return [(full[:, 0:KA, :], w_ao_k[:, :, i * P:(i + 1) * P]),
                    (full[:, KA:KA + KC, :], w_co_k[:, :, i * P:(i + 1) * P])]
        if kind == "wo":
            n, k = i // 4, i % 4
            return [(raw.rearrange("p (k c) -> p k c", k=2),
                     w_o_k[:, 2 * k:2 * k + 2, n * TOK:(n + 1) * TOK])]
        c = base_col[kind] + i * P
        return [(full, w_in_k[:, :, c:c + P])]

    with ExitStack() as ctx:
        def sb(name, shape, dt=FP32):
            return ctx.enter_context(nc.sbuf_tensor(name, shape, dt))

        def sem(name):
            return ctx.enter_context(nc.semaphore(name))

        raw = sb("raw", [P, RAW, D])
        w_hi = sb("w_hi", [P, 2, D], F32R)
        w_lo = sb("w_lo", [P, 2, D], F32R)
        xs = sb("x_rows", [P, TILES, D])
        h = sb("h_rows", [P, TILES, D])
        hT_hi = sb("hT_hi", [P, KD, TOK], F32R)
        hT_lo = sb("hT_lo", [P, KD, TOK], F32R)
        kT = sb("kT", [P, TILES, KEYS])
        vT = sb("vT", [P, CHUNK + TOK])
        vmT = sb("vmT", [P, META])
        bias = sb("bias", [P, HEADS, KEYS])
        meta_step = sb("meta_step", [P, HEADS, META])
        sinks = sb("sinks", [P, HEADS])
        oT_hi = sb("oT_hi", [P, KA, TOK], F32R)
        oT_lo = sb("oT_lo", [P, KA, TOK], F32R)
        zT_hi = sb("zT_hi", [P, KC, TOK], F32R)
        zT_lo = sb("zT_lo", [P, KC, TOK], F32R)
        work = [sb(f"work{i}", [P, TOK + 2]) for i in range(4)]
        u_tail = sb("u_tail", [P, KC, 2])
        cw = sb("conv_taps", [P, KC, TAPS])
        w_r = sb("router_weights", [P, KD, L])
        b_r = sb("router_bias", [P, L])
        ident = sb("ident", [P, P])
        g0, b0 = sb("ln0_gain", [P, D]), sb("ln0_bias", [P, D])
        g1, b1 = sb("ln1_gain", [P, D]), sb("ln1_bias", [P, D])
        stats = sb("stats", [P, 2, 6])
        moments = sb("moments", [P, 2])
        rstd = sb("rstd", [P, 1])
        minus_half = sb("minus_half", [P, 1])
        top = sb("top", [P, 4])
        neg_top = sb("neg_top", [P, 2, 4])
        sink_gap = sb("sink_gap", [P, 2, 4])
        den = sb("den", [P, 2, HEADS])
        sink_e = sb("sink_e", [P, 2, HEADS])
        rden = sb("rden", [P, HEADS])
        shared = -(-nc.sbuf_base // 32) * 32
        arena = sb("arena", [P, 2 * KD * TOK])

        def place(at, name, shape, dt=FP32):
            size = 4 * math.prod(shape[1:])
            assert at[0] + size <= shared + 4 * 2 * KD * TOK
            placed = nc.alloc_sbuf_tensor_at(name, shape, dt, offset=at[0])
            at[0] += size
            return placed

        at = [shared]
        qT = place(at, "qT", [P, PAIRS, TOK])
        prob = place(at, "prob", [P, 2, 4, KEYS])
        pTa = place(at, "pTa", [P, 2, 4 * P])
        pTb = place(at, "pTb", [P, 2, 4 * P])
        o_rows = place(at, "o_rows", [P, AW])
        v_own = place(at, "v_own", [P, TILES, KVW])
        v_before = place(at, "v_before", [P, TILES, KVW])
        vBT = place(at, "vBT", [P, TILES, PREV])
        attention_end = at[0]
        at = [shared]
        mT_hi = place(at, "mixT_hi", [P, KD, TOK], F32R)
        mT_lo = place(at, "mixT_lo", [P, KD, TOK], F32R)
        end = shared + 4 * 2 * KD * TOK
        rowsT = place([end - 4 * D], "router_rowsT", [P, KD, P])
        logitsT = place([end - 4 * (D + TOK)], "router_logitsT", [P, TOK])
        assert attention_end <= end - 4 * HEADS * CHUNK
        bias_prev = place([end - 4 * HEADS * CHUNK], "bias_prev", [P // 2, HEADS, CHUNK])

        banks = [ctx.enter_context(nc.psum_tensor(f"bank{i}", [P, TOK], FP32)) for i in range(8)]
        pj = banks[0:2]
        quad = banks[2:6]
        tp = banks[6:8]

        with ExitStack() as c1, nc.Block() as block:
            def sem1(name):
                return c1.enter_context(nc.semaphore(name))
            meta_in, consts_in, x_in = sem1("meta_in"), sem1("consts_in"), sem1("x_in")
            router_in = sem1("router_in")
            raw_in = [sem1(f"meta_raw_in{i}") for i in range(RAW)]
            raw_used = sem1("meta_raw_used")
            ln_step, ln_moments, ln_rstd, ln_normed, ln_scaled, ln_done = (
                sem1("ln_step"), sem1("ln_moments"), sem1("ln_rstd"), sem1("ln_normed"),
                sem1("ln_scaled"), sem1("ln_done"))
            pool_step, dve_step = sem1("pool_step"), sem1("dve_step")
            ident_ready, dist_ready = sem1("ident_ready"), sem1("dist_ready")
            tp_ready, tp_taken_act, tp_taken_dve = sem1("tp_ready"), sem1("tp_taken_act"), sem1("tp_taken_dve")
            pj_ready, pj_taken = sem1("mpj_ready"), sem1("mpj_taken")

            meta_strips = [("k", 0), ("v", 0)] + [s for i in range(KC) for s in (("cc", i), ("ch", i))]
            hm = h[0:META, 0, :]
            hmT = work[0][:, 0:KD * META].rearrange("p (k m) -> p k m", k=KD)
            lns = [(META, hm)] + [(P, xs[:, i, :]) for i in range(TILES)]

            @block.sync
            def _(sp):
                sp.dma_start(hm, t["meta"]).then_inc(meta_in, 16)
                for dst, src in ((g0, t["ln0_g"]), (b0, t["ln0_b"]), (g1, t["ln1_g"]), (b1, t["ln1_b"])):
                    sp.dma_start(dst[:, :], src.unsqueeze(0).to_broadcast([P, D])).then_inc(consts_in, 16)
                sp.dma_start(rden[:, :], t["sinks"].unsqueeze(0).to_broadcast([P, HEADS])).then_inc(consts_in, 16)
                for k in range(TAPS):
                    sp.dma_start(cw[:, :, k], t["conv_w"][k].rearrange("(i p) -> p i", p=P),
                                 allow_slow_non_contiguous=True).then_inc(consts_in, 16)
                sp.dma_start(xs[:, :, :], x[0:TOK, :].rearrange("(t p) d -> p t d", p=P)).then_inc(x_in, 16)
                with nc.allow_non_contiguous_dma(reason="the router's 36 columns"):
                    for dst, w in ((w_r[:, :, 0:G], t["w_rg"]), (w_r[:, :, G:L], t["w_re"])):
                        sp.dma_start(dst, w.rearrange("(k p) n -> p k n", p=P)).then_inc(router_in, 16)
                for dst, row in ((b_r[:, 0:G], t["b_rg"]), (b_r[:, G:L], t["b_re"])):
                    sp.dma_start(dst, row.unsqueeze(0).to_broadcast([P, row.shape[0]])).then_inc(router_in, 16)
                for n, (kind, i) in enumerate(meta_strips):
                    if n >= RAW:
                        sp.wait_ge(raw_used, n - RAW + 1)
                    for dst, src in strip_dmas(kind, i, raw[:, n % RAW, :]):
                        sp.dma_start(dst, src).then_inc(raw_in[n % RAW], 16)
                sp.wait_ge(router_in, 64)

            @block.gpsimd
            def _(po):
                steps = [0]

                def link(ins):
                    steps[0] += 1
                    ins.then_inc(pool_step, 1)
                    po.wait_ge(pool_step, steps[0])

                po.memset(minus_half[:, :], -0.5)
                link(po.memset(ident[:, :], 0.0))
                po.affine_select(out=ident[:, :], in_=ident[:, :], compare_op=ALU.not_equal, fill=1.0, base=0,
                                 pattern=[[-1, P]], channel_multiplier=1).then_inc(ident_ready, 1)
                dist = work[1]
                link(po.iota(dist[:, 0:META], pattern=[[-1, META]], base=META, channel_multiplier=1,
                             allow_small_or_imprecise_dtypes=True))
                po.iota(dist[:, META:KEYS], pattern=[[-1, CHUNK + P]], base=CHUNK, channel_multiplier=1,
                        allow_small_or_imprecise_dtypes=True).then_inc(dist_ready, 1)
                po.wait_ge(dist_ready, 2)
                for i in range(PAIRS):
                    for g in range(2):
                        slope = 2.0 ** (-8.0 * (i + 4 * g + 1) / HEADS)
                        hh = 2 * i + g
                        link(po.tensor_scalar(bias[:, hh, :], dist[:, 0:KEYS], -slope, None, ALU.mult))
                        link(po.memset(meta_step[:, hh, :], -slope * P))
                link(po.tensor_copy(bias_prev[:, :, :], bias[0:CHUNK, :, META:PREV]))
                link(po.memset(bias[:, :, META:PREV], NEG_INF))
                link(po.memset(bias[0:CHUNK, :, PREV + CHUNK:KEYS], NEG_INF))
                po.wait_ge(consts_in, 16 * (5 + TAPS))
                link(po.tensor_copy(sinks[:, :].rearrange("p (i g) -> p i g", g=2),
                                    rden[:, :].rearrange("p (g i) -> p i g", g=2)))
                for n, (rows, xx) in enumerate(lns):
                    po.wait_ge(ln_moments, n + 1)
                    rsqrt(po, rows, moments, rstd, minus_half, ln_rstd, 2 * n)
                    po.wait_ge(ln_normed, n + 1)
                    po.tensor_tensor(xx, xx, g0[0:rows, :], ALU.mult).then_inc(ln_scaled, 1)
                    po.wait_ge(ln_scaled, n + 1)
                    po.tensor_tensor(xx, xx, b0[0:rows, :], ALU.add).then_inc(ln_done, 1)

            @block.vector
            def _(v):
                v.wait_ge(dist_ready, 1)
                v.scalar_tensor_tensor(out=work[1][:, 0:KEYS], in0=work[1][:, 0:KEYS], scalar=-1.0,
                                       in1=work[1][:, 0:KEYS], op0=ALU.mult, op1=ALU.max).then_inc(dist_ready, 1)
                v.memset(kT[:, :, :], 0.0)
                v.memset(vT[:, :], 0.0)
                for n, (rows, xx) in enumerate(lns):
                    v.wait_ge(meta_in if n == 0 else x_in, 16)
                    layernorm_stats(v, rows, xx, stats, moments, ln_step, n, ln_moments)
                    v.wait_ge(ln_moments, n + 1)
                    v.wait_ge(ln_rstd, 2 * n + 2)
                    v.tensor_scalar(xx, xx, moments[0:rows, 0:1], rstd[0:rows, 0:1], ALU.subtract, ALU.mult)\
                     .then_inc(ln_normed, 1)
                    if n == 0:
                        v.wait_ge(tp_ready, 1)
                        v.tensor_copy(hmT, tp[0][:, 0:KD * META].rearrange("p (k m) -> p k m", k=KD))\
                         .then_inc(tp_taken_dve, 1)
                    else:
                        for half in range(2):
                            q = 2 * (n - 1) + half
                            v.wait_ge(tp_taken_act, q + 1)
                            dst = (slice(None), slice(4 * half, 4 * half + 4), slice((n - 1) * P, n * P))
                            v.tensor_tensor(hT_lo[dst], tp[q % 2][:, :].rearrange("p (k c) -> p k c", k=4),
                                            hT_hi[dst].bitcast(FP32), ALU.subtract).then_inc(tp_taken_dve, 1)
                v.memset(h[:, :, :], 0.0)
                for n, (kind, i) in enumerate(meta_strips):
                    v.wait_ge(pj_ready, n + 1)
                    got = pj[n % 2][:, 0:META]
                    if kind == "k":
                        v.tensor_copy(kT[:, :, 0:META], got.unsqueeze(1).to_broadcast([P, TILES, META]))\
                         .then_inc(pj_taken, 1)
                    elif kind == "v":
                        v.tensor_copy(vmT[:, :], got).then_inc(pj_taken, 1)
                    elif kind == "cc":
                        v.tensor_copy(u_tail[:, i, :], got[:, META - 2:META]).then_inc(pj_taken, 1)
                    else:
                        v.wait_ge(pj_taken, n)
                        v.tensor_tensor(u_tail[:, i, :], u_tail[:, i, :], got[:, META - 2:META], ALU.mult)\
                         .then_inc(pj_taken, 1)

            @block.scalar
            def _(a):
                for n in range(1, len(lns)):
                    for half in range(2):
                        q = 2 * (n - 1) + half
                        a.wait_ge(tp_ready, q + 2)
                        a.activation(hT_hi[:, 4 * half:4 * half + 4, (n - 1) * P:n * P],
                                     tp[q % 2][:, :].rearrange("p (k c) -> p k c", k=4), ACT.Copy)\
                         .then_inc(tp_taken_act, 1)

            @block.tensor
            def _(pe):
                pe.wait_ge(ident_ready, 1)
                pe.wait_ge(ln_done, 1)
                for k in range(KD):
                    mm = pe.transpose(tp[0][:, k * META:(k + 1) * META], hm[:, k * P:(k + 1) * P],
                                      ident[0:META, 0:META])
                mm.then_inc(tp_ready, 1)
                for n in range(1, len(lns)):
                    pe.wait_ge(ln_done, n + 1)
                    for half in range(2):
                        q = 2 * (n - 1) + half
                        pe.wait_ge(tp_taken_dve, max(1, q))
                        for k in range(4):
                            mm = pe.transpose(tp[q % 2][:, k * P:(k + 1) * P],
                                              xs[:, n - 1, (4 * half + k) * P:(4 * half + k + 1) * P], ident[:, :])
                        mm.then_inc(tp_ready, 1)
                uses = [0] * RAW
                for n, (kind, i) in enumerate(meta_strips):
                    uses[n % RAW] += 16 * len(strip_dmas(kind, i, raw[:, 0, :]))
                    pe.wait_ge(raw_in[n % RAW], uses[n % RAW])
                    if n >= 2:
                        pe.wait_ge(pj_taken, n - 1)
                    for k in range(KD):
                        mm = pe.matmul(pj[n % 2][:, 0:META], raw[:, n % RAW, k * P:(k + 1) * P], hmT[:, k, :],
                                       start=(k == 0), stop=(k == KD - 1))
                    mm.then_inc(pj_ready, 1)
                    pe.wait_ge(pj_ready, n + 1)
                    pe.nop().then_inc(raw_used, 1)

        raw_in = [sem(f"raw_in{i}") for i in range(RAW)]
        x_in = [sem(f"x_in{i}") for i in range(TILES)]
        h1_out = [sem(f"h1_out{i}") for i in range(TILES)]
        hi_ready = sem("hi_ready")
        lo_ready = sem("lo_ready")
        strip_done = sem("strip_done")
        branch_ready = sem("branch_ready")
        pj_taken = [sem(f"pj_taken{i}") for i in range(2)]
        carried = sem("carried")
        vbt_ready = sem("vbt_ready")
        v_ready, v_taken = sem("v_ready"), sem("v_taken")
        s_ready, s_prep = sem("s_ready"), sem("s_prep")
        p_ready = sem("p_ready")
        pT_ready, pTa_taken, pTb_taken = sem("pT_ready"), sem("pTa_taken"), sem("pTb_taken")
        o_ready, o_taken = sem("o_ready"), sem("o_taken")
        oT_ready, oThi_ready, oTlo_ready = sem("oT_ready"), sem("oThi_ready"), sem("oTlo_ready")
        z_ready, zhi_ready, zlo_ready = sem("z_ready"), sem("zhi_ready"), sem("zlo_ready")
        m_ready, mhi_ready, mlo_ready = sem("m_ready"), sem("mhi_ready"), sem("mlo_ready")
        wo_ready, wo_taken = sem("wo_ready"), sem("wo_taken")
        hx_ready, hx_hi, hx_lo = sem("hx_ready"), sem("hx_hi"), sem("hx_lo")
        ln_step, ln_moments, ln_rstd, ln_normed, ln_scaled, ln_done = (
            sem("ln_step2"), sem("ln_moments2"), sem("ln_rstd2"), sem("ln_normed2"), sem("ln_scaled2"),
            sem("ln_done2"))
        h_copied = sem("h_copied")
        dve_step = sem("dve_step2")
        prev_set = sem("prev_set")
        rt_ready = sem("rt_ready")
        rt_act, rt_dve = sem("rt_act"), sem("rt_dve")
        lgT_ready, lgT_taken = sem("lgT_ready"), sem("lgT_taken")
        lg_ready, lg_taken = sem("lg_ready"), sem("lg_taken")

        LN1_AT = {1 + i: i for i in range(TILES)}
        RT_AT = {MIX0 + i: i for i in range(TILES + 1)}
        LGT_AT, LG_AT = MIX0 + TILES + 1, MIX0 + TILES + 2
        X_AT = {MIX0 + 8 + i: i for i in range(TILES)}
        LN0_AT = {MIX0 + 8 + 3 * i: i for i in range(TILES)}
        HX_AT = {WO0 - 1 + i: i for i in range(2 * TILES)}
        LNS = 2 * TILES

        def raw_uses(s, b):
            per = lambda ss: 16 * len(strip_dmas(*strips[ss], raw[:, 0, :]))
            slot = s % RAW
            in_block = sum(per(q) for q in range(slot, N, RAW))
            return b * in_block + sum(per(q) for q in range(slot, s + 1, RAW))

        with nc.Block() as block:
            @block.sync
            def _(sp):
                def load(s, b):
                    hold(sp, lo_ready, b * N + s + 1)
                    for dst, src in strip_dmas(*strips[s % N], raw[:, s % RAW, :]):
                        sp.dma_start(dst, src).then_inc(raw_in[s % RAW], 16)

                load(0, 0)
                with sp.Fori(0, BLOCKS) as b:
                    for s in range(N):
                        load(s + 1, b)
                        if s - 3 in LN1_AT:
                            i1 = LN1_AT[s - 3]
                            hold(sp, ln_done, b * LNS + i1 + 1)
                            sp.dma_start(h1[bass.ds(b * TOK + i1 * P, P), :], h[:, i1, :]).then_inc(h1_out[i1], 16)
                        if s in X_AT:
                            i1 = X_AT[s]
                            hold(sp, h_copied, b * TILES + i1 + 1)
                            nxt = (b + 1) % BLOCKS
                            sp.dma_start(xs[:, i1, :], x[bass.ds(nxt * TOK + i1 * P, P), :]).then_inc(x_in[i1], 16)
                for i1 in range(TILES):
                    sp.wait_ge(ln_done, BLOCKS * LNS + i1 + 1)
                    sp.dma_start(h1[BLOCKS * TOK + i1 * P:BLOCKS * TOK + (i1 + 1) * P, :], h[:, i1, :])\
                      .then_inc(h1_out[i1], 16)
                for i1 in range(TILES):
                    sp.wait_ge(h1_out[i1], 16 * (BLOCKS + 1))

            @block.gpsimd
            def _(po):
                def scale(n, i1, rows, gain, shift):
                    hold(po, ln_moments, n + 1)
                    rsqrt(po, P, moments, rstd, minus_half, ln_rstd, 2 * n)
                    po.wait_ge(ln_normed, n + 1)
                    po.tensor_tensor(rows[:, i1, :], rows[:, i1, :], gain[:, :], ALU.mult).then_inc(ln_scaled, 1)
                    po.wait_ge(ln_scaled, n + 1)
                    po.tensor_tensor(rows[:, i1, :], rows[:, i1, :], shift[:, :], ALU.add).then_inc(ln_done, 1)

                with po.Fori(0, BLOCKS) as b:
                    for i1 in range(TILES):
                        scale(b * LNS + i1, i1, h, g1, b1)
                    for i1 in range(TILES):
                        hold(po, h1_out[i1], 16 * b + 16)
                        hold(po, rt_ready, b * 2 * TILES + 2 * i1 + 2)
                        po.tensor_copy(h[:, i1, :], xs[:, i1, :]).then_inc(h_copied, 1)
                    for i1 in range(TILES):
                        scale(b * LNS + TILES + i1, i1, xs, g0, b0)
                for i1 in range(TILES):
                    po.wait_ge(ln_moments, BLOCKS * LNS + i1 + 1)
                    rsqrt(po, P, moments, rstd, minus_half, ln_rstd, 2 * (BLOCKS * LNS + i1))

            @block.scalar
            def _(a):
                def split_hi(b, s):
                    uses = raw_uses(s, b) if s < N else raw_uses(0, b + 1)
                    a.wait_ge(raw_in[s % RAW], uses)
                    a.wait_ge(strip_done, b * N + s + 1)
                    a.activation(w_hi[:, s % 2, :], raw[:, s % RAW, :], ACT.Copy).then_inc(hi_ready, 1)

                def take(b, s):
                    kind, i = strips[s]
                    n = out_no[(s, 0)]
                    got, taken_act = pj[n % 2][:, :], pj_taken[n % 2]
                    if kind in ("k", "v"):
                        a.wait_ge(carried, b + 1)
                    a.wait_ge(strip_done, b * N + s + 3)
                    if kind == "k":
                        tiles = got.rearrange("p (t c) -> p t c", t=TILES)
                        a.activation(kT[:, :, PREV:KEYS], tiles, ACT.Copy)
                        a.activation(kT[:, 1:TILES, META:PREV], tiles[:, 0:TILES - 1, P - CHUNK:P], ACT.Copy)\
                         .then_inc(taken_act, 1)
                    elif kind == "v":
                        a.activation(vT[:, CHUNK:], got, ACT.Copy).then_inc(taken_act, 1)
                    elif kind == "q":
                        a.activation(qT[:, i, :], got, ACT.Copy).then_inc(taken_act, 1)
                    elif kind == "cc":
                        a.activation(work[0][:, 0:TOK], got, ACT.Copy).then_inc(taken_act, 1)
                    elif kind in ("ga", "gc"):
                        w = work[0] if kind == "ga" else work[1]
                        a.activation(w[:, 0:TOK], got, ACT.Sigmoid).then_inc(taken_act, 1)

                def take_rows(b, i):
                    a.wait_ge(rt_ready, (b * TILES + i) * 2 + 1)
                    a.activation(rowsT[:, 0:4, :], tp[0][:, :].rearrange("p (k c) -> p k c", k=4), ACT.Copy)\
                     .then_inc(rt_act, 1)

                split_hi(0, 0)
                with a.Fori(0, BLOCKS) as b:
                    for s, (kind, i) in enumerate(strips):
                        n = s - CONV0
                        if s == CONV0:
                            a.wait_ge(v_ready, b * 2 + 1)
                            a.activation(v_own[:, :, :], tp[0][:, :].rearrange("p (t c) -> p t c", t=TILES),
                                         ACT.Copy).then_inc(v_taken, 1)
                            a.wait_ge(v_ready, b * 2 + 2)
                            a.activation(v_before[0:PREV, :, :],
                                         tp[1][0:PREV, :].rearrange("p (t c) -> p t c", t=TILES),
                                         ACT.Copy).then_inc(v_taken, 1)
                        if n >= 5 and n % 2 == 1 and (n - 5) // 2 < TILES:
                            tt = (n - 5) // 2
                            a.wait_ge(oT_ready, b * TILES + tt + 1)
                            a.activation(oT_hi[:, :, tt * P:(tt + 1) * P],
                                         quad[3][:, :].rearrange("p (k c) -> p k c", k=KA),
                                         ACT.Copy).then_inc(oThi_ready, 1)
                        if 0 <= n < UNITS:
                            a.wait_ge(s_prep, b * UNITS + n + 1)
                            tt, half = n // 2, n % 2
                            for q in range(4):
                                hh = 4 * half + q
                                head = hh // 2 + 4 * (hh % 2)
                                a.activation(prob[:, n % 2, q, :], prob[:, n % 2, q, :], ACT.Exp,
                                             bias=neg_top[:, n % 2, q:q + 1],
                                             accum_out=den[:, tt % 2, head:head + 1])
                            a.activation(sink_e[:, tt % 2, :].rearrange("p (g i) -> p i g", g=2)
                                         [:, 2 * half:2 * half + 2, :],
                                         sink_gap[:, n % 2, :].rearrange("p (i g) -> p i g", g=2), ACT.Exp)\
                             .then_inc(p_ready, 1)
                        split_hi(b, s + 1)
                        if kind in by_act:
                            take(b, s)
                        if 1 <= n <= UNITS:
                            a.wait_ge(pT_ready, b * UNITS + n)
                            a.activation(pTa[:, (n - 1) % 2, :], tp[0][:, :], ACT.Copy).then_inc(pTa_taken, 1)
                            a.activation(pTb[0:PREV, (n - 1) % 2, :], tp[1][0:PREV, :], ACT.Copy)\
                             .then_inc(pTb_taken, 1)
                        if kind == "cb":
                            a.wait_ge(z_ready, b * KC + i + 1)
                            a.activation(zT_hi[:, i, :], work[3][:, 0:TOK], ACT.Copy).then_inc(zhi_ready, 1)
                        if kind == "out":
                            a.wait_ge(m_ready, b * KD + i + 1)
                            a.activation(mT_hi[:, i, :], work[2][:, 0:TOK], ACT.Copy).then_inc(mhi_ready, 1)
                        if RT_AT.get(s, TILES) < TILES:
                            take_rows(b, RT_AT[s])
                        if s in HX_AT:
                            q = HX_AT[s]
                            a.wait_ge(hx_ready, b * 2 * TILES + q + 1)
                            a.activation(hT_hi[:, 4 * (q % 2):4 * (q % 2) + 4, (q // 2) * P:(q // 2 + 1) * P],
                                         tp[q % 2][:, :].rearrange("p (k c) -> p k c", k=4), ACT.Copy)\
                             .then_inc(hx_hi, 1)
                for i in range(TILES):
                    take_rows(BLOCKS, i)

            DVE_STEPS = 3 * UNITS + TILES + 2 * TILES + 4 * KC

            @block.vector
            def _(v):
                def layernorm(n, i1, rows):
                    layernorm_stats(v, P, rows[:, i1, :], stats, moments, ln_step, n, ln_moments)
                    v.wait_ge(ln_moments, n + 1)
                    v.wait_ge(ln_rstd, 2 * n + 2)
                    v.tensor_scalar(rows[:, i1, :], rows[:, i1, :], moments[:, 0:1], rstd[:, 0:1],
                                    ALU.subtract, ALU.mult).then_inc(ln_normed, 1)

                def take_rows(b, i):
                    v.wait_ge(rt_ready, (b * TILES + i) * 2 + 2)
                    v.tensor_copy(rowsT[:, 4:8, :], tp[1][:, :].rearrange("p (k c) -> p k c", k=4))\
                     .then_inc(rt_dve, 1)

                def take_logitsT(b):
                    v.wait_ge(lgT_ready, b + 1)
                    v.tensor_copy(logitsT[0:L, :], quad[0][0:L, :]).then_inc(lgT_taken, 1)

                def take_logits(b, block_of):
                    v.wait_ge(lg_ready, b + 1)
                    v.tensor_tensor(logits[:, bass.ds(block_of * TILES, TILES), :],
                                    quad[1][:, 0:TILES * L].rearrange("p (t l) -> p t l", l=L),
                                    b_r[:, :].unsqueeze(1).to_broadcast([P, TILES, L]), ALU.add).then_inc(lg_taken, 1)

                v.sem_inc(lo_ready, RAW)
                v.sem_inc(strip_done, 2)
                v.sem_inc(pj_taken[0], 1)
                v.sem_inc(pj_taken[1], 1)
                v.sem_inc(wo_taken, 1)
                v.sem_inc(hx_lo, 1)
                v.wait_ge(hi_ready, 1)
                v.tensor_tensor(w_lo[:, 0, :], raw[:, 0, :], w_hi[:, 0, :].bitcast(FP32), ALU.subtract)\
                 .then_inc(lo_ready, 1)
                with v.Fori(0, BLOCKS) as b:
                    steps = [0]

                    def link(ins):
                        steps[0] += 1
                        ins.then_inc(dve_step, 1)
                        v.wait_ge(dve_step, b * DVE_STEPS + steps[0])

                    def split_lo(s):
                        v.wait_ge(hi_ready, b * N + s + 1)
                        v.tensor_tensor(w_lo[:, s % 2, :], raw[:, s % RAW, :], w_hi[:, s % 2, :].bitcast(FP32),
                                        ALU.subtract).then_inc(lo_ready, 1)

                    def output(s, part=0):
                        n = out_no[(s, part)]
                        if strips[s][0] == "out" and part == 0:
                            v.wait_ge(branch_ready, b * KD + strips[s][1] + 1)
                        else:
                            v.wait_ge(strip_done, b * N + s + 3)
                        return pj[n % 2][:, :], pj_taken[n % 2], b * (NOUT // 2) + n // 2 + 2

                    def taken_by_act(s):
                        n = out_no[(s, 0)]
                        v.wait_ge(pj_taken[n % 2], b * (NOUT // 2) + n // 2 + 2)

                    v.tensor_copy(kT[:, 0, META:PREV], kT[:, TILES - 1, KEYS - CHUNK:KEYS])
                    v.tensor_copy(vT[:, 0:CHUNK], vT[:, TOK:TOK + CHUNK]).then_inc(carried, 1)
                    for s, (kind, i) in enumerate(strips):
                        n = s - CONV0
                        if s in LN1_AT:
                            if s == 1:
                                v.wait_ge(wo_taken, b * 2 * TILES + 1)
                            layernorm(b * LNS + LN1_AT[s], LN1_AT[s], h)
                        if s in LN0_AT:
                            v.wait_ge(x_in[LN0_AT[s]], b * 16 + 16)
                            layernorm(b * LNS + TILES + LN0_AT[s], LN0_AT[s], xs)
                        if n >= 5 and n % 2 == 1 and (n - 5) // 2 < TILES:
                            tt = (n - 5) // 2
                            v.wait_ge(oThi_ready, b * TILES + tt + 1)
                            v.tensor_tensor(oT_lo[:, :, tt * P:(tt + 1) * P],
                                            quad[3][:, :].rearrange("p (k c) -> p k c", k=KA),
                                            oT_hi[:, :, tt * P:(tt + 1) * P].bitcast(FP32),
                                            ALU.subtract).then_inc(oTlo_ready, 1)
                        if 4 <= n <= UNITS + 2 and n % 2 == 0:
                            tt = (n - 4) // 2
                            v.wait_ge(o_ready, b * TILES + tt + 1)
                            link(v.tensor_tensor(rden[:, :], den[:, tt % 2, :], sink_e[:, tt % 2, :], ALU.add))
                            link(v.reciprocal(rden[:, :], rden[:, :]))
                            v.tensor_tensor(o_rows[:, :].rearrange("p (h c) -> p h c", h=HEADS),
                                            quad[2][:, :].rearrange("p (h c) -> p h c", h=HEADS),
                                            rden[:, :].unsqueeze(2).to_broadcast([P, HEADS, HEAD]), ALU.mult)\
                             .then_inc(o_taken, 1)
                        if 0 <= n < UNITS:
                            tt, half = n // 2, n % 2
                            v.wait_ge(s_ready, b * UNITS + n + 1)
                            for g in range(2):
                                ins = v.scalar_tensor_tensor(
                                    out=prob[:, n % 2, g:4:2, :],
                                    in0=quad[g][:, 0:2 * KEYS].rearrange("p (q c) -> p q c", q=2),
                                    scalar=HEAD ** -0.5, in1=bias[:, 4 * half + g:4 * half + 4:2, :],
                                    op0=ALU.mult, op1=ALU.add)
                            link(ins)
                            link(v.tensor_reduce(top[:, :], prob[:, n % 2, :, :], AX, ALU.max))
                            link(v.tensor_tensor(top[:, :], top[:, :], sinks[:, 4 * half:4 * half + 4], ALU.max))
                            v.tensor_tensor(sink_gap[:, n % 2, :], sinks[:, 4 * half:4 * half + 4], top[:, :],
                                            ALU.subtract)
                            v.tensor_scalar(neg_top[:, n % 2, :], top[:, :], -1.0, None, ALU.mult)\
                             .then_inc(s_prep, 1)
                            if n == 1:
                                with v.If(b == 0):
                                    v.tensor_copy(bias[0:CHUNK, :, META:PREV], bias_prev[:, :, :])\
                                     .then_inc(prev_set, 1)
                                v.wait_ge(prev_set, 1)
                            if half == 1:
                                link(v.tensor_tensor(bias[:, :, 0:META], bias[:, :, 0:META], meta_step[:, :, :],
                                                     ALU.add))
                        split_lo(s + 1)
                        if s > CONV0 and strips[s - 1][0] == "cb":
                            i1 = strips[s - 1][1]
                            v.wait_ge(zhi_ready, b * KC + i1 + 1)
                            v.tensor_tensor(zT_lo[:, i1, :], work[3][:, 0:TOK], zT_hi[:, i1, :].bitcast(FP32),
                                            ALU.subtract).then_inc(zlo_ready, 1)
                        if s == 2:
                            v.tensor_copy(vBT[:, :, 0:META], vmT[:, :].unsqueeze(1).to_broadcast([P, TILES, META]))
                            taken_by_act(1)
                            v.tensor_copy(vBT[:, :, META:PREV],
                                          vT[:, 0:TOK].rearrange("p (t c) -> p t c", t=TILES)[:, :, 0:CHUNK])\
                             .then_inc(vbt_ready, 1)
                        if kind == "ch":
                            taken_by_act(s - 1)
                            v.tensor_copy(work[2][:, 0:2], u_tail[:, i, :])
                            got, taken, count = output(s)
                            v.tensor_tensor(work[2][:, 2:TOK + 2], got, work[0][:, 0:TOK], ALU.mult).then_inc(taken, 1)
                            v.wait_ge(taken, count)
                            link(v.tensor_scalar(work[1][:, 0:TOK], work[2][:, 0:TOK], cw[:, i, 0:1], None, ALU.mult))
                            for k in (1, 2):
                                link(v.scalar_tensor_tensor(
                                    out=work[1][:, 0:TOK], in0=work[2][:, k:k + TOK], scalar=cw[:, i, k:k + 1],
                                    in1=work[1][:, 0:TOK], op0=ALU.mult, op1=ALU.add))
                            link(v.tensor_copy(u_tail[:, i, :], work[2][:, TOK:TOK + 2]))
                        if kind == "cb":
                            got, taken, count = output(s)
                            v.tensor_tensor(work[3][:, 0:TOK], got, work[1][:, 0:TOK], ALU.mult).then_inc(taken, 1)
                            v.wait_ge(taken, count)
                            v.sem_inc(z_ready, 1)
                        if kind == "out":
                            taken_by_act(s - 1)
                            got, taken, _ = output(s, 0)
                            v.tensor_tensor(work[2][:, 0:TOK], got, work[0][:, 0:TOK], ALU.mult).then_inc(taken, 1)
                            got, taken, count = output(s, 1)
                            v.tensor_tensor(work[3][:, 0:TOK], got, work[1][:, 0:TOK], ALU.mult).then_inc(taken, 1)
                            v.wait_ge(taken, count)
                            v.tensor_tensor(work[2][:, 0:TOK], work[2][:, 0:TOK], work[3][:, 0:TOK], ALU.add)\
                             .then_inc(m_ready, 1)
                            v.wait_ge(mhi_ready, b * KD + i + 1)
                            v.tensor_tensor(mT_lo[:, i, :], work[2][:, 0:TOK], mT_hi[:, i, :].bitcast(FP32),
                                            ALU.subtract).then_inc(mlo_ready, 1)
                        if kind == "wo" and i % 4 == 3:
                            half = i // 4
                            if half == 0:
                                v.wait_ge(h_copied, b * TILES + TILES)
                            for tt in range(TILES):
                                if tt == TILES - 1:
                                    v.wait_ge(strip_done, b * N + s + 3)
                                else:
                                    v.wait_ge(wo_ready, (b * 2 + half) * (TILES - 1) + tt + 1)
                                part = h[:, tt, half * TOK:(half + 1) * TOK]
                                v.scalar_tensor_tensor(out=part, in0=part, scalar=ALPHA, in1=quad[tt][:, :],
                                                       op0=ALU.mult, op1=ALU.add).then_inc(wo_taken, 1)
                        if RT_AT.get(s, TILES) < TILES:
                            take_rows(b, RT_AT[s])
                        if s == LGT_AT:
                            take_logitsT(b)
                        if s == LG_AT:
                            take_logits(b, (b + BLOCKS - 1) % BLOCKS)
                        if s in HX_AT:
                            q = HX_AT[s]
                            v.wait_ge(hx_hi, b * 2 * TILES + q + 1)
                            dst = (slice(None), slice(4 * (q % 2), 4 * (q % 2) + 4),
                                   slice((q // 2) * P, (q // 2 + 1) * P))
                            v.tensor_tensor(hT_lo[dst], tp[q % 2][:, :].rearrange("p (k c) -> p k c", k=4),
                                            hT_hi[dst].bitcast(FP32), ALU.subtract).then_inc(hx_lo, 1)
                    assert steps[0] == DVE_STEPS
                v.wait_ge(wo_taken, BLOCKS * 2 * TILES + 1)
                for i1 in range(TILES):
                    n = BLOCKS * LNS + i1
                    rows = h[:, i1, :]
                    layernorm_stats(v, P, rows, stats, moments, ln_step, n, ln_moments)
                    v.wait_ge(ln_moments, n + 1)
                    v.scalar_tensor_tensor(out=rows, in0=rows, scalar=moments[:, 0:1], in1=g1[:, :],
                                           op0=ALU.subtract, op1=ALU.mult).then_inc(ln_normed, 1)
                    v.wait_ge(ln_normed, n + 1)
                    v.wait_ge(ln_rstd, 2 * n + 2)
                    v.scalar_tensor_tensor(out=rows, in0=rows, scalar=rstd[:, 0:1], in1=b1[:, :],
                                           op0=ALU.mult, op1=ALU.add).then_inc(ln_done, 1)
                    if i1:
                        take_rows(BLOCKS, i1 - 1)
                take_rows(BLOCKS, TILES - 1)
                take_logitsT(BLOCKS)
                take_logits(BLOCKS, BLOCKS - 1)

            @block.tensor
            def _(pe):
                def product(out, hi, lo, x_hi, x_lo, first, last):
                    pe.matmul(out, hi, x_hi, start=first, stop=False)
                    pe.matmul(out, hi, x_lo, start=False, stop=False)
                    return pe.matmul(out, lo, x_hi, start=False, stop=last)

                def router_rows(b, i):
                    pe.wait_ge(ln_done, b * LNS + i + 1)
                    for half, taken in ((0, rt_act), (1, rt_dve)):
                        if i:
                            pe.wait_ge(taken, b * TILES + i)
                        for k in range(4):
                            c = (4 * half + k) * P
                            mm = pe.transpose(tp[half][:, k * P:(k + 1) * P], h[:, i, c:c + P], ident[:, :])
                        mm.then_inc(rt_ready, 1)

                def router_product(b, i):
                    pe.wait_ge(rt_act, b * TILES + i + 1)
                    pe.wait_ge(rt_dve, b * TILES + i + 1)
                    for k in range(KD):
                        mm = pe.matmul(quad[0][0:L, i * P:(i + 1) * P], w_r[:, k, :], rowsT[:, k, :],
                                       start=(k == 0), stop=(k == KD - 1))
                    if i == TILES - 1:
                        mm.then_inc(lgT_ready, 1)

                def router_logits(b):
                    hold(pe, lgT_taken, b + 1)
                    for i in range(TILES):
                        mm = pe.transpose(quad[1][:, i * L:(i + 1) * L], logitsT[0:L, i * P:(i + 1) * P],
                                          ident[0:L, 0:L])
                    mm.then_inc(lg_ready, 1)

                with pe.Fori(0, BLOCKS) as b:
                    pe.wait_ge(hx_lo, b * 2 * TILES + 1)
                    for s, (kind, i) in enumerate(strips):
                        n = s - CONV0
                        if s == CONV0:
                            taken = out_no[(s - 1, 0)]
                            pe.wait_ge(pj_taken[taken % 2], b * (NOUT // 2) + taken // 2 + 2)
                            for tt in range(TILES):
                                mm = pe.transpose(tp[0][:, tt * KVW:(tt + 1) * KVW],
                                                  vT[:, CHUNK + tt * P:CHUNK + (tt + 1) * P], ident[:, :])
                            mm.then_inc(v_ready, 1)
                            pe.wait_ge(vbt_ready, b + 1)
                            for tt in range(TILES):
                                mm = pe.transpose(tp[1][0:PREV, tt * KVW:(tt + 1) * KVW], vBT[:, tt, :], ident[:, :])
                            mm.then_inc(v_ready, 1)
                            pe.wait_ge(carried, b + 1)
                            pe.wait_ge(wo_taken, b * 2 * TILES + 1)
                        if 0 <= n < UNITS:
                            tt, half = n // 2, n % 2
                            if n:
                                pe.wait_ge(s_prep, b * UNITS + n)
                            for q in range(2):
                                for g in range(2):
                                    rows = slice(g * HEAD, (g + 1) * HEAD)
                                    qh = qT[rows, 2 * half + q, tt * P:(tt + 1) * P]
                                    mm = pe.matmul(quad[g][:, q * KEYS:(q + 1) * KEYS], qh, kT[rows, tt, :],
                                                   start=True, stop=True)
                            mm.then_inc(s_ready, 1)
                        pe.wait_ge(lo_ready, b * N + RAW + s + 1)
                        if kind == "out" and i == 0:
                            pe.wait_ge(oTlo_ready, b * TILES + TILES)
                            pe.wait_ge(zlo_ready, b * KC + KC)
                        if kind == "wo":
                            half, kk = i // 4, i % 4
                            if half == 0:
                                pe.wait_ge(mlo_ready, b * KD + 2 * kk + 2)
                            if s == WO0:
                                pe.wait_ge(lg_taken, b + 1)
                            for tt in range(TILES):
                                if half == 1 and kk == 0:
                                    pe.wait_ge(wo_taken, b * 2 * TILES + tt + 2)
                                toks = slice(tt * P, (tt + 1) * P)
                                for k in range(2):
                                    w = slice(k * TOK, (k + 1) * TOK)
                                    mm = product(quad[tt][:, :], mT_hi[:, 2 * kk + k, toks], mT_lo[:, 2 * kk + k, toks],
                                                 w_hi[:, s % 2, w], w_lo[:, s % 2, w],
                                                 kk == 0 and k == 0, kk == 3 and k == 1)
                                if tt == TILES - 1:
                                    mm.then_inc(strip_done, 1)
                                elif kk == 3:
                                    mm.then_inc(wo_ready, 1)
                        else:
                            if kind == "out":
                                parts = [(oT_hi, oT_lo, 0, KA), (zT_hi, zT_lo, KA, KC)]
                            else:
                                parts = [(hT_hi, hT_lo, 0, KD)]
                            for part, (x_hi, x_lo, k0, ks) in enumerate(parts):
                                no = out_no[(s, part)]
                                pe.wait_ge(pj_taken[no % 2], b * (NOUT // 2) + no // 2 + 1)
                                for k in range(ks):
                                    w = slice((k0 + k) * P, (k0 + k + 1) * P)
                                    mm = product(pj[no % 2][:, :], w_hi[:, s % 2, w], w_lo[:, s % 2, w],
                                                 x_hi[:, k, :], x_lo[:, k, :], k == 0, k == ks - 1)
                                mm.then_inc(strip_done if part == len(parts) - 1 else branch_ready, 1)
                        if n >= 4 and n % 2 == 0 and (n - 4) // 2 < TILES:
                            tt = (n - 4) // 2
                            pe.wait_ge(o_taken, b * TILES + tt + 1)
                            if tt:
                                pe.wait_ge(oTlo_ready, b * TILES + tt)
                            for k in range(KA):
                                mm = pe.transpose(quad[3][:, k * P:(k + 1) * P], o_rows[:, k * P:(k + 1) * P],
                                                  ident[:, :])
                            mm.then_inc(oT_ready, 1)
                        if 2 <= n <= UNITS + 1:
                            tt, half, buf = (n - 2) // 2, n % 2, n % 2
                            pe.wait_ge(pTa_taken, b * UNITS + n - 1)
                            pe.wait_ge(pTb_taken, b * UNITS + n - 1)
                            if half == 0 and tt:
                                pe.wait_ge(o_taken, b * TILES + tt)
                            for q in range(4):
                                hh = 4 * half + q
                                g = hh % 2
                                head = hh // 2 + 4 * g
                                out = quad[2][:, head * HEAD:(head + 1) * HEAD]
                                cols = slice(g * HEAD, (g + 1) * HEAD)
                                pe.matmul(out, pTb[0:PREV, buf, q * P:(q + 1) * P], v_before[0:PREV, tt, cols],
                                          start=True, stop=False)
                                mm = pe.matmul(out, pTa[:, buf, q * P:(q + 1) * P], v_own[:, tt, cols],
                                               start=False, stop=True)
                            if half == 1:
                                mm.then_inc(o_ready, 1)
                        if 1 <= n <= UNITS:
                            buf = (n - 1) % 2
                            pe.wait_ge(p_ready, b * UNITS + n)
                            if n == 1:
                                pe.wait_ge(v_taken, b * 2 + 2)
                            else:
                                pe.wait_ge(pTa_taken, b * UNITS + n - 1)
                                pe.wait_ge(pTb_taken, b * UNITS + n - 1)
                            for q in range(4):
                                pe.transpose(tp[0][:, q * P:(q + 1) * P], prob[:, buf, q, PREV:KEYS], ident[:, :])
                                mm = pe.transpose(tp[1][0:PREV, q * P:(q + 1) * P], prob[:, buf, q, 0:PREV],
                                                  ident[:, :])
                            mm.then_inc(pT_ready, 1)
                        if s in RT_AT:
                            i1 = RT_AT[s]
                            if i1 == 0:
                                pe.wait_ge(s_prep, b * UNITS + UNITS)
                            else:
                                router_product(b, i1 - 1)
                            if i1 < TILES:
                                router_rows(b, i1)
                        if s == LG_AT:
                            router_logits(b)
                        if s in HX_AT:
                            q = HX_AT[s]
                            pe.wait_ge(ln_done, b * LNS + TILES + q // 2 + 1)
                            if q >= 2:
                                pe.wait_ge(hx_lo, b * 2 * TILES + q)
                            for k in range(4):
                                c = (4 * (q % 2) + k) * P
                                mm = pe.transpose(tp[q % 2][:, k * P:(k + 1) * P], xs[:, q // 2, c:c + P], ident[:, :])
                            mm.then_inc(hx_ready, 1)
                pe.wait_ge(hx_lo, BLOCKS * 2 * TILES + 1)
                pe.wait_ge(wo_taken, BLOCKS * 2 * TILES + 1)
                for i in range(TILES):
                    router_rows(BLOCKS, i)
                    router_product(BLOCKS, i)
                router_logits(BLOCKS)


def route(nc, t, logits, keep):
    NT = logits.shape[1]
    G, E = t["w_rg"].shape[1], t["w_re"].shape[1]
    EG = E // G
    L = G + E
    slot1, slot2, weight1, weight2, slot_token, bounds, slot_tiles = keep
    MT = slot_tiles

    with ExitStack() as ctx:
        def sb(name, shape, dt=FP32):
            return ctx.enter_context(nc.sbuf_tensor(name, shape, dt))

        def sem(name):
            return ctx.enter_context(nc.semaphore(name))

        before = sb("r_before", [P, P])
        ones = sb("r_ones", [P, P])
        desc = sb("r_desc", [P, E])
        count_up = sb("r_count_up", [P, P])
        token = sb("r_token", [P, NT])
        gmax, gsum, gtop = sb("r_gmax", [P, NT]), sb("r_gsum", [P, NT]), sb("r_gtop", [P, NT])
        gdiff, gexp = sb("r_gdiff", [P, NT, G]), sb("r_gexp", [P, NT, G])
        group, penalty = sb("r_group", [P, NT, G]), sb("r_penalty", [P, NT, G])
        inside, tie = sb("r_inside", [P, NT, E]), sb("r_tie", [P, NT, E])
        hot1, hot2, both = sb("r_hot1", [P, NT, E]), sb("r_hot2", [P, NT, E]), sb("r_both", [P, NT, E])
        best1, best2, tied = sb("r_best1", [P, NT]), sb("r_best2", [P, NT]), sb("r_tied", [P, NT])
        gap, gap_exp = sb("r_gap", [P, NT]), sb("r_gap_exp", [P, NT])
        earlier = sb("r_earlier", [P, NT, E])
        total = sb("r_total", [P, E])
        tiles_i, tiles_f = sb("r_tiles_i", [P, E], I32), sb("r_tiles_f", [P, E])
        upto, first = sb("r_upto", [P, E]), sb("r_first", [P, E])
        slot_f, slot_i = sb("r_slot_f", [P, 2, NT]), sb("r_slot_i", [P, 2, NT], I32)
        in_tile_i, tile_of_i = sb("r_in_tile_i", [P, 2 * NT], I32), sb("r_tile_of_i", [P, 2 * NT], I32)
        in_tile, tile_of = sb("r_in_tile", [P, 2 * NT]), sb("r_tile_of", [P, 2 * NT])
        OH = 8
        hot_lo, hot_hi = sb("r_hot_lo", [P, OH, P]), sb("r_hot_hi", [P, OH, MT])
        ranks = [ctx.enter_context(nc.psum_tensor(f"r_rank{i}", [P, TOK], FP32)) for i in range(2)]
        totals = [ctx.enter_context(nc.psum_tensor(f"r_totals{i}", [P, TOK], FP32)) for i in range(2)]

        tables = sem("r_tables")
        po_step, step = sem("r_po_step"), sem("r_step")
        gdiff_ready, gexp_ready, gap_ready, gap_exp_ready = (
            sem("r_gdiff_ready"), sem("r_gexp_ready"), sem("r_gap_ready"), sem("r_gap_exp_ready"))
        both_ready, counted = sem("r_both_ready"), sem("r_counted")
        places_ready, lo_made, hi_made, hi_made_dve, listed_up, hots_used = (
            sem("r_places_ready"), sem("r_lo_made"), sem("r_hi_made"), sem("r_hi_made_dve"), sem("r_listed_up"), sem("r_hots_used"))

        def number_tile(eng, j, made):
            if j >= OH:
                eng.wait_ge(hots_used, j - OH + 1)
            eng.tensor_scalar(hot_hi[:, j % OH, :], count_up[:, 0:MT], tile_of[:, j:j + 1],
                              token[:, j % NT:j % NT + 1], ALU.is_equal, ALU.mult).then_inc(made, 1)

        with nc.Block() as block:
            @block.gpsimd
            def _(po):
                steps = [0]

                def link(ins):
                    steps[0] += 1
                    ins.then_inc(po_step, 1)
                    po.wait_ge(po_step, steps[0])

                link(po.memset(before[:, :], 1.0))
                po.affine_select(out=before[:, :], in_=before[:, :], compare_op=ALU.is_gt, fill=0.0, base=0,
                                 pattern=[[1, P]], channel_multiplier=-1).then_inc(tables, 1)
                po.iota(desc[:, :], pattern=[[-1, E]], base=E, channel_multiplier=0,
                        allow_small_or_imprecise_dtypes=True).then_inc(tables, 1)
                po.iota(count_up[:, :], pattern=[[1, P]], base=0, channel_multiplier=0,
                        allow_small_or_imprecise_dtypes=True).then_inc(tables, 1)
                po.iota(token[:, :], pattern=[[P, NT]], base=TOK, channel_multiplier=1,
                        allow_small_or_imprecise_dtypes=True).then_inc(tables, 1)
                po.wait_ge(tables, 4)
                po.wait_ge(places_ready, 2)
                for j in range(2 * NT):
                    if j % 3 == 0:
                        number_tile(po, j, hi_made)

            @block.scalar
            def _(a):
                a.wait_ge(gdiff_ready, 1)
                a.activation(gexp[:, :, :], gdiff[:, :, :], ACT.Exp).then_inc(gexp_ready, 1)
                a.wait_ge(gap_ready, 1)
                a.activation(gap_exp[:, :], gap[:, :], ACT.Exp).then_inc(gap_exp_ready, 1)

            @block.vector
            def _(v):
                steps = [0]

                def link(ins):
                    steps[0] += 1
                    ins.then_inc(step, 1)
                    v.wait_ge(step, steps[0])

                v.memset(ones[:, :], 1.0)
                v.wait_ge(tables, 4)

                def over(ap, n):
                    return ap.unsqueeze(2).to_broadcast([P, NT, n])

                def first_best(values, best, n, hot):
                    link(v.tensor_tensor(tie[:, :, 0:n], values, over(best[:, :], n), ALU.is_equal))
                    link(v.tensor_tensor(tie[:, :, 0:n], tie[:, :, 0:n],
                                         desc[:, E - n:E].unsqueeze(1).to_broadcast([P, NT, n]), ALU.mult))
                    link(v.tensor_reduce(tied[:, :], tie[:, :, 0:n], AX, ALU.max))
                    link(v.tensor_tensor(hot[:, :, :], tie[:, :, 0:n], over(tied[:, :], n), ALU.is_equal))

                g_logits, e_logits = logits[:, :, 0:G], logits[:, :, G:L]
                link(v.tensor_reduce(gmax[:, :], g_logits, AX, ALU.max))
                v.tensor_tensor(gdiff[:, :, :], g_logits, over(gmax[:, :], G), ALU.subtract).then_inc(gdiff_ready, 1)
                first_best(g_logits, gmax, G, group)
                v.wait_ge(gexp_ready, 1)
                link(v.tensor_reduce(gsum[:, :], gexp[:, :, :], AX, ALU.add))
                link(v.reciprocal(gtop[:, :], gsum[:, :]))
                link(v.tensor_scalar(penalty[:, :, :], group[:, :, :], -NEG_INF, NEG_INF, ALU.mult, ALU.add))
                by_group = lambda ap: ap.rearrange("p t (g e) -> p t g e", g=G)
                spread = lambda ap: ap.unsqueeze(3).to_broadcast([P, NT, G, EG])
                link(v.tensor_tensor(by_group(inside[:, :, :]), by_group(e_logits), spread(group[:, :, :]), ALU.mult))
                link(v.tensor_tensor(by_group(inside[:, :, :]), by_group(inside[:, :, :]), spread(penalty[:, :, :]),
                                     ALU.add))
                link(v.tensor_reduce(best1[:, :], inside[:, :, :], AX, ALU.max))
                first_best(inside[:, :, :], best1, E, hot1)
                link(v.scalar_tensor_tensor(out=inside[:, :, :], in0=hot1[:, :, :], scalar=3 * NEG_INF,
                                            in1=inside[:, :, :], op0=ALU.mult, op1=ALU.add))
                link(v.tensor_reduce(best2[:, :], inside[:, :, :], AX, ALU.max))
                v.tensor_tensor(gap[:, :], best2[:, :], best1[:, :], ALU.subtract).then_inc(gap_ready, 1)
                first_best(inside[:, :, :], best2, E, hot2)
                v.tensor_tensor(both[:, :, :], hot1[:, :, :], hot2[:, :, :], ALU.add).then_inc(both_ready, 1)
                v.wait_ge(gap_exp_ready, 1)
                link(v.tensor_scalar(weight1[:, :], gap_exp[:, :], 1.0, None, ALU.add))
                link(v.reciprocal(weight1[:, :], weight1[:, :]))
                link(v.tensor_tensor(weight1[:, :], weight1[:, :], gtop[:, :], ALU.mult))
                link(v.tensor_tensor(weight2[:, :], weight1[:, :], gap_exp[:, :], ALU.mult))
                v.wait_ge(counted, 1)
                half = NT // 2
                tot = lambda q: totals[q // half][:, (q % half) * E:(q % half + 1) * E]
                link(v.memset(earlier[:, 0, :], 0.0))
                for q in range(1, NT):
                    link(v.tensor_tensor(earlier[:, q, :], earlier[:, q - 1, :], tot(q - 1), ALU.add))
                link(v.tensor_tensor(total[:, :], earlier[:, NT - 1, :], tot(NT - 1), ALU.add))
                link(v.tensor_scalar(tiles_i[:, :], total[:, :], float(P - 1), None, ALU.add))
                link(v.tensor_scalar(tiles_i[:, :], tiles_i[:, :], P.bit_length() - 1, None, ALU.arith_shift_right))
                link(v.tensor_copy(tiles_f[:, :], tiles_i[:, :]))
                link(v.tensor_scalar(tiles_f[:, :], tiles_f[:, :], 1.0, None, ALU.max))
                link(v.tensor_tensor_scan(upto[:, :], ones[:, 0:E], tiles_f[:, :], 0.0, ALU.mult, ALU.add))
                link(v.tensor_tensor(first[:, :], upto[:, :], tiles_f[:, :], ALU.subtract))
                v.tensor_copy(bounds[:, 0, :], first[:, :])
                v.tensor_copy(bounds[:, 1, :], upto[:, :])
                v.tensor_scalar(bounds[:, 2, 0:E - 1], upto[:, 0:E - 1], -1.0, None, ALU.add)
                v.memset(bounds[:, 2, E - 1:E], MT)
                v.tensor_scalar(bounds[:, 3, :], upto[:, E - 1:E].to_broadcast([P, E]), -16.0, 16.0 * MT,
                                ALU.mult, ALU.add)
                link(v.tensor_scalar(first[:, :], first[:, :], float(P), None, ALU.mult))
                for q in range(2):
                    part = slice(q * half, (q + 1) * half)
                    link(v.tensor_tensor(earlier[:, part, :], earlier[:, part, :],
                                         ranks[q][:, :].rearrange("p (t e) -> p t e", e=E), ALU.add))
                link(v.tensor_tensor(earlier[:, :, :], earlier[:, :, :],
                                     first[:, :].unsqueeze(1).to_broadcast([P, NT, E]), ALU.add))
                for q, hot in enumerate((hot1, hot2)):
                    link(v.tensor_tensor(hot[:, :, :], hot[:, :, :], earlier[:, :, :], ALU.mult))
                    link(v.tensor_reduce(slot_f[:, q, :], hot[:, :, :], AX, ALU.add))
                v.tensor_copy(slot1[:, :], slot_f[:, 0, :])
                v.tensor_copy(slot2[:, :], slot_f[:, 1, :])
                link(v.tensor_copy(slot_i[:, :, :], slot_f[:, :, :]))
                flat = slot_i[:, :, :].rearrange("p k t -> p (k t)")
                link(v.tensor_scalar(in_tile_i[:, :], flat, P - 1, None, ALU.bitwise_and))
                link(v.tensor_scalar(tile_of_i[:, :], flat, P.bit_length() - 1, None, ALU.arith_shift_right))
                v.tensor_copy(in_tile[:, :], in_tile_i[:, :]).then_inc(places_ready, 1)
                v.tensor_copy(tile_of[:, :], tile_of_i[:, :]).then_inc(places_ready, 1)
                v.wait_ge(places_ready, 2)
                for j in range(2 * NT):
                    if j % 3:
                        number_tile(v, j, hi_made_dve)
                    if j >= OH:
                        v.wait_ge(hots_used, j - OH + 1)
                    v.tensor_scalar(hot_lo[:, j % OH, :], count_up[:, :], in_tile[:, j:j + 1], None, ALU.is_equal)\
                     .then_inc(lo_made, 1)
                v.wait_ge(listed_up, 1)
                v.tensor_copy(slot_token[:, :], ranks[0][:, 0:MT])

            @block.tensor
            def _(pe):
                pe.wait_ge(tables, 4)
                pe.wait_ge(both_ready, 1)
                flat = both[:, :, :].rearrange("p t e -> p (t e)")
                for q in range(2):
                    pe.matmul(ranks[q][:, :], before[:, :], flat[:, q * TOK:(q + 1) * TOK], start=True, stop=True)
                    mm = pe.matmul(totals[q][:, :], ones[:, :], flat[:, q * TOK:(q + 1) * TOK], start=True, stop=True)
                mm.then_inc(counted, 1)
                for j in range(2 * NT):
                    pe.wait_ge(lo_made, j + 1)
                    pe.wait_ge(hi_made, j // 3 + 1)
                    if j:
                        pe.wait_ge(hi_made_dve, j - j // 3)
                    mm = pe.matmul(ranks[0][:, 0:MT], hot_lo[:, j % OH, :], hot_hi[:, j % OH, :],
                                   start=(j == 0), stop=(j == 2 * NT - 1))
                    if j < 2 * NT - 1:
                        mm.then_inc(hots_used, 1)
                mm.then_inc(listed_up, 1)


def experts(nc, t, h1, ys, keep):
    D = h1.shape[1]
    E, _, F = t["w_gate"].shape
    KD, KF = D // P, F // P
    slot1, slot2, weight1, weight2, slot_token, bounds, MT = keep
    GC = KD * F // D
    CH = 3 * GC
    KC = KD // GC

    def chunk(e, c):
        if c < 2 * GC:
            w, j = (t["w_gate"], c) if c < GC else (t["w_up"], c - GC)
            return w[bass.ds(e, 1), j * KC * P:(j + 1) * KC * P, :].rearrange("o (k p) n -> p (o k) n", p=P)
        j = c - 2 * GC
        return t["w_down"][bass.ds(e, 1), j * P:(j + 1) * P, :].rearrange("o p n -> p (o n)")

    with ExitStack() as ctx:
        def sb(name, shape, dt=FP32):
            return ctx.enter_context(nc.sbuf_tensor(name, shape, dt))

        def sem(name):
            return ctx.enter_context(nc.semaphore(name))

        raw = sb("e_raw", [P, CH, D])
        w_hi, w_lo = sb("e_w_hi", [P, CH, D], F32R), sb("e_w_lo", [P, CH, D], F32R)
        rows = sb("e_rows", [P, D])
        xT_hi, xT_lo = sb("e_xT_hi", [P, KD, P], F32R), sb("e_xT_lo", [P, KD, P], F32R)
        act = sb("e_act", [P, F])
        prod = sb("e_prod", [P, F])
        aT_hi, aT_lo = sb("e_aT_hi", [P, KF, P], F32R), sb("e_aT_lo", [P, KF, P], F32R)
        y = sb("e_y", [P, D])
        index = sb("e_index", [P, 1], I32)
        filler = sb("e_filler", [P, D])
        ident = sb("e_ident", [P, P])
        bank = [ctx.enter_context(nc.psum_tensor(f"e_bank{i}", [P, TOK], FP32)) for i in range(8)]
        gate_p, up_p, aT_p, tp, yp = bank[0], bank[1], bank[2:4], bank[4:6], bank[6:8]

        raw_in = [sem(f"e_raw_in{c}") for c in range(CH)]
        hi_ready, lo_ready = sem("e_hi_ready"), sem("e_lo_ready")
        gate_ready = sem("e_gate_ready")
        up_ready = sem("e_up_ready")
        act_ready = sem("e_act_ready")
        prod_ready = sem("e_prod_ready")
        aT_up, aT_himade, a_ready = sem("e_aT_up"), sem("e_aT_himade"), sem("e_a_ready")
        rows_in, index_set = sem("e_rows_in"), sem("e_index_set")
        t_ready = sem("e_t_ready")
        t_hi, t_lo = sem("e_t_hi"), sem("e_t_lo")
        y_ready = sem("e_y_ready")
        y_act, y_dve = sem("e_y_act"), sem("e_y_dve")
        y_out = sem("e_y_out")
        filled = sem("e_filled")
        ident_ready = sem("e_ident_ready")

        def tiles_of(eng, e):
            return [eng.value_load(bounds[0:1, q, bass.ds(e, 1)], min_val=0, max_val=top)
                    for q, top in ((0, MT - 1), (1, MT - 1), (2, MT))]

        with nc.Block() as block:
            @block.sync
            def _(sp):
                def load(e, c):
                    dst = raw[:, c, :]
                    if c < 2 * GC:
                        dst = dst.rearrange("p (k n) -> p k n", k=KC)
                    sp.dma_start(dst, chunk(e, c)).then_inc(raw_in[c], 16)

                for c in range(CH):
                    load(0, c)

                def stores(e):
                    lo, hi, _ = tiles_of(sp, e)
                    with sp.Fori(lo, hi) as g:
                        hold(sp, y_act, g + 2)
                        hold(sp, y_dve, g + 2)
                        sp.dma_start(ys[bass.ds(g * P, P), :], y[:, :]).then_inc(y_out, 16)

                with sp.Fori(0, E - 1) as e:
                    for c in range(CH):
                        hold(sp, lo_ready, e * CH + c + 1)
                        load(e + 1, c)
                    stores(e)
                stores(E - 1)
                total = sp.value_load(bounds[0:1, 1, E - 1:E], min_val=1, max_val=MT - 1)
                hold(sp, y_out, total * 16 + 16)

            @block.gpsimd
            def _(po):
                po.memset(filler[:, :], 0.0)
                po.memset(ident[:, :], 0.0).then_inc(ident_ready, 1)
                po.wait_ge(ident_ready, 1)
                po.affine_select(out=ident[:, :], in_=ident[:, :], compare_op=ALU.not_equal, fill=1.0, base=0,
                                 pattern=[[-1, P]], channel_multiplier=1).then_inc(ident_ready, 1)
                total = po.value_load(bounds[0:1, 1, E - 1:E], min_val=1, max_val=MT - 1)
                unfilled = po.value_load(bounds[0:1, 3, 0:1], min_val=16, max_val=16 * MT)

                def gather(g):
                    hold(po, t_ready, g * 2 + 2)
                    po.tensor_copy(index[:, :], slot_token[:, bass.ds(g, 1)]).then_inc(index_set, 1)
                    hold(po, index_set, g + 1)
                    po.indirect_dma_start(out=rows[:, :], out_offset=None, in_=h1[:, :],
                                          in_offset=bass.IndirectOffsetOnAxis(ap=index[:, 0:1], axis=0))\
                      .then_inc(rows_in, 16)
                    hold(po, rows_in, g * 16 + 16)

                with po.Fori(0, total + 1) as g:
                    gather(g)
                with po.Fori(total, MT) as g:
                    po.dma_start(ys[bass.ds(g * P, P), :], filler[:, :]).then_inc(filled, 16)
                hold(po, filled, unfilled)

            @block.scalar
            def _(a):
                def evacuate(count):
                    for half in range(2):
                        a.wait_ge(t_ready, count + half + 1)
                        a.activation(xT_hi[:, 4 * half:4 * half + 4, :],
                                     tp[half][:, :].rearrange("p (k c) -> p k c", k=4), ACT.Copy).then_inc(t_hi, 1)

                def split_hi(e, c):
                    a.wait_ge(raw_in[c], e * 16 + 16)
                    a.activation(w_hi[:, c, :], raw[:, c, :], ACT.Copy).then_inc(hi_ready, 1)

                for c in range(GC):
                    a.wait_ge(raw_in[c], 16)
                    a.activation(w_hi[:, c, :], raw[:, c, :], ACT.Copy).then_inc(hi_ready, 1)
                evacuate(2)
                with a.Fori(0, E) as e:
                    lo, hi, swap = tiles_of(a, e)
                    a.wait_ge(up_ready, lo + 1)
                    for c in range(GC, 2 * GC):
                        split_hi(e, c)
                    a.wait_ge(y_ready, lo * 2 + 2)
                    for c in range(2 * GC, CH):
                        split_hi(e, c)
                    with a.Fori(lo, hi) as g:
                        a.wait_ge(gate_ready, g + 1)
                        a.activation(act[:, :], gate_p[:, :], ACT.Silu).then_inc(act_ready, 1)
                        with a.If(g == swap):
                            for c in range(GC):
                                split_hi(e + 1, c)
                        for j in range(KF):
                            a.wait_ge(aT_up, g * KF + j + 1)
                            a.activation(aT_hi[:, j, :], aT_p[j % 2][:, 0:P], ACT.Copy).then_inc(aT_himade, 1)
                        evacuate(g * 2 + 4)
                        a.wait_ge(y_ready, g * 2 + 3)
                        a.wait_ge(y_out, g * 16 + 16)
                        a.activation(y[:, 0:TOK], yp[0][:, :], ACT.Copy).then_inc(y_act, 1)

            @block.vector
            def _(v):
                def evacuate(hi_count):
                    for half in range(2):
                        v.wait_ge(t_hi, hi_count + half + 1)
                        part = slice(4 * half, 4 * half + 4)
                        v.tensor_tensor(xT_lo[:, part, :], tp[half][:, :].rearrange("p (k c) -> p k c", k=4),
                                        xT_hi[:, part, :].bitcast(FP32), ALU.subtract).then_inc(t_lo, 1)

                def split_lo(e, c):
                    v.wait_ge(hi_ready, e * CH + c + 1)
                    v.tensor_tensor(w_lo[:, c, :], raw[:, c, :], w_hi[:, c, :].bitcast(FP32), ALU.subtract)\
                     .then_inc(lo_ready, 1)

                v.sem_inc(up_ready, 1)
                v.sem_inc(act_ready, 1)
                v.sem_inc(t_ready, 2)
                v.sem_inc(y_ready, 2)
                v.sem_inc(y_act, 1)
                v.sem_inc(y_dve, 1)
                v.sem_inc(y_out, 16)
                for c in range(GC):
                    split_lo(0, c)
                evacuate(0)
                with v.Fori(0, E) as e:
                    lo, hi, swap = tiles_of(v, e)
                    for c in range(GC, CH):
                        split_lo(e, c)
                    with v.Fori(lo, hi) as g:
                        with v.If(g == swap):
                            for c in range(GC):
                                split_lo(e + 1, c)
                        v.wait_ge(act_ready, g + 2)
                        v.wait_ge(up_ready, g + 2)
                        for j in range(KF):
                            part = slice(j * P, (j + 1) * P)
                            v.tensor_tensor(prod[:, part], up_p[:, part], act[:, part], ALU.mult).then_inc(prod_ready, 1)
                        for j in range(KF):
                            v.wait_ge(aT_himade, g * KF + j + 1)
                            v.tensor_tensor(aT_lo[:, j, :], aT_p[j % 2][:, 0:P], aT_hi[:, j, :].bitcast(FP32),
                                            ALU.subtract).then_inc(a_ready, 1)
                        evacuate(g * 2 + 2)
                        v.wait_ge(y_ready, g * 2 + 4)
                        v.wait_ge(y_out, g * 16 + 16)
                        v.tensor_copy(y[:, TOK:2 * TOK], yp[1][:, :]).then_inc(y_dve, 1)

            @block.tensor
            def _(pe):
                def product(out, hi, lo, x_hi, x_lo, first, last):
                    pe.matmul(out, hi, x_hi, start=first, stop=False)
                    pe.matmul(out, hi, x_lo, start=False, stop=False)
                    return pe.matmul(out, lo, x_hi, start=False, stop=last)

                def transposes(rows_count):
                    pe.wait_ge(rows_in, rows_count)
                    for half in range(2):
                        for k in range(4):
                            c = (4 * half + k) * P
                            mm = pe.transpose(tp[half][:, k * P:(k + 1) * P], rows[:, c:c + P], ident[:, :])
                        mm.then_inc(t_ready, 1)

                pe.wait_ge(ident_ready, 2)
                transposes(16)
                with pe.Fori(0, E) as e:
                    lo, hi, _ = tiles_of(pe, e)
                    with pe.Fori(lo, hi) as g:
                        pe.wait_ge(t_lo, g * 2 + 2)
                        pe.wait_ge(act_ready, g + 1)
                        for out, c0, ready in ((gate_p, 0, gate_ready), (up_p, GC, up_ready)):
                            for k in range(KD):
                                c = c0 + k // KC
                                w = slice((k % KC) * F, (k % KC + 1) * F)
                                if k % KC == 0:
                                    pe.wait_ge(lo_ready, e * CH + c + 1)
                                mm = product(out[:, :], xT_hi[:, k, :], xT_lo[:, k, :], w_hi[:, c, w], w_lo[:, c, w],
                                             k == 0, k == KD - 1)
                            mm.then_inc(ready, 1)
                        transposes(g * 16 + 32)
                        pe.wait_ge(y_act, g + 1)
                        pe.wait_ge(y_dve, g + 1)
                        for q in range(KF + 1):
                            if q < KF:
                                pe.wait_ge(prod_ready, g * KF + q + 1)
                                part = slice(q * P, (q + 1) * P)
                                pe.transpose(aT_p[q % 2][:, 0:P], prod[:, part], ident[:, :]).then_inc(aT_up, 1)
                            if q:
                                j = q - 1
                                pe.wait_ge(lo_ready, e * CH + 2 * GC + j + 1)
                                pe.wait_ge(a_ready, g * KF + j + 1)
                                for half in range(2):
                                    w = slice(half * TOK, (half + 1) * TOK)
                                    mm = product(yp[half][:, :], aT_hi[:, j, :], aT_lo[:, j, :],
                                                 w_hi[:, 2 * GC + j, w], w_lo[:, 2 * GC + j, w], j == 0, j == KF - 1)
                                    if j == KF - 1:
                                        mm.then_inc(y_ready, 1)


def combine(nc, t, h1, ys, out, keep):
    S, D = out.shape
    NT = S // P
    slot1, slot2, weight1, weight2, slot_token, bounds, MT = keep
    RING = 4

    with ExitStack() as ctx:
        def sb(name, shape, dt=FP32):
            return ctx.enter_context(nc.sbuf_tensor(name, shape, dt))

        def sem(name):
            return ctx.enter_context(nc.semaphore(name))

        y1, y2 = sb("c_y1", [P, RING, D]), sb("c_y2", [P, RING, D])
        h = sb("c_h", [P, RING, D])
        gain, shift = sb("c_gain", [P, D]), sb("c_bias", [P, D])
        stats, moments, rstd = sb("c_stats", [P, 2, 6]), sb("c_moments", [P, RING, 2]), sb("c_rstd", [P, RING, 1])
        minus_half = sb("c_minus_half", [P, 1])
        index = sb("c_index", [P, RING, 2], I32)
        consts_in = sem("c_consts_in")
        h_in = [sem(f"c_h_in{i}") for i in range(RING)]
        y_in = [sem(f"c_y_in{i}") for i in range(RING)]
        stored = [sem(f"c_stored{i}") for i in range(RING)]
        index_set, summed = sem("c_index_set"), sem("c_summed")
        scaled_h, sum1 = sem("c_scaled_h"), sem("c_sum1")
        ln_step, ln_moments, ln_rstd, ln_gained, ln_done = (
            sem("c_ln_step"), sem("c_ln_moments"), sem("c_ln_rstd"), sem("c_ln_gained"), sem("c_ln_done"))
        half_set = sem("c_half_set")

        with nc.Block() as block:
            @block.sync
            def _(sp):
                sp.dma_start(gain[:, :], t["ln2_g"].unsqueeze(0).to_broadcast([P, D])).then_inc(consts_in, 16)
                sp.dma_start(shift[:, :], t["ln2_b"].unsqueeze(0).to_broadcast([P, D])).then_inc(consts_in, 16)
                def load(i, u):
                    hold(sp, stored[u], i * 16 + 16)
                    sp.dma_start(h[:, u, :], h1[bass.ds(i * RING * P + TOK + u * P, P), :]).then_inc(h_in[u], 16)

                def store(i, u):
                    hold(sp, ln_done, i * RING + u + 1)
                    sp.dma_start(out[bass.ds(i * RING * P + u * P, P), :], h[:, u, :]).then_inc(stored[u], 16)

                for u in range(RING - 1):
                    load(0, u)
                with sp.Fori(0, NT // RING - 1) as i:
                    load(i, RING - 1)
                    for u in range(RING - 1):
                        store(i, u)
                        load(i + 1, u)
                    store(i, RING - 1)
                load(NT // RING - 1, RING - 1)
                for u in range(RING):
                    store(NT // RING - 1, u)
                for u in range(RING):
                    sp.wait_ge(stored[u], (NT // RING + 1) * 16)

            @block.scalar
            def _(a):
                with a.Fori(0, NT // RING) as i:
                    for u in range(RING):
                        a.wait_ge(h_in[u], i * 16 + 16)
                        a.activation(h[:, u, :], h[:, u, :], ACT.Copy, scale=ALPHA).then_inc(scaled_h, 1)

            @block.gpsimd
            def _(po):
                def gather(i, u):
                    n = i * RING + u
                    hold(po, summed, n + 1)
                    for q, slot in enumerate((slot1, slot2)):
                        po.tensor_copy(index[:, u, q:q + 1], slot[:, bass.ds(n, 1)]).then_inc(index_set, 1)
                    hold(po, index_set, n * 2 + 2)
                    for q, y in enumerate((y1, y2)):
                        po.indirect_dma_start(out=y[:, u, :], out_offset=None, in_=ys[:, :],
                                              in_offset=bass.IndirectOffsetOnAxis(ap=index[:, u, q:q + 1], axis=0))\
                          .then_inc(y_in[u], 16)

                def deviation(i, u):
                    n = i * RING + u
                    hold(po, ln_moments, n + 1)
                    po.tensor_scalar(rstd[:, u, :], moments[:, u, 1:2], LN_EPS, None, ALU.add).then_inc(ln_rstd, 1)
                    po.wait_ge(ln_rstd, n * 2 + 1)
                    po.tensor_tensor(rstd[:, u, :], rstd[:, u, :], minus_half[:, :], ALU.pow).then_inc(ln_rstd, 1)

                po.memset(minus_half[:, :], -0.5).then_inc(half_set, 1)
                po.wait_ge(half_set, 1)
                for u in range(RING):
                    gather(0, u)
                with po.Fori(0, NT // RING - 1) as i:
                    for u in range(RING):
                        deviation(i, u)
                        gather(i + 1, u)
                for u in range(RING):
                    deviation(NT // RING - 1, u)

            @block.vector
            def _(v):
                v.sem_inc(summed, RING)
                for u in range(RING):
                    v.sem_inc(stored[u], 16)
                v.wait_ge(consts_in, 32)
                def sum1_of(n, i, u):
                    v.wait_ge(scaled_h, n + 1)
                    v.wait_ge(y_in[u], i * 32 + 32)
                    v.scalar_tensor_tensor(out=h[:, u, :], in0=y1[:, u, :], scalar=weight1[:, bass.ds(n, 1)],
                                           in1=h[:, u, :], op0=ALU.mult, op1=ALU.add).then_inc(sum1, 1)

                def sum2_of(n, i, u):
                    v.wait_ge(sum1, n + 1)
                    v.scalar_tensor_tensor(out=h[:, u, :], in0=y2[:, u, :], scalar=weight2[:, bass.ds(n, 1)],
                                           in1=h[:, u, :], op0=ALU.mult, op1=ALU.add).then_inc(summed, 1)

                def stats_of(n, i, u):
                    v.wait_ge(summed, n + RING + 1)
                    v.bn_stats(stats[:, 0, :], h[:, u, 0:D // 2])
                    v.bn_stats(stats[:, 1, :], h[:, u, D // 2:D]).then_inc(ln_step, 1)

                def tile(i, u, last):
                    n = i * RING + u
                    after = None if last else (n + 1, i + (u + 1) // RING, (u + 1) % RING)
                    if after:
                        sum1_of(*after)
                    hold(v, ln_step, n + 1)
                    v.bn_aggr(moments[:, u, :], stats[:, :, :]).then_inc(ln_moments, 1)
                    if after:
                        sum2_of(*after)
                    v.wait_ge(ln_moments, n + 1)
                    v.scalar_tensor_tensor(out=h[:, u, :], in0=h[:, u, :], scalar=moments[:, u, 0:1],
                                           in1=gain[:, :], op0=ALU.subtract, op1=ALU.mult).then_inc(ln_gained, 1)
                    if after:
                        stats_of(*after)
                    v.wait_ge(ln_gained, n + 1)
                    v.wait_ge(ln_rstd, n * 2 + 2)
                    v.scalar_tensor_tensor(out=h[:, u, :], in0=h[:, u, :], scalar=rstd[:, u, 0:1],
                                           in1=shift[:, :], op0=ALU.mult, op1=ALU.add).then_inc(ln_done, 1)

                for step_of in (sum1_of, sum2_of, stats_of):
                    step_of(0, 0, 0)
                with v.Fori(0, NT // RING - 1) as i:
                    for u in range(RING):
                        tile(i, u, last=False)
                for u in range(RING):
                    tile(NT // RING - 1, u, last=(u == RING - 1))


def encoder_block(nc, x, meta_tokens, ln0_g, ln0_b, w_in, attn_sinks, conv_w, w_attn_out, w_conv_out, w_o,
                  ln1_g, ln1_b, w_router_group, b_router_group, w_router_expert, b_router_expert,
                  w_exp_gate, w_exp_up, w_exp_down, ln2_g, ln2_b, out):
    x2, out2 = x[0], out[0]
    S, D = x2.shape
    E = w_router_expert.shape[2]
    NT = S // P
    slot_tiles = 2 * NT + E + 1
    slot_tiles += slot_tiles % 2
    t = dict(meta=meta_tokens, ln0_g=ln0_g, ln0_b=ln0_b, ln1_g=ln1_g[0], ln1_b=ln1_b[0], ln2_g=ln2_g[0],
             ln2_b=ln2_b[0], sinks=attn_sinks[0], conv_w=conv_w[0], w_rg=w_router_group[0],
             b_rg=b_router_group[0], w_re=w_router_expert[0], b_re=b_router_expert[0],
             w_gate=w_exp_gate[0], w_up=w_exp_up[0], w_down=w_exp_down[0])
    h1 = nc.dram_tensor("h1_rows", [TOK + S, D], FP32).ap()
    ys = nc.dram_tensor("expert_rows", [slot_tiles * P, D], FP32).ap()
    with ExitStack() as ctx:
        def sb(name, shape, dt=FP32):
            return ctx.enter_context(nc.sbuf_tensor(name, shape, dt))
        logits = sb("logits", [P, NT, w_router_group.shape[2] + E])
        mixer(nc, t, x2, w_in[0], w_attn_out[0], w_conv_out[0], w_o[0], h1, logits)
        keep = (sb("slot1", [P, NT], I32), sb("slot2", [P, NT], I32), sb("weight1", [P, NT]),
                sb("weight2", [P, NT]), sb("slot_token", [P, slot_tiles], I32), sb("bounds", [P, 4, E], I32),
                slot_tiles)
        route(nc, t, logits, keep)
        experts(nc, t, h1, ys, keep)
        combine(nc, t, h1, ys, out2, keep)


_INS = ["x", "meta_tokens", "ln0_g", "ln0_b", "w_in", "attn_sinks", "conv_w", "w_attn_out", "w_conv_out", "w_o",
        "ln1_g", "ln1_b", "w_router_group", "b_router_group", "w_router_expert", "b_router_expert",
        "w_exp_gate", "w_exp_up", "w_exp_down", "ln2_g", "ln2_b"]


def kernel(**inputs):
    import numpy as _np
    import concourse.bacc as _bacc
    from concourse import mybir as _mybir
    from concourse.bass_utils import run_bass_kernel_spmd as _run

    nc = _bacc.Bacc("TRN2", target_bir_lowering=False, num_devices=1)
    arrays, args = {}, []
    for name in _INS:
        a = _np.ascontiguousarray(inputs[name])
        arrays[f"in_{name}_dram"] = a
        args.append(nc.dram_tensor(f"in_{name}_dram", a.shape, _mybir.dt.from_np(a.dtype), kind="ExternalInput").ap())
    shape = arrays["in_x_dram"].shape
    args.append(nc.dram_tensor("out_0_dram", shape, _mybir.dt.float32, kind="ExternalOutput").ap())
    encoder_block(nc, *args)
    r = _run(nc, [arrays], core_ids=[0])
    return r.results[0]["out_0_dram"]
```

```python
import concourse.bass as bass
from concourse import mybir
from contextlib import ExitStack
import math

FP32 = mybir.dt.float32
F32R = mybir.dt.float32r
I32 = mybir.dt.int32
ALU = mybir.AluOpType
ACT = mybir.ActivationFunctionType
AX = mybir.AxisListType.X

P = 128
ALPHA = 2.0 ** 0.25
LN_EPS = 1e-5
NEG_INF = -1e30
CHUNK = 64
HEAD = 64
HEADS = 8
PAIRS = HEADS // 2
TAPS = 3

TOK = 512
TILES = TOK // P
BOTH = 1024


def hold(eng, sem, value):
    eng.wait_ge(sem, value)
    eng.nop(nofuse=True)


def layernorm_stats(v, rows, x, stats, moments, ln_step, step0, ln_moments):
    half = x.shape[1] // 2
    v.bn_stats(stats[0:rows, 0, :], x[:, 0:half])
    v.bn_stats(stats[0:rows, 1, :], x[:, half:2 * half]).then_inc(ln_step, 1)
    hold(v, ln_step, step0 + 1)
    v.bn_aggr(moments[0:rows, :], stats[0:rows, :, :]).then_inc(ln_moments, 1)


def rsqrt(po, rows, moments, rstd, minus_half, ln_rstd, count):
    po.tensor_scalar(rstd[0:rows, :], moments[0:rows, 1:2], LN_EPS, None, ALU.add).then_inc(ln_rstd, 1)
    po.wait_ge(ln_rstd, count + 1)
    po.tensor_tensor(rstd[0:rows, :], rstd[0:rows, :], minus_half[0:rows, :], ALU.pow).then_inc(ln_rstd, 1)


def mixer(nc, t, x, w_in, w_attn_out, w_conv_out, w_o, h1, logits):
    D = x.shape[1]
    S = x.shape[0]
    KD = D // P
    BLOCKS = S // TOK
    AW = w_attn_out.shape[0]
    CW = w_conv_out.shape[0]
    KA, KC = AW // P, CW // P
    KVW = 128
    META = t["meta"].shape[0]
    PREV = META + CHUNK
    KEYS = PREV + P
    G, E = t["w_rg"].shape[1], t["w_re"].shape[1]
    L = G + E

    Q0, K0, V0 = 0, AW, AW + KVW
    CB0 = V0 + KVW
    CC0, CH0 = CB0 + CW, CB0 + 2 * CW
    GA0 = CB0 + 3 * CW
    GC0 = GA0 + D

    w_in_k = w_in.rearrange("(k p) n -> p k n", p=P)
    w_ao_k = w_attn_out.rearrange("(k p) n -> p k n", p=P)
    w_co_k = w_conv_out.rearrange("(k p) n -> p k n", p=P)
    w_o_k = w_o.rearrange("(k p) n -> p k n", p=P)

    strips = [("k", 0), ("v", 0)] + [("q", i) for i in range(PAIRS)]
    for i in range(KC):
        strips += [("cc", i), ("ch", i), ("cb", i)]
    for j in range(KD):
        strips += [("ga", j), ("gc", j), ("out", j)]
    for n in range(2):
        strips += [("wo", 4 * n + k) for k in range(4)]
    N = len(strips)
    RAW = 5
    assert N % RAW == 0 and N % 2 == 0
    CONV0 = 2 + PAIRS
    MIX0 = CONV0 + 3 * KC
    WO0 = MIX0 + 3 * KD
    UNITS = 2 * TILES
    base_col = {"k": K0, "v": V0, "cc": CC0, "ch": CH0, "cb": CB0, "ga": GA0, "gc": GC0}

    outputs = []
    for s, (kind, i) in enumerate(strips):
        if kind == "out":
            outputs += [(s, 0), (s, 1)]
        elif kind != "wo":
            outputs += [(s, 0)]
    NOUT = len(outputs)
    assert NOUT % 2 == 0
    out_no = {o: n for n, o in enumerate(outputs)}
    by_act = {"k", "v", "q", "cc", "ga", "gc"}

    def strip_dmas(kind, i, raw):
        full = raw.rearrange("p (k c) -> p k c", k=KD)
        if kind == "q":
            return [(full[:, :, g * HEAD:(g + 1) * HEAD],
                     w_in_k[:, :, Q0 + (i + 4 * g) * HEAD:Q0 + (i + 4 * g + 1) * HEAD]) for g in range(2)]
        if kind == "out":
            return [(full[:, 0:KA, :], w_ao_k[:, :, i * P:(i + 1) * P]),
                    (full[:, KA:KA + KC, :], w_co_k[:, :, i * P:(i + 1) * P])]
        if kind == "wo":
            n, k = i // 4, i % 4
            return [(raw.rearrange("p (k c) -> p k c", k=2),
                     w_o_k[:, 2 * k:2 * k + 2, n * TOK:(n + 1) * TOK])]
        c = base_col[kind] + i * P
        return [(full, w_in_k[:, :, c:c + P])]

    with ExitStack() as ctx:
        def sb(name, shape, dt=FP32):
            return ctx.enter_context(nc.sbuf_tensor(name, shape, dt))

        def sem(name):
            return ctx.enter_context(nc.semaphore(name))

        raw = sb("raw", [P, RAW, D])
        w_hi = sb("w_hi", [P, 2, D], F32R)
        w_lo = sb("w_lo", [P, 2, D], F32R)
        xs = sb("x_rows", [P, TILES, D])
        h = sb("h_rows", [P, TILES, D])
        hT_hi = sb("hT_hi", [P, KD, TOK], F32R)
        hT_lo = sb("hT_lo", [P, KD, TOK], F32R)
        kT = sb("kT", [P, TILES, KEYS])
        vT = sb("vT", [P, CHUNK + TOK])
        vmT = sb("vmT", [P, META])
        bias = sb("bias", [P, HEADS, KEYS])
        meta_step = sb("meta_step", [P, HEADS, META])
        sinks = sb("sinks", [P, HEADS])
        oT_hi = sb("oT_hi", [P, KA, TOK], F32R)
        oT_lo = sb("oT_lo", [P, KA, TOK], F32R)
        zT_hi = sb("zT_hi", [P, KC, TOK], F32R)
        zT_lo = sb("zT_lo", [P, KC, TOK], F32R)
        work = [sb(f"work{i}", [P, TOK + 2]) for i in range(4)]
        u_tail = sb("u_tail", [P, KC, 2])
        cw = sb("conv_taps", [P, KC, TAPS])
        w_r = sb("router_weights", [P, KD, L])
        b_r = sb("router_bias", [P, L])
        ident = sb("ident", [P, P])
        g0, b0 = sb("ln0_gain", [P, D]), sb("ln0_bias", [P, D])
        g1, b1 = sb("ln1_gain", [P, D]), sb("ln1_bias", [P, D])
        stats = sb("stats", [P, 2, 6])
        moments = sb("moments", [P, 2])
        rstd = sb("rstd", [P, 1])
        minus_half = sb("minus_half", [P, 1])
        top = sb("top", [P, 4])
        neg_top = sb("neg_top", [P, 2, 4])
        sink_gap = sb("sink_gap", [P, 2, 4])
        den = sb("den", [P, 2, HEADS])
        sink_e = sb("sink_e", [P, 2, HEADS])
        rden = sb("rden", [P, HEADS])
        shared = -(-nc.sbuf_base // 32) * 32
        arena = sb("arena", [P, 2 * KD * TOK])

        def place(at, name, shape, dt=FP32):
            size = 4 * math.prod(shape[1:])
            assert at[0] + size <= shared + 4 * 2 * KD * TOK
            placed = nc.alloc_sbuf_tensor_at(name, shape, dt, offset=at[0])
            at[0] += size
            return placed

        at = [shared]
        qT = place(at, "qT", [P, PAIRS, TOK])
        prob = place(at, "prob", [P, 2, 4, KEYS])
        pTa = place(at, "pTa", [P, 2, 4 * P])
        pTb = place(at, "pTb", [P, 2, 4 * P])
        o_rows = place(at, "o_rows", [P, AW])
        v_own = place(at, "v_own", [P, TILES, KVW])
        v_before = place(at, "v_before", [P, TILES, KVW])
        vBT = place(at, "vBT", [P, TILES, PREV])
        attention_end = at[0]
        at = [shared]
        mT_hi = place(at, "mixT_hi", [P, KD, TOK], F32R)
        mT_lo = place(at, "mixT_lo", [P, KD, TOK], F32R)
        end = shared + 4 * 2 * KD * TOK
        rowsT = place([end - 4 * D], "router_rowsT", [P, KD, P])
        logitsT = place([end - 4 * (D + TOK)], "router_logitsT", [P, TOK])
        assert attention_end <= end - 4 * HEADS * CHUNK
        bias_prev = place([end - 4 * HEADS * CHUNK], "bias_prev", [P // 2, HEADS, CHUNK])

        banks = [ctx.enter_context(nc.psum_tensor(f"bank{i}", [P, TOK], FP32)) for i in range(8)]
        pj = banks[0:2]
        quad = banks[2:6]
        tp = banks[6:8]

        with ExitStack() as c1, nc.Block() as block:
            def sem1(name):
                return c1.enter_context(nc.semaphore(name))
            meta_in, consts_in, x_in = sem1("meta_in"), sem1("consts_in"), sem1("x_in")
            gains_in = sem1("gains_in")
            raw_in = [sem1(f"meta_raw_in{i}") for i in range(RAW)]
            ln_step, ln_moments, ln_rstd, ln_gained, ln_done = (
                sem1("ln_step"), sem1("ln_moments"), sem1("ln_rstd"), sem1("ln_gained"), sem1("ln_done"))
            pool_step = sem1("pool_step")
            ident_ready, dist_ready = sem1("ident_ready"), sem1("dist_ready")
            tp_ready, tp_taken_act, tp_taken_dve = sem1("tp_ready"), sem1("tp_taken_act"), sem1("tp_taken_dve")
            pj_ready, pj_taken = sem1("mpj_ready"), sem1("mpj_taken")

            meta_strips = [("k", 0), ("v", 0)] + [s for i in range(KC) for s in (("cc", i), ("ch", i))]
            hm = h[0:META, 0, :]
            hmT = work[0][:, 0:KD * META].rearrange("p (k m) -> p k m", k=KD)
            lns = [(META, hm)] + [(P, xs[:, i, :]) for i in range(TILES)]
            order = []
            per_tile = -(-len(meta_strips) // (TILES + 1))
            for n in range(len(meta_strips)):
                order.append(("strip", n))
                if n % per_tile == per_tile - 1 and n // per_tile < TILES:
                    order.append(("rows", n // per_tile + 1))
            assert sum(what == "rows" for what, _ in order) == TILES

            @block.sync
            def _(sp):
                def load_strip(n):
                    for dst, src in strip_dmas(*meta_strips[n], raw[:, n % RAW, :]):
                        sp.dma_start(dst, src).then_inc(raw_in[n % RAW], 16)

                sp.dma_start(hm, t["meta"]).then_inc(meta_in, 16)
                for dst, src in ((g0, t["ln0_g"]), (b0, t["ln0_b"])):
                    sp.dma_start(dst[:, :], src.unsqueeze(0).to_broadcast([P, D])).then_inc(gains_in, 16)
                load_strip(0)
                sp.dma_start(xs[:, :, :], x[0:TOK, :].rearrange("(t p) d -> p t d", p=P)).then_inc(x_in, 16)
                for n in range(1, RAW):
                    load_strip(n)
                for dst, src in ((g1, t["ln1_g"]), (b1, t["ln1_b"])):
                    sp.dma_start(dst[:, :], src.unsqueeze(0).to_broadcast([P, D])).then_inc(consts_in, 16)
                sp.dma_start(rden[:, :], t["sinks"].unsqueeze(0).to_broadcast([P, HEADS])).then_inc(consts_in, 16)
                for k in range(TAPS):
                    sp.dma_start(cw[:, :, k], t["conv_w"][k].rearrange("(i p) -> p i", p=P),
                                 allow_slow_non_contiguous=True).then_inc(consts_in, 16)
                with nc.allow_non_contiguous_dma(reason="the router's 36 columns"):
                    for dst, w in ((w_r[:, :, 0:G], t["w_rg"]), (w_r[:, :, G:L], t["w_re"])):
                        sp.dma_start(dst, w.rearrange("(k p) n -> p k n", p=P)).then_inc(consts_in, 16)
                for dst, row in ((b_r[:, 0:G], t["b_rg"]), (b_r[:, G:L], t["b_re"])):
                    sp.dma_start(dst, row.unsqueeze(0).to_broadcast([P, row.shape[0]])).then_inc(consts_in, 16)
                for n in range(RAW, len(meta_strips)):
                    sp.wait_ge(pj_ready, n - RAW + 1)
                    load_strip(n)
                sp.wait_ge(consts_in, 16 * (7 + TAPS))

            @block.gpsimd
            def _(po):
                steps = [0]

                def link(ins):
                    steps[0] += 1
                    ins.then_inc(pool_step, 1)
                    po.wait_ge(pool_step, steps[0])

                po.memset(minus_half[:, :], -0.5)
                link(po.memset(ident[:, :], 0.0))
                po.affine_select(out=ident[:, :], in_=ident[:, :], compare_op=ALU.not_equal, fill=1.0, base=0,
                                 pattern=[[-1, P]], channel_multiplier=1).then_inc(ident_ready, 1)
                dist = work[1]
                link(po.iota(dist[:, 0:META], pattern=[[-1, META]], base=META, channel_multiplier=1,
                             allow_small_or_imprecise_dtypes=True))
                po.iota(dist[:, META:KEYS], pattern=[[-1, CHUNK + P]], base=CHUNK, channel_multiplier=1,
                        allow_small_or_imprecise_dtypes=True).then_inc(dist_ready, 1)
                po.wait_ge(dist_ready, 2)
                for n, (rows, _) in enumerate(lns):
                    po.wait_ge(ln_moments, n + 1)
                    rsqrt(po, rows, moments, rstd, minus_half, ln_rstd, 2 * n)
                    for g in range(2 if n < PAIRS else 0):
                        slope = 2.0 ** (-8.0 * (n + 4 * g + 1) / HEADS)
                        hh = 2 * n + g
                        link(po.tensor_scalar(bias[:, hh, :], dist[:, 0:KEYS], -slope, None, ALU.mult))
                        link(po.memset(meta_step[:, hh, :], -slope * P))
                link(po.tensor_copy(bias_prev[:, :, :], bias[0:CHUNK, :, META:PREV]))
                link(po.memset(bias[:, :, META:PREV], NEG_INF))
                link(po.memset(bias[0:CHUNK, :, PREV + CHUNK:KEYS], NEG_INF))
                po.wait_ge(consts_in, 16 * (7 + TAPS))
                link(po.tensor_copy(sinks[:, :].rearrange("p (i g) -> p i g", g=2),
                                    rden[:, :].rearrange("p (g i) -> p i g", g=2)))
                po.wait_ge(tp_ready, 1)
                po.memset(h[:, :, :], 0.0)

            @block.vector
            def _(v):
                v.wait_ge(dist_ready, 1)
                v.scalar_tensor_tensor(out=work[1][:, 0:KEYS], in0=work[1][:, 0:KEYS], scalar=-1.0,
                                       in1=work[1][:, 0:KEYS], op0=ALU.mult, op1=ALU.max).then_inc(dist_ready, 1)
                v.memset(kT[:, :, META:KEYS], 0.0)
                v.memset(vT[:, :], 0.0)
                def take_lo(n):
                    for half in range(2):
                        q = 2 * (n - 1) + half
                        v.wait_ge(tp_taken_act, q + 1)
                        dst = (slice(None), slice(4 * half, 4 * half + 4), slice((n - 1) * P, n * P))
                        v.tensor_tensor(hT_lo[dst], tp[q % 2][:, :].rearrange("p (k c) -> p k c", k=4),
                                        hT_hi[dst].bitcast(FP32), ALU.subtract).then_inc(tp_taken_dve, 1)

                v.wait_ge(gains_in, 32)
                for n, (rows, xx) in enumerate(lns):
                    v.wait_ge(meta_in if n == 0 else x_in, 16)
                    layernorm_stats(v, rows, xx, stats, moments, ln_step, n, ln_moments)
                    v.wait_ge(ln_moments, n + 1)
                    v.scalar_tensor_tensor(out=xx, in0=xx, scalar=moments[0:rows, 0:1], in1=g0[0:rows, :],
                                           op0=ALU.subtract, op1=ALU.mult).then_inc(ln_gained, 1)
                    v.wait_ge(ln_gained, n + 1)
                    v.wait_ge(ln_rstd, 2 * n + 2)
                    v.scalar_tensor_tensor(out=xx, in0=xx, scalar=rstd[0:rows, 0:1], in1=b0[0:rows, :],
                                           op0=ALU.mult, op1=ALU.add).then_inc(ln_done, 1)
                    if n == 0:
                        v.wait_ge(tp_ready, 1)
                        v.tensor_copy(hmT, tp[0][:, 0:KD * META].rearrange("p (k m) -> p k m", k=KD))\
                         .then_inc(tp_taken_dve, 1)
                    elif n >= 2:
                        take_lo(n - 1)
                take_lo(TILES)

            @block.scalar
            def _(a):
                for what, n in order:
                    if what == "rows":
                        for half in range(2):
                            q = 2 * (n - 1) + half
                            a.wait_ge(tp_ready, q + 2)
                            a.activation(hT_hi[:, 4 * half:4 * half + 4, (n - 1) * P:n * P],
                                         tp[q % 2][:, :].rearrange("p (k c) -> p k c", k=4), ACT.Copy)\
                             .then_inc(tp_taken_act, 1)
                        continue
                    kind, i = meta_strips[n]
                    a.wait_ge(pj_ready, n + 1)
                    got = pj[n % 2][:, 0:META]
                    if kind == "k":
                        for tt in range(TILES):
                            ins = a.activation(kT[:, tt, 0:META], got, ACT.Copy)
                    elif kind == "v":
                        ins = a.activation(vmT[:, :], got, ACT.Copy)
                    elif kind == "cc":
                        ins = a.activation(work[2][:, 2 * i:2 * i + 2], got[:, META - 2:META], ACT.Copy)
                    else:
                        a.wait_ge(pj_taken, n)
                        for c in range(2):
                            ins = a.activation(u_tail[:, i, c:c + 1], got[:, META - 2 + c:META - 1 + c], ACT.Copy,
                                               scale=work[2][:, 2 * i + c:2 * i + c + 1])
                    ins.then_inc(pj_taken, 1)

            @block.tensor
            def _(pe):
                pe.wait_ge(ident_ready, 1)
                pe.wait_ge(ln_done, 1)
                for k in range(KD):
                    mm = pe.transpose(tp[0][:, k * META:(k + 1) * META], hm[:, k * P:(k + 1) * P],
                                      ident[0:META, 0:META])
                mm.then_inc(tp_ready, 1)
                uses = [0] * RAW
                for what, n in order:
                    if what == "rows":
                        pe.wait_ge(ln_done, n + 1)
                        for half in range(2):
                            q = 2 * (n - 1) + half
                            pe.wait_ge(tp_taken_dve, max(1, q))
                            for k in range(4):
                                mm = pe.transpose(tp[q % 2][:, k * P:(k + 1) * P],
                                                  xs[:, n - 1, (4 * half + k) * P:(4 * half + k + 1) * P], ident[:, :])
                            mm.then_inc(tp_ready, 1)
                        continue
                    kind, i = meta_strips[n]
                    uses[n % RAW] += 16 * len(strip_dmas(kind, i, raw[:, 0, :]))
                    pe.wait_ge(raw_in[n % RAW], uses[n % RAW])
                    if n == 0:
                        pe.wait_ge(tp_taken_dve, 1)
                    if n >= 2:
                        pe.wait_ge(pj_taken, n - 1)
                    for k in range(KD):
                        mm = pe.matmul(pj[n % 2][:, 0:META], raw[:, n % RAW, k * P:(k + 1) * P], hmT[:, k, :],
                                       start=(k == 0), stop=(k == KD - 1))
                    mm.then_inc(pj_ready, 1)

        raw_in = [sem(f"raw_in{i}") for i in range(RAW)]
        x_in = [sem(f"x_in{i}") for i in range(TILES)]
        h1_out = [sem(f"h1_out{i}") for i in range(TILES)]
        hi_ready = sem("hi_ready")
        lo_ready = sem("lo_ready")
        strip_done = sem("strip_done")
        branch_ready = sem("branch_ready")
        pj_taken = [sem(f"pj_taken{i}") for i in range(2)]
        carried = sem("carried")
        vbt_ready = sem("vbt_ready")
        v_ready, v_taken = sem("v_ready"), sem("v_taken")
        s_ready, s_prep = sem("s_ready"), sem("s_prep")
        p_ready = sem("p_ready")
        pT_ready, pTa_taken, pTb_taken = sem("pT_ready"), sem("pTa_taken"), sem("pTb_taken")
        o_ready, o_taken = sem("o_ready"), sem("o_taken")
        oT_ready, oThi_ready, oTlo_ready = sem("oT_ready"), sem("oThi_ready"), sem("oTlo_ready")
        z_ready, zhi_ready, zlo_ready = sem("z_ready"), sem("zhi_ready"), sem("zlo_ready")
        m_ready, mhi_ready, mlo_ready = sem("m_ready"), sem("mhi_ready"), sem("mlo_ready")
        wo_ready, wo_taken = sem("wo_ready"), sem("wo_taken")
        hx_ready, hx_hi, hx_lo = sem("hx_ready"), sem("hx_hi"), sem("hx_lo")
        ln_step, ln_moments, ln_rstd, ln_normed, ln_scaled, ln_done = (
            sem("ln_step2"), sem("ln_moments2"), sem("ln_rstd2"), sem("ln_normed2"), sem("ln_scaled2"),
            sem("ln_done2"))
        h_copied = sem("h_copied")
        dve_step = sem("dve_step2")
        prev_set = sem("prev_set")
        rt_ready = sem("rt_ready")
        rt_act, rt_dve = sem("rt_act"), sem("rt_dve")
        lgT_ready, lgT_taken = sem("lgT_ready"), sem("lgT_taken")
        lg_ready, lg_taken = sem("lg_ready"), sem("lg_taken")

        LN1_AT = {1 + i: i for i in range(TILES)}
        RT_AT = {MIX0 + i: i for i in range(TILES + 1)}
        LGT_AT, LG_AT = MIX0 + TILES + 1, MIX0 + TILES + 2
        X_AT = {MIX0 + 8 + i: i for i in range(TILES)}
        LN0_AT = {MIX0 + 8 + 3 * i: i for i in range(TILES)}
        HX_AT = {WO0 - 1 + i: i for i in range(2 * TILES)}
        LNS = 2 * TILES

        def raw_uses(s, b):
            per = lambda ss: 16 * len(strip_dmas(*strips[ss], raw[:, 0, :]))
            slot = s % RAW
            in_block = sum(per(q) for q in range(slot, N, RAW))
            return b * in_block + sum(per(q) for q in range(slot, s + 1, RAW))

        with nc.Block() as block:
            @block.sync
            def _(sp):
                def load(s, b):
                    hold(sp, lo_ready, b * N + s + 1)
                    for dst, src in strip_dmas(*strips[s % N], raw[:, s % RAW, :]):
                        sp.dma_start(dst, src).then_inc(raw_in[s % RAW], 16)

                load(0, 0)
                with sp.Fori(0, BLOCKS) as b:
                    for s in range(N):
                        load(s + 1, b)
                        if s - 3 in LN1_AT:
                            i1 = LN1_AT[s - 3]
                            hold(sp, ln_done, b * LNS + i1 + 1)
                            sp.dma_start(h1[bass.ds(b * TOK + i1 * P, P), :], h[:, i1, :]).then_inc(h1_out[i1], 16)
                        if s in X_AT:
                            i1 = X_AT[s]
                            hold(sp, h_copied, b * TILES + i1 + 1)
                            nxt = (b + 1) % BLOCKS
                            sp.dma_start(xs[:, i1, :], x[bass.ds(nxt * TOK + i1 * P, P), :]).then_inc(x_in[i1], 16)
                for i1 in range(TILES):
                    sp.wait_ge(ln_done, BLOCKS * LNS + i1 + 1)
                    sp.dma_start(h1[BLOCKS * TOK + i1 * P:BLOCKS * TOK + (i1 + 1) * P, :], h[:, i1, :])\
                      .then_inc(h1_out[i1], 16)
                for i1 in range(TILES):
                    sp.wait_ge(h1_out[i1], 16 * (BLOCKS + 1))

            @block.gpsimd
            def _(po):
                def scale(n, i1, rows, gain, shift):
                    hold(po, ln_moments, n + 1)
                    rsqrt(po, P, moments, rstd, minus_half, ln_rstd, 2 * n)
                    po.wait_ge(ln_normed, n + 1)
                    po.tensor_tensor(rows[:, i1, :], rows[:, i1, :], gain[:, :], ALU.mult).then_inc(ln_scaled, 1)
                    po.wait_ge(ln_scaled, n + 1)
                    po.tensor_tensor(rows[:, i1, :], rows[:, i1, :], shift[:, :], ALU.add).then_inc(ln_done, 1)

                with po.Fori(0, BLOCKS) as b:
                    for i1 in range(TILES):
                        scale(b * LNS + i1, i1, h, g1, b1)
                    for i1 in range(TILES):
                        hold(po, h1_out[i1], 16 * b + 16)
                        hold(po, rt_ready, b * 2 * TILES + 2 * i1 + 2)
                        po.tensor_copy(h[:, i1, :], xs[:, i1, :]).then_inc(h_copied, 1)
                    for i1 in range(TILES):
                        scale(b * LNS + TILES + i1, i1, xs, g0, b0)
                for i1 in range(TILES):
                    po.wait_ge(ln_moments, BLOCKS * LNS + i1 + 1)
                    rsqrt(po, P, moments, rstd, minus_half, ln_rstd, 2 * (BLOCKS * LNS + i1))

            @block.scalar
            def _(a):
                def split_hi(b, s):
                    uses = raw_uses(s, b) if s < N else raw_uses(0, b + 1)
                    a.wait_ge(raw_in[s % RAW], uses)
                    a.wait_ge(strip_done, b * N + s + 1)
                    a.activation(w_hi[:, s % 2, :], raw[:, s % RAW, :], ACT.Copy).then_inc(hi_ready, 1)

                def take(b, s):
                    kind, i = strips[s]
                    n = out_no[(s, 0)]
                    got, taken_act = pj[n % 2][:, :], pj_taken[n % 2]
                    if kind in ("k", "v"):
                        a.wait_ge(carried, b + 1)
                    a.wait_ge(strip_done, b * N + s + 3)
                    if kind == "k":
                        tiles = got.rearrange("p (t c) -> p t c", t=TILES)
                        a.activation(kT[:, :, PREV:KEYS], tiles, ACT.Copy)
                        a.activation(kT[:, 1:TILES, META:PREV], tiles[:, 0:TILES - 1, P - CHUNK:P], ACT.Copy)\
                         .then_inc(taken_act, 1)
                    elif kind == "v":
                        a.activation(vT[:, CHUNK:], got, ACT.Copy).then_inc(taken_act, 1)
                    elif kind == "q":
                        a.activation(qT[:, i, :], got, ACT.Copy).then_inc(taken_act, 1)
                    elif kind == "cc":
                        a.activation(work[0][:, 0:TOK], got, ACT.Copy).then_inc(taken_act, 1)
                    elif kind in ("ga", "gc"):
                        w = work[0] if kind == "ga" else work[1]
                        a.activation(w[:, 0:TOK], got, ACT.Sigmoid).then_inc(taken_act, 1)

                def take_rows(b, i):
                    a.wait_ge(rt_ready, (b * TILES + i) * 2 + 1)
                    a.activation(rowsT[:, 0:4, :], tp[0][:, :].rearrange("p (k c) -> p k c", k=4), ACT.Copy)\
                     .then_inc(rt_act, 1)

                split_hi(0, 0)
                with a.Fori(0, BLOCKS) as b:
                    for s, (kind, i) in enumerate(strips):
                        n = s - CONV0
                        if s == CONV0:
                            a.wait_ge(v_ready, b * 2 + 1)
                            a.activation(v_own[:, :, :], tp[0][:, :].rearrange("p (t c) -> p t c", t=TILES),
                                         ACT.Copy).then_inc(v_taken, 1)
                            a.wait_ge(v_ready, b * 2 + 2)
                            a.activation(v_before[0:PREV, :, :],
                                         tp[1][0:PREV, :].rearrange("p (t c) -> p t c", t=TILES),
                                         ACT.Copy).then_inc(v_taken, 1)
                        if n >= 5 and n % 2 == 1 and (n - 5) // 2 < TILES:
                            tt = (n - 5) // 2
                            a.wait_ge(oT_ready, b * TILES + tt + 1)
                            a.activation(oT_hi[:, :, tt * P:(tt + 1) * P],
                                         quad[3][:, :].rearrange("p (k c) -> p k c", k=KA),
                                         ACT.Copy).then_inc(oThi_ready, 1)
                        if 0 <= n < UNITS:
                            a.wait_ge(s_prep, b * UNITS + n + 1)
                            tt, half = n // 2, n % 2
                            for q in range(4):
                                hh = 4 * half + q
                                head = hh // 2 + 4 * (hh % 2)
                                a.activation(prob[:, n % 2, q, :], prob[:, n % 2, q, :], ACT.Exp,
                                             bias=neg_top[:, n % 2, q:q + 1],
                                             accum_out=den[:, tt % 2, head:head + 1])
                            a.activation(sink_e[:, tt % 2, :].rearrange("p (g i) -> p i g", g=2)
                                         [:, 2 * half:2 * half + 2, :],
                                         sink_gap[:, n % 2, :].rearrange("p (i g) -> p i g", g=2), ACT.Exp)\
                             .then_inc(p_ready, 1)
                        split_hi(b, s + 1)
                        if kind in by_act:
                            take(b, s)
                        if 1 <= n <= UNITS:
                            a.wait_ge(pT_ready, b * UNITS + n)
                            a.activation(pTa[:, (n - 1) % 2, :], tp[0][:, :], ACT.Copy).then_inc(pTa_taken, 1)
                            a.activation(pTb[0:PREV, (n - 1) % 2, :], tp[1][0:PREV, :], ACT.Copy)\
                             .then_inc(pTb_taken, 1)
                        if kind == "cb":
                            a.wait_ge(z_ready, b * KC + i + 1)
                            a.activation(zT_hi[:, i, :], work[3][:, 0:TOK], ACT.Copy).then_inc(zhi_ready, 1)
                        if kind == "out":
                            a.wait_ge(m_ready, b * KD + i + 1)
                            a.activation(mT_hi[:, i, :], work[2][:, 0:TOK], ACT.Copy).then_inc(mhi_ready, 1)
                        if RT_AT.get(s, TILES) < TILES:
                            take_rows(b, RT_AT[s])
                        if s in HX_AT:
                            q = HX_AT[s]
                            a.wait_ge(hx_ready, b * 2 * TILES + q + 1)
                            a.activation(hT_hi[:, 4 * (q % 2):4 * (q % 2) + 4, (q // 2) * P:(q // 2 + 1) * P],
                                         tp[q % 2][:, :].rearrange("p (k c) -> p k c", k=4), ACT.Copy)\
                             .then_inc(hx_hi, 1)
                for i in range(TILES):
                    take_rows(BLOCKS, i)

            DVE_STEPS = 3 * UNITS + TILES + 2 * TILES + 4 * KC

            @block.vector
            def _(v):
                def layernorm(n, i1, rows):
                    layernorm_stats(v, P, rows[:, i1, :], stats, moments, ln_step, n, ln_moments)
                    v.wait_ge(ln_moments, n + 1)
                    v.wait_ge(ln_rstd, 2 * n + 2)
                    v.tensor_scalar(rows[:, i1, :], rows[:, i1, :], moments[:, 0:1], rstd[:, 0:1],
                                    ALU.subtract, ALU.mult).then_inc(ln_normed, 1)

                def take_rows(b, i):
                    v.wait_ge(rt_ready, (b * TILES + i) * 2 + 2)
                    v.tensor_copy(rowsT[:, 4:8, :], tp[1][:, :].rearrange("p (k c) -> p k c", k=4))\
                     .then_inc(rt_dve, 1)

                def take_logitsT(b):
                    v.wait_ge(lgT_ready, b + 1)
                    v.tensor_copy(logitsT[0:L, :], quad[0][0:L, :]).then_inc(lgT_taken, 1)

                def take_logits(b, block_of):
                    v.wait_ge(lg_ready, b + 1)
                    v.tensor_tensor(logits[:, bass.ds(block_of * TILES, TILES), :],
                                    quad[1][:, 0:TILES * L].rearrange("p (t l) -> p t l", l=L),
                                    b_r[:, :].unsqueeze(1).to_broadcast([P, TILES, L]), ALU.add).then_inc(lg_taken, 1)

                v.sem_inc(lo_ready, RAW)
                v.sem_inc(strip_done, 2)
                v.sem_inc(pj_taken[0], 1)
                v.sem_inc(pj_taken[1], 1)
                v.sem_inc(wo_taken, 1)
                v.sem_inc(hx_lo, 1)
                v.wait_ge(hi_ready, 1)
                v.tensor_tensor(w_lo[:, 0, :], raw[:, 0, :], w_hi[:, 0, :].bitcast(FP32), ALU.subtract)\
                 .then_inc(lo_ready, 1)
                with v.Fori(0, BLOCKS) as b:
                    steps = [0]

                    def link(ins):
                        steps[0] += 1
                        ins.then_inc(dve_step, 1)
                        v.wait_ge(dve_step, b * DVE_STEPS + steps[0])

                    def split_lo(s):
                        v.wait_ge(hi_ready, b * N + s + 1)
                        v.tensor_tensor(w_lo[:, s % 2, :], raw[:, s % RAW, :], w_hi[:, s % 2, :].bitcast(FP32),
                                        ALU.subtract).then_inc(lo_ready, 1)

                    def output(s, part=0):
                        n = out_no[(s, part)]
                        if strips[s][0] == "out" and part == 0:
                            v.wait_ge(branch_ready, b * KD + strips[s][1] + 1)
                        else:
                            v.wait_ge(strip_done, b * N + s + 3)
                        return pj[n % 2][:, :], pj_taken[n % 2], b * (NOUT // 2) + n // 2 + 2

                    def taken_by_act(s):
                        n = out_no[(s, 0)]
                        v.wait_ge(pj_taken[n % 2], b * (NOUT // 2) + n // 2 + 2)

                    v.tensor_copy(kT[:, 0, META:PREV], kT[:, TILES - 1, KEYS - CHUNK:KEYS])
                    v.tensor_copy(vT[:, 0:CHUNK], vT[:, TOK:TOK + CHUNK]).then_inc(carried, 1)
                    for s, (kind, i) in enumerate(strips):
                        n = s - CONV0
                        if s in LN1_AT:
                            if s == 1:
                                v.wait_ge(wo_taken, b * 2 * TILES + 1)
                            layernorm(b * LNS + LN1_AT[s], LN1_AT[s], h)
                        if s in LN0_AT:
                            v.wait_ge(x_in[LN0_AT[s]], b * 16 + 16)
                            layernorm(b * LNS + TILES + LN0_AT[s], LN0_AT[s], xs)
                        if n >= 5 and n % 2 == 1 and (n - 5) // 2 < TILES:
                            tt = (n - 5) // 2
                            v.wait_ge(oThi_ready, b * TILES + tt + 1)
                            v.tensor_tensor(oT_lo[:, :, tt * P:(tt + 1) * P],
                                            quad[3][:, :].rearrange("p (k c) -> p k c", k=KA),
                                            oT_hi[:, :, tt * P:(tt + 1) * P].bitcast(FP32),
                                            ALU.subtract).then_inc(oTlo_ready, 1)
                        if 4 <= n <= UNITS + 2 and n % 2 == 0:
                            tt = (n - 4) // 2
                            v.wait_ge(o_ready, b * TILES + tt + 1)
                            link(v.tensor_tensor(rden[:, :], den[:, tt % 2, :], sink_e[:, tt % 2, :], ALU.add))
                            link(v.reciprocal(rden[:, :], rden[:, :]))
                            v.tensor_tensor(o_rows[:, :].rearrange("p (h c) -> p h c", h=HEADS),
                                            quad[2][:, :].rearrange("p (h c) -> p h c", h=HEADS),
                                            rden[:, :].unsqueeze(2).to_broadcast([P, HEADS, HEAD]), ALU.mult)\
                             .then_inc(o_taken, 1)
                        if 0 <= n < UNITS:
                            tt, half = n // 2, n % 2
                            v.wait_ge(s_ready, b * UNITS + n + 1)
                            for g in range(2):
                                ins = v.scalar_tensor_tensor(
                                    out=prob[:, n % 2, g:4:2, :],
                                    in0=quad[g][:, 0:2 * KEYS].rearrange("p (q c) -> p q c", q=2),
                                    scalar=HEAD ** -0.5, in1=bias[:, 4 * half + g:4 * half + 4:2, :],
                                    op0=ALU.mult, op1=ALU.add)
                            link(ins)
                            link(v.tensor_reduce(top[:, :], prob[:, n % 2, :, :], AX, ALU.max))
                            link(v.tensor_tensor(top[:, :], top[:, :], sinks[:, 4 * half:4 * half + 4], ALU.max))
                            v.tensor_tensor(sink_gap[:, n % 2, :], sinks[:, 4 * half:4 * half + 4], top[:, :],
                                            ALU.subtract)
                            v.tensor_scalar(neg_top[:, n % 2, :], top[:, :], -1.0, None, ALU.mult)\
                             .then_inc(s_prep, 1)
                            if n == 1:
                                with v.If(b == 0):
                                    v.tensor_copy(bias[0:CHUNK, :, META:PREV], bias_prev[:, :, :])\
                                     .then_inc(prev_set, 1)
                                v.wait_ge(prev_set, 1)
                            if half == 1:
                                link(v.tensor_tensor(bias[:, :, 0:META], bias[:, :, 0:META], meta_step[:, :, :],
                                                     ALU.add))
                        split_lo(s + 1)
                        if s > CONV0 and strips[s - 1][0] == "cb":
                            i1 = strips[s - 1][1]
                            v.wait_ge(zhi_ready, b * KC + i1 + 1)
                            v.tensor_tensor(zT_lo[:, i1, :], work[3][:, 0:TOK], zT_hi[:, i1, :].bitcast(FP32),
                                            ALU.subtract).then_inc(zlo_ready, 1)
                        if s == 2:
                            v.tensor_copy(vBT[:, :, 0:META], vmT[:, :].unsqueeze(1).to_broadcast([P, TILES, META]))
                            taken_by_act(1)
                            v.tensor_copy(vBT[:, :, META:PREV],
                                          vT[:, 0:TOK].rearrange("p (t c) -> p t c", t=TILES)[:, :, 0:CHUNK])\
                             .then_inc(vbt_ready, 1)
                        if kind == "ch":
                            taken_by_act(s - 1)
                            v.tensor_copy(work[2][:, 0:2], u_tail[:, i, :])
                            got, taken, count = output(s)
                            v.tensor_tensor(work[2][:, 2:TOK + 2], got, work[0][:, 0:TOK], ALU.mult).then_inc(taken, 1)
                            v.wait_ge(taken, count)
                            link(v.tensor_scalar(work[1][:, 0:TOK], work[2][:, 0:TOK], cw[:, i, 0:1], None, ALU.mult))
                            for k in (1, 2):
                                link(v.scalar_tensor_tensor(
                                    out=work[1][:, 0:TOK], in0=work[2][:, k:k + TOK], scalar=cw[:, i, k:k + 1],
                                    in1=work[1][:, 0:TOK], op0=ALU.mult, op1=ALU.add))
                            link(v.tensor_copy(u_tail[:, i, :], work[2][:, TOK:TOK + 2]))
                        if kind == "cb":
                            got, taken, count = output(s)
                            v.tensor_tensor(work[3][:, 0:TOK], got, work[1][:, 0:TOK], ALU.mult).then_inc(taken, 1)
                            v.wait_ge(taken, count)
                            v.sem_inc(z_ready, 1)
                        if kind == "out":
                            taken_by_act(s - 1)
                            got, taken, _ = output(s, 0)
                            v.tensor_tensor(work[2][:, 0:TOK], got, work[0][:, 0:TOK], ALU.mult).then_inc(taken, 1)
                            got, taken, count = output(s, 1)
                            v.tensor_tensor(work[3][:, 0:TOK], got, work[1][:, 0:TOK], ALU.mult).then_inc(taken, 1)
                            v.wait_ge(taken, count)
                            v.tensor_tensor(work[2][:, 0:TOK], work[2][:, 0:TOK], work[3][:, 0:TOK], ALU.add)\
                             .then_inc(m_ready, 1)
                            v.wait_ge(mhi_ready, b * KD + i + 1)
                            v.tensor_tensor(mT_lo[:, i, :], work[2][:, 0:TOK], mT_hi[:, i, :].bitcast(FP32),
                                            ALU.subtract).then_inc(mlo_ready, 1)
                        if kind == "wo" and i % 4 == 3:
                            half = i // 4
                            if half == 0:
                                v.wait_ge(h_copied, b * TILES + TILES)
                            for tt in range(TILES):
                                if tt == TILES - 1:
                                    v.wait_ge(strip_done, b * N + s + 3)
                                else:
                                    v.wait_ge(wo_ready, (b * 2 + half) * (TILES - 1) + tt + 1)
                                part = h[:, tt, half * TOK:(half + 1) * TOK]
                                v.scalar_tensor_tensor(out=part, in0=part, scalar=ALPHA, in1=quad[tt][:, :],
                                                       op0=ALU.mult, op1=ALU.add).then_inc(wo_taken, 1)
                        if RT_AT.get(s, TILES) < TILES:
                            take_rows(b, RT_AT[s])
                        if s == LGT_AT:
                            take_logitsT(b)
                        if s == LG_AT:
                            take_logits(b, (b + BLOCKS - 1) % BLOCKS)
                        if s in HX_AT:
                            q = HX_AT[s]
                            v.wait_ge(hx_hi, b * 2 * TILES + q + 1)
                            dst = (slice(None), slice(4 * (q % 2), 4 * (q % 2) + 4),
                                   slice((q // 2) * P, (q // 2 + 1) * P))
                            v.tensor_tensor(hT_lo[dst], tp[q % 2][:, :].rearrange("p (k c) -> p k c", k=4),
                                            hT_hi[dst].bitcast(FP32), ALU.subtract).then_inc(hx_lo, 1)
                    assert steps[0] == DVE_STEPS
                v.wait_ge(wo_taken, BLOCKS * 2 * TILES + 1)
                for i1 in range(TILES):
                    n = BLOCKS * LNS + i1
                    rows = h[:, i1, :]
                    layernorm_stats(v, P, rows, stats, moments, ln_step, n, ln_moments)
                    v.wait_ge(ln_moments, n + 1)
                    v.scalar_tensor_tensor(out=rows, in0=rows, scalar=moments[:, 0:1], in1=g1[:, :],
                                           op0=ALU.subtract, op1=ALU.mult).then_inc(ln_normed, 1)
                    v.wait_ge(ln_normed, n + 1)
                    v.wait_ge(ln_rstd, 2 * n + 2)
                    v.scalar_tensor_tensor(out=rows, in0=rows, scalar=rstd[:, 0:1], in1=b1[:, :],
                                           op0=ALU.mult, op1=ALU.add).then_inc(ln_done, 1)
                    if i1:
                        take_rows(BLOCKS, i1 - 1)
                take_rows(BLOCKS, TILES - 1)
                take_logitsT(BLOCKS)
                take_logits(BLOCKS, BLOCKS - 1)

            @block.tensor
            def _(pe):
                def product(out, hi, lo, x_hi, x_lo, first, last):
                    pe.matmul(out, hi, x_hi, start=first, stop=False)
                    pe.matmul(out, hi, x_lo, start=False, stop=False)
                    return pe.matmul(out, lo, x_hi, start=False, stop=last)

                def router_rows(b, i):
                    pe.wait_ge(ln_done, b * LNS + i + 1)
                    for half, taken in ((0, rt_act), (1, rt_dve)):
                        if i:
                            pe.wait_ge(taken, b * TILES + i)
                        for k in range(4):
                            c = (4 * half + k) * P
                            mm = pe.transpose(tp[half][:, k * P:(k + 1) * P], h[:, i, c:c + P], ident[:, :])
                        mm.then_inc(rt_ready, 1)

                def router_product(b, i):
                    pe.wait_ge(rt_act, b * TILES + i + 1)
                    pe.wait_ge(rt_dve, b * TILES + i + 1)
                    for k in range(KD):
                        mm = pe.matmul(quad[0][0:L, i * P:(i + 1) * P], w_r[:, k, :], rowsT[:, k, :],
                                       start=(k == 0), stop=(k == KD - 1))
                    if i == TILES - 1:
                        mm.then_inc(lgT_ready, 1)

                def router_logits(b):
                    hold(pe, lgT_taken, b + 1)
                    for i in range(TILES):
                        mm = pe.transpose(quad[1][:, i * L:(i + 1) * L], logitsT[0:L, i * P:(i + 1) * P],
                                          ident[0:L, 0:L])
                    mm.then_inc(lg_ready, 1)

                with pe.Fori(0, BLOCKS) as b:
                    pe.wait_ge(hx_lo, b * 2 * TILES + 1)
                    for s, (kind, i) in enumerate(strips):
                        n = s - CONV0
                        if s == CONV0:
                            taken = out_no[(s - 1, 0)]
                            pe.wait_ge(pj_taken[taken % 2], b * (NOUT // 2) + taken // 2 + 2)
                            for tt in range(TILES):
                                mm = pe.transpose(tp[0][:, tt * KVW:(tt + 1) * KVW],
                                                  vT[:, CHUNK + tt * P:CHUNK + (tt + 1) * P], ident[:, :])
                            mm.then_inc(v_ready, 1)
                            pe.wait_ge(vbt_ready, b + 1)
                            for tt in range(TILES):
                                mm = pe.transpose(tp[1][0:PREV, tt * KVW:(tt + 1) * KVW], vBT[:, tt, :], ident[:, :])
                            mm.then_inc(v_ready, 1)
                            pe.wait_ge(carried, b + 1)
                            pe.wait_ge(wo_taken, b * 2 * TILES + 1)
                        if 0 <= n < UNITS:
                            tt, half = n // 2, n % 2
                            if n:
                                pe.wait_ge(s_prep, b * UNITS + n)
                            for q in range(2):
                                for g in range(2):
                                    rows = slice(g * HEAD, (g + 1) * HEAD)
                                    qh = qT[rows, 2 * half + q, tt * P:(tt + 1) * P]
                                    mm = pe.matmul(quad[g][:, q * KEYS:(q + 1) * KEYS], qh, kT[rows, tt, :],
                                                   start=True, stop=True)
                            mm.then_inc(s_ready, 1)
                        pe.wait_ge(lo_ready, b * N + RAW + s + 1)
                        if kind == "out" and i == 0:
                            pe.wait_ge(oTlo_ready, b * TILES + TILES)
                            pe.wait_ge(zlo_ready, b * KC + KC)
                        if kind == "wo":
                            half, kk = i // 4, i % 4
                            if half == 0:
                                pe.wait_ge(mlo_ready, b * KD + 2 * kk + 2)
                            if s == WO0:
                                pe.wait_ge(lg_taken, b + 1)
                            for tt in range(TILES):
                                if half == 1 and kk == 0:
                                    pe.wait_ge(wo_taken, b * 2 * TILES + tt + 2)
                                toks = slice(tt * P, (tt + 1) * P)
                                for k in range(2):
                                    w = slice(k * TOK, (k + 1) * TOK)
                                    mm = product(quad[tt][:, :], mT_hi[:, 2 * kk + k, toks], mT_lo[:, 2 * kk + k, toks],
                                                 w_hi[:, s % 2, w], w_lo[:, s % 2, w],
                                                 kk == 0 and k == 0, kk == 3 and k == 1)
                                if tt == TILES - 1:
                                    mm.then_inc(strip_done, 1)
                                elif kk == 3:
                                    mm.then_inc(wo_ready, 1)
                        else:
                            if kind == "out":
                                parts = [(oT_hi, oT_lo, 0, KA), (zT_hi, zT_lo, KA, KC)]
                            else:
                                parts = [(hT_hi, hT_lo, 0, KD)]
                            for part, (x_hi, x_lo, k0, ks) in enumerate(parts):
                                no = out_no[(s, part)]
                                pe.wait_ge(pj_taken[no % 2], b * (NOUT // 2) + no // 2 + 1)
                                for k in range(ks):
                                    w = slice((k0 + k) * P, (k0 + k + 1) * P)
                                    mm = product(pj[no % 2][:, :], w_hi[:, s % 2, w], w_lo[:, s % 2, w],
                                                 x_hi[:, k, :], x_lo[:, k, :], k == 0, k == ks - 1)
                                mm.then_inc(strip_done if part == len(parts) - 1 else branch_ready, 1)
                        if n >= 4 and n % 2 == 0 and (n - 4) // 2 < TILES:
                            tt = (n - 4) // 2
                            pe.wait_ge(o_taken, b * TILES + tt + 1)
                            if tt:
                                pe.wait_ge(oTlo_ready, b * TILES + tt)
                            for k in range(KA):
                                mm = pe.transpose(quad[3][:, k * P:(k + 1) * P], o_rows[:, k * P:(k + 1) * P],
                                                  ident[:, :])
                            mm.then_inc(oT_ready, 1)
                        if 2 <= n <= UNITS + 1:
                            tt, half, buf = (n - 2) // 2, n % 2, n % 2
                            pe.wait_ge(pTa_taken, b * UNITS + n - 1)
                            pe.wait_ge(pTb_taken, b * UNITS + n - 1)
                            if half == 0 and tt:
                                pe.wait_ge(o_taken, b * TILES + tt)
                            for q in range(4):
                                hh = 4 * half + q
                                g = hh % 2
                                head = hh // 2 + 4 * g
                                out = quad[2][:, head * HEAD:(head + 1) * HEAD]
                                cols = slice(g * HEAD, (g + 1) * HEAD)
                                pe.matmul(out, pTb[0:PREV, buf, q * P:(q + 1) * P], v_before[0:PREV, tt, cols],
                                          start=True, stop=False)
                                mm = pe.matmul(out, pTa[:, buf, q * P:(q + 1) * P], v_own[:, tt, cols],
                                               start=False, stop=True)
                            if half == 1:
                                mm.then_inc(o_ready, 1)
                        if 1 <= n <= UNITS:
                            buf = (n - 1) % 2
                            pe.wait_ge(p_ready, b * UNITS + n)
                            if n == 1:
                                pe.wait_ge(v_taken, b * 2 + 2)
                            else:
                                pe.wait_ge(pTa_taken, b * UNITS + n - 1)
                                pe.wait_ge(pTb_taken, b * UNITS + n - 1)
                            for q in range(4):
                                pe.transpose(tp[0][:, q * P:(q + 1) * P], prob[:, buf, q, PREV:KEYS], ident[:, :])
                                mm = pe.transpose(tp[1][0:PREV, q * P:(q + 1) * P], prob[:, buf, q, 0:PREV],
                                                  ident[:, :])
                            mm.then_inc(pT_ready, 1)
                        if s in RT_AT:
                            i1 = RT_AT[s]
                            if i1 == 0:
                                pe.wait_ge(s_prep, b * UNITS + UNITS)
                            else:
                                router_product(b, i1 - 1)
                            if i1 < TILES:
                                router_rows(b, i1)
                        if s == LG_AT:
                            router_logits(b)
                        if s in HX_AT:
                            q = HX_AT[s]
                            pe.wait_ge(ln_done, b * LNS + TILES + q // 2 + 1)
                            if q >= 2:
                                pe.wait_ge(hx_lo, b * 2 * TILES + q)
                            for k in range(4):
                                c = (4 * (q % 2) + k) * P
                                mm = pe.transpose(tp[q % 2][:, k * P:(k + 1) * P], xs[:, q // 2, c:c + P], ident[:, :])
                            mm.then_inc(hx_ready, 1)
                pe.wait_ge(hx_lo, BLOCKS * 2 * TILES + 1)
                pe.wait_ge(wo_taken, BLOCKS * 2 * TILES + 1)
                for i in range(TILES):
                    router_rows(BLOCKS, i)
                    router_product(BLOCKS, i)
                router_logits(BLOCKS)


def route(nc, t, logits, keep):
    NT = logits.shape[1]
    G, E = t["w_rg"].shape[1], t["w_re"].shape[1]
    EG = E // G
    L = G + E
    slot1, slot2, weight1, weight2, slot_token, bounds, slot_tiles = keep
    MT = slot_tiles

    with ExitStack() as ctx:
        def sb(name, shape, dt=FP32):
            return ctx.enter_context(nc.sbuf_tensor(name, shape, dt))

        def sem(name):
            return ctx.enter_context(nc.semaphore(name))

        before = sb("r_before", [P, P])
        ones = sb("r_ones", [P, P])
        desc = sb("r_desc", [P, E])
        count_up = sb("r_count_up", [P, P])
        token = sb("r_token", [P, NT])
        gmax, gsum, gtop = sb("r_gmax", [P, NT]), sb("r_gsum", [P, NT]), sb("r_gtop", [P, NT])
        gdiff, gexp = sb("r_gdiff", [P, NT, G]), sb("r_gexp", [P, NT, G])
        group, masked = sb("r_group", [P, NT, G]), sb("r_masked", [P, NT, E])
        inside, tie = sb("r_inside", [P, NT, EG]), sb("r_tie", [P, NT, EG])
        place1, place2 = sb("r_place1", [P, NT, EG]), sb("r_place2", [P, NT, EG])
        hot1, hot2, both = sb("r_hot1", [P, NT, E]), sb("r_hot2", [P, NT, E]), sb("r_both", [P, NT, E])
        best1, best2, tied = sb("r_best1", [P, NT]), sb("r_best2", [P, NT]), sb("r_tied", [P, NT])
        gap, gap_exp = sb("r_gap", [P, NT]), sb("r_gap_exp", [P, NT])
        earlier = sb("r_earlier", [P, NT, E])
        total = sb("r_total", [P, E])
        tiles_i, tiles_f = sb("r_tiles_i", [P, E], I32), sb("r_tiles_f", [P, E])
        upto, first = sb("r_upto", [P, E]), sb("r_first", [P, E])
        slot_f, slot_i = sb("r_slot_f", [P, 2, NT]), sb("r_slot_i", [P, 2, NT], I32)
        in_tile_i, tile_of_i = sb("r_in_tile_i", [P, 2 * NT], I32), sb("r_tile_of_i", [P, 2 * NT], I32)
        in_tile, tile_of = sb("r_in_tile", [P, 2 * NT]), sb("r_tile_of", [P, 2 * NT])
        OH = 8
        hot_lo, hot_hi = sb("r_hot_lo", [P, OH, P]), sb("r_hot_hi", [P, OH, MT])
        ranks = [ctx.enter_context(nc.psum_tensor(f"r_rank{i}", [P, TOK], FP32)) for i in range(2)]
        totals = [ctx.enter_context(nc.psum_tensor(f"r_totals{i}", [P, TOK], FP32)) for i in range(2)]

        tables = sem("r_tables")
        po_step, step = sem("r_po_step"), sem("r_step")
        diff_ready, exp_ready = sem("r_diff_ready"), sem("r_exp_ready")
        both_ready, counted = sem("r_both_ready"), sem("r_counted")
        places_ready, lo_made, hi_made, hi_made_dve, listed_up, hots_used = (
            sem("r_places_ready"), sem("r_lo_made"), sem("r_hi_made"), sem("r_hi_made_dve"), sem("r_listed_up"), sem("r_hots_used"))

        def number_tile(eng, j, made):
            if j >= OH:
                eng.wait_ge(hots_used, j - OH + 1)
            eng.tensor_scalar(hot_hi[:, j % OH, :], count_up[:, 0:MT], tile_of[:, j:j + 1],
                              token[:, j % NT:j % NT + 1], ALU.is_equal, ALU.mult).then_inc(made, 1)

        with nc.Block() as block:
            @block.gpsimd
            def _(po):
                steps = [0]

                def link(ins):
                    steps[0] += 1
                    ins.then_inc(po_step, 1)
                    po.wait_ge(po_step, steps[0])

                link(po.memset(before[:, :], 1.0))
                po.affine_select(out=before[:, :], in_=before[:, :], compare_op=ALU.is_gt, fill=0.0, base=0,
                                 pattern=[[1, P]], channel_multiplier=-1).then_inc(tables, 1)
                po.iota(desc[:, :], pattern=[[-1, E]], base=E, channel_multiplier=0,
                        allow_small_or_imprecise_dtypes=True).then_inc(tables, 1)
                po.iota(count_up[:, :], pattern=[[1, P]], base=0, channel_multiplier=0,
                        allow_small_or_imprecise_dtypes=True).then_inc(tables, 1)
                po.iota(token[:, :], pattern=[[P, NT]], base=TOK, channel_multiplier=1,
                        allow_small_or_imprecise_dtypes=True).then_inc(tables, 1)
                po.wait_ge(tables, 4)
                po.wait_ge(places_ready, 2)
                for j in range(2 * NT):
                    if j % 3 == 0:
                        number_tile(po, j, hi_made)

            @block.scalar
            def _(a):
                a.wait_ge(diff_ready, 1)
                a.activation(gexp[:, :, :], gdiff[:, :, :], ACT.Exp).then_inc(exp_ready, 1)
                a.wait_ge(diff_ready, 2)
                a.activation(gap_exp[:, :], gap[:, :], ACT.Exp).then_inc(exp_ready, 1)

            @block.vector
            def _(v):
                steps = [0]

                def link(ins):
                    steps[0] += 1
                    ins.then_inc(step, 1)
                    v.wait_ge(step, steps[0])

                v.memset(ones[:, :], 1.0)
                v.wait_ge(tables, 4)

                def over(ap, n):
                    return ap.unsqueeze(2).to_broadcast([P, NT, n])

                def first_best(values, best, n, hot):
                    link(v.tensor_tensor(tie[:, :, 0:n], values, over(best[:, :], n), ALU.is_equal))
                    link(v.tensor_tensor(tie[:, :, 0:n], tie[:, :, 0:n],
                                         desc[:, E - n:E].unsqueeze(1).to_broadcast([P, NT, n]), ALU.mult))
                    link(v.tensor_reduce(tied[:, :], tie[:, :, 0:n], AX, ALU.max))
                    link(v.tensor_tensor(hot[:, :, :], tie[:, :, 0:n], over(tied[:, :], n), ALU.is_equal))

                g_logits, e_logits = logits[:, :, 0:G], logits[:, :, G:L]
                link(v.tensor_reduce(gmax[:, :], g_logits, AX, ALU.max))
                v.tensor_tensor(gdiff[:, :, :], g_logits, over(gmax[:, :], G), ALU.subtract).then_inc(diff_ready, 1)
                first_best(g_logits, gmax, G, group)
                v.wait_ge(exp_ready, 1)
                link(v.tensor_reduce(gsum[:, :], gexp[:, :, :], AX, ALU.add))
                link(v.reciprocal(gtop[:, :], gsum[:, :]))
                by_group = lambda ap: ap.rearrange("p t (g e) -> p t g e", g=G)
                spread = lambda ap: ap.unsqueeze(3).to_broadcast([P, NT, G, EG])
                link(v.tensor_tensor(by_group(masked[:, :, :]), by_group(e_logits), spread(group[:, :, :]), ALU.mult))
                link(v.tensor_reduce(inside[:, :, :], masked[:, :, :].rearrange("p t (g e) -> p t e g", g=G),
                                     AX, ALU.add))
                link(v.tensor_reduce(best1[:, :], inside[:, :, :], AX, ALU.max))
                first_best(inside[:, :, :], best1, EG, place1)
                link(v.scalar_tensor_tensor(out=inside[:, :, :], in0=place1[:, :, :], scalar=NEG_INF,
                                            in1=inside[:, :, :], op0=ALU.mult, op1=ALU.add))
                link(v.tensor_reduce(best2[:, :], inside[:, :, :], AX, ALU.max))
                v.tensor_tensor(gap[:, :], best2[:, :], best1[:, :], ALU.subtract).then_inc(diff_ready, 1)
                first_best(inside[:, :, :], best2, EG, place2)
                for hot, place in ((hot1, place1), (hot2, place2)):
                    ins = v.tensor_tensor(by_group(hot[:, :, :]), spread(group[:, :, :]),
                                          place[:, :, :].unsqueeze(2).to_broadcast([P, NT, G, EG]), ALU.mult)
                link(ins)
                v.tensor_tensor(both[:, :, :], hot1[:, :, :], hot2[:, :, :], ALU.add).then_inc(both_ready, 1)
                v.wait_ge(exp_ready, 2)
                link(v.tensor_scalar(weight1[:, :], gap_exp[:, :], 1.0, None, ALU.add))
                link(v.reciprocal(weight1[:, :], weight1[:, :]))
                link(v.tensor_tensor(weight1[:, :], weight1[:, :], gtop[:, :], ALU.mult))
                link(v.tensor_tensor(weight2[:, :], weight1[:, :], gap_exp[:, :], ALU.mult))
                v.wait_ge(counted, 1)
                half = NT // 2
                tot = lambda q: totals[q // half][:, (q % half) * E:(q % half + 1) * E]
                link(v.memset(earlier[:, 0, :], 0.0))
                for q in range(1, NT):
                    link(v.tensor_tensor(earlier[:, q, :], earlier[:, q - 1, :], tot(q - 1), ALU.add))
                link(v.tensor_tensor(total[:, :], earlier[:, NT - 1, :], tot(NT - 1), ALU.add))
                link(v.tensor_scalar(tiles_i[:, :], total[:, :], float(P - 1), None, ALU.add))
                link(v.tensor_scalar(tiles_i[:, :], tiles_i[:, :], P.bit_length() - 1, None, ALU.arith_shift_right))
                link(v.tensor_copy(tiles_f[:, :], tiles_i[:, :]))
                link(v.tensor_scalar(tiles_f[:, :], tiles_f[:, :], 1.0, None, ALU.max))
                link(v.tensor_tensor_scan(upto[:, :], ones[:, 0:E], tiles_f[:, :], 0.0, ALU.mult, ALU.add))
                link(v.tensor_tensor(first[:, :], upto[:, :], tiles_f[:, :], ALU.subtract))
                v.tensor_copy(bounds[:, 0, :], first[:, :])
                v.tensor_copy(bounds[:, 1, :], upto[:, :])
                v.scalar_tensor_tensor(out=bounds[:, 4, :], in0=upto[:, :], scalar=float(BOTH), in1=first[:, :],
                                       op0=ALU.mult, op1=ALU.add)
                v.tensor_scalar(bounds[:, 2, 0:E - 1], upto[:, 0:E - 1], -1.0, None, ALU.add)
                v.memset(bounds[:, 2, E - 1:E], MT)
                v.tensor_scalar(bounds[:, 3, 0:1], upto[:, E - 1:E], -16.0, 16.0 * MT, ALU.mult, ALU.add)
                v.tensor_scalar(bounds[:, 3, 1:2], upto[:, E - 1:E], -1.0, float(MT), ALU.mult, ALU.add)
                link(v.tensor_scalar(first[:, :], first[:, :], float(P), None, ALU.mult))
                for q in range(2):
                    part = slice(q * half, (q + 1) * half)
                    link(v.tensor_tensor(earlier[:, part, :], earlier[:, part, :],
                                         ranks[q][:, :].rearrange("p (t e) -> p t e", e=E), ALU.add))
                link(v.tensor_tensor(earlier[:, :, :], earlier[:, :, :],
                                     first[:, :].unsqueeze(1).to_broadcast([P, NT, E]), ALU.add))
                for q, hot in enumerate((hot1, hot2)):
                    link(v.tensor_tensor(hot[:, :, :], hot[:, :, :], earlier[:, :, :], ALU.mult))
                    link(v.tensor_reduce(slot_f[:, q, :], hot[:, :, :], AX, ALU.add))
                v.tensor_copy(slot1[:, :], slot_f[:, 0, :])
                v.tensor_copy(slot2[:, :], slot_f[:, 1, :])
                link(v.tensor_copy(slot_i[:, :, :], slot_f[:, :, :]))
                flat = slot_i[:, :, :].rearrange("p k t -> p (k t)")
                link(v.tensor_scalar(in_tile_i[:, :], flat, P - 1, None, ALU.bitwise_and))
                link(v.tensor_scalar(tile_of_i[:, :], flat, P.bit_length() - 1, None, ALU.arith_shift_right))
                v.tensor_copy(in_tile[:, :], in_tile_i[:, :]).then_inc(places_ready, 1)
                v.tensor_copy(tile_of[:, :], tile_of_i[:, :]).then_inc(places_ready, 1)
                v.wait_ge(places_ready, 2)
                for j in range(2 * NT):
                    if j % 3:
                        number_tile(v, j, hi_made_dve)
                    if j >= OH:
                        v.wait_ge(hots_used, j - OH + 1)
                    v.tensor_scalar(hot_lo[:, j % OH, :], count_up[:, :], in_tile[:, j:j + 1], None, ALU.is_equal)\
                     .then_inc(lo_made, 1)
                v.wait_ge(listed_up, 1)
                v.tensor_copy(slot_token[:, :], ranks[0][:, 0:MT])

            @block.tensor
            def _(pe):
                pe.wait_ge(tables, 4)
                pe.wait_ge(both_ready, 1)
                flat = both[:, :, :].rearrange("p t e -> p (t e)")
                for q in range(2):
                    pe.matmul(ranks[q][:, :], before[:, :], flat[:, q * TOK:(q + 1) * TOK], start=True, stop=True)
                    mm = pe.matmul(totals[q][:, :], ones[:, :], flat[:, q * TOK:(q + 1) * TOK], start=True, stop=True)
                mm.then_inc(counted, 1)
                for j in range(2 * NT):
                    pe.wait_ge(lo_made, j + 1)
                    pe.wait_ge(hi_made, j // 3 + 1)
                    if j:
                        pe.wait_ge(hi_made_dve, j - j // 3)
                    mm = pe.matmul(ranks[0][:, 0:MT], hot_lo[:, j % OH, :], hot_hi[:, j % OH, :],
                                   start=(j == 0), stop=(j == 2 * NT - 1))
                    if j < 2 * NT - 1:
                        mm.then_inc(hots_used, 1)
                mm.then_inc(listed_up, 1)


def experts(nc, t, h1, ys, keep):
    D = h1.shape[1]
    E, _, F = t["w_gate"].shape
    KD, KF = D // P, F // P
    slot1, slot2, weight1, weight2, slot_token, bounds, MT = keep
    least = 2 * slot1.shape[1]
    assert MT - least + 1 < least
    GC = KD * F // D
    CH = 3 * GC
    KC = KD // GC

    def chunk(e, c):
        if c < 2 * GC:
            w, j = (t["w_gate"], c) if c < GC else (t["w_up"], c - GC)
            return w[bass.ds(e, 1), j * KC * P:(j + 1) * KC * P, :].rearrange("o (k p) n -> p (o k) n", p=P)
        j = c - 2 * GC
        return t["w_down"][bass.ds(e, 1), j * P:(j + 1) * P, :].rearrange("o p n -> p (o n)")

    with ExitStack() as ctx:
        def sb(name, shape, dt=FP32):
            return ctx.enter_context(nc.sbuf_tensor(name, shape, dt))

        def sem(name):
            return ctx.enter_context(nc.semaphore(name))

        raw = sb("e_raw", [P, CH, D])
        w_hi, w_lo = sb("e_w_hi", [P, CH, D], F32R), sb("e_w_lo", [P, CH, D], F32R)
        rows = sb("e_rows", [P, D])
        xT_hi, xT_lo = sb("e_xT_hi", [P, KD, P], F32R), sb("e_xT_lo", [P, KD, P], F32R)
        act = sb("e_act", [P, F])
        prod = sb("e_prod", [P, F])
        aT_hi, aT_lo = sb("e_aT_hi", [P, KF, P], F32R), sb("e_aT_lo", [P, KF, P], F32R)
        y = sb("e_y", [P, D])
        index = sb("e_index", [P, 1], I32)
        filler = sb("e_filler", [P, D])
        ident = sb("e_ident", [P, P])
        bank = [ctx.enter_context(nc.psum_tensor(f"e_bank{i}", [P, TOK], FP32)) for i in range(8)]
        gate_p, aT_p, tp, yp = bank[0], bank[2:4], bank[4:6], bank[6:8]
        up_p = (bank[1], bank[0])

        raw_in = [sem(f"e_raw_in{c}") for c in range(CH)]
        hi_ready, lo_ready = sem("e_hi_ready"), sem("e_lo_ready")
        down_hi, down_lo = sem("e_down_hi"), sem("e_down_lo")
        gate_ready = sem("e_gate_ready")
        up_ready = sem("e_up_ready")
        act_ready = sem("e_act_ready")
        prod_ready = sem("e_prod_ready")
        aT_up, aT_himade, a_ready = sem("e_aT_up"), sem("e_aT_himade"), sem("e_a_ready")
        rows_in, index_set = sem("e_rows_in"), sem("e_index_set")
        t_ready = sem("e_t_ready")
        t_hi, t_lo = sem("e_t_hi"), sem("e_t_lo")
        y_ready = sem("e_y_ready")
        y_taken = sem("e_y_taken")
        y_out = sem("e_y_out")
        filled = sem("e_filled")
        ident_ready = sem("e_ident_ready")

        def tiles_of(eng, e, values=2):
            return [eng.value_load(bounds[0:1, q, bass.ds(e, 1)], min_val=0, max_val=top)
                    for q, top in ((0, MT - 1), (1, MT - 1), (2, MT))[0:values]]

        def split_count(e, c, high):
            if c < 2 * GC:
                return (hi_ready if high else lo_ready), e * 2 * GC + c + 1
            return (down_hi if high else down_lo), e * (CH - 2 * GC) + c - 2 * GC + 1

        with nc.Block() as block:
            @block.sync
            def _(sp):
                def load(e, c):
                    dst = raw[:, c, :]
                    if c < 2 * GC:
                        dst = dst.rearrange("p (k n) -> p k n", k=KC)
                    sp.dma_start(dst, chunk(e, c)).then_inc(raw_in[c], 16)

                for c in range(CH):
                    if c == GC:
                        sp.wait_ge(rows_in, 16)
                    load(0, c)

                def stores(e):
                    lo, hi = tiles_of(sp, e)
                    with sp.Fori(lo, hi) as g:
                        hold(sp, y_taken, g * 2 + 4)
                        sp.dma_start(ys[bass.ds(g * P, P), :], y[:, :]).then_inc(y_out, 16)

                with sp.Fori(0, E - 1) as e:
                    for c in range(CH):
                        hold(sp, *split_count(e, c, False))
                        load(e + 1, c)
                    stores(e)
                stores(E - 1)
                total = sp.value_load(bounds[0:1, 1, E - 1:E], min_val=1, max_val=MT - 1)
                hold(sp, y_out, total * 16 + 16)

            @block.gpsimd
            def _(po):
                po.memset(filler[:, :], 0.0)
                po.memset(ident[:, :], 0.0).then_inc(ident_ready, 1)
                po.wait_ge(ident_ready, 1)
                po.affine_select(out=ident[:, :], in_=ident[:, :], compare_op=ALU.not_equal, fill=1.0, base=0,
                                 pattern=[[-1, P]], channel_multiplier=1).then_inc(ident_ready, 1)
                total = po.value_load(bounds[0:1, 1, E - 1:E], min_val=least, max_val=MT - 1)
                filled_count = po.value_load(bounds[0:1, 3, 0:1], min_val=16, max_val=16 * (MT - least))
                unfilled = po.value_load(bounds[0:1, 3, 1:2], min_val=1, max_val=MT - least)

                def gather(g):
                    hold(po, t_ready, g * 2 + 2)
                    po.tensor_copy(index[:, :], slot_token[:, bass.ds(g, 1)]).then_inc(index_set, 1)
                    hold(po, index_set, g + 1)
                    po.indirect_dma_start(out=rows[:, :], out_offset=None, in_=h1[:, :],
                                          in_offset=bass.IndirectOffsetOnAxis(ap=index[:, 0:1], axis=0))\
                      .then_inc(rows_in, 16)
                    hold(po, rows_in, g * 16 + 16)

                gather(0)
                gather(1)
                with po.Fori(0, unfilled) as j:
                    po.dma_start(ys[bass.ds((MT - 1) * P - j * P, P), :], filler[:, :]).then_inc(filled, 16)
                    gather(j + 2)
                with po.Fori(unfilled + 2, total + 1) as g:
                    gather(g)
                hold(po, filled, filled_count)

            @block.scalar
            def _(a):
                def evacuate(count):
                    for half in range(2):
                        a.wait_ge(t_ready, count + half + 1)
                        a.activation(xT_hi[:, 4 * half:4 * half + 4, :],
                                     tp[half][:, :].rearrange("p (k c) -> p k c", k=4), ACT.Copy).then_inc(t_hi, 1)

                def split_hi(e, c):
                    a.wait_ge(raw_in[c], e * 16 + 16)
                    a.activation(w_hi[:, c, :], raw[:, c, :], ACT.Copy).then_inc(split_count(e, c, True)[0], 1)

                for c in range(2 * GC):
                    if c == GC:
                        evacuate(2)
                    split_hi(0, c)
                with a.Fori(0, E) as e:
                    lo, hi, swap = tiles_of(a, e, 3)
                    with a.Fori(lo, hi) as g:
                        a.wait_ge(gate_ready, g + 1)
                        a.activation(act[:, :], gate_p[:, :], ACT.Silu).then_inc(act_ready, 1)
                        with a.If(g == lo):
                            a.wait_ge(y_ready, g * 2 + 2)
                            for c in range(2 * GC, CH):
                                split_hi(e, c)
                        with a.If(g == swap):
                            for c in range(GC):
                                split_hi(e + 1, c)
                        for j in range(KF):
                            if j == 2:
                                evacuate(g * 2 + 4)
                            a.wait_ge(aT_up, g * KF + j + 1)
                            a.activation(aT_hi[:, j, :], aT_p[j % 2][:, 0:P], ACT.Copy).then_inc(aT_himade, 1)
                        with a.If(g == swap):
                            a.wait_ge(up_ready, g * 2 + 3)
                            for c in range(GC, 2 * GC):
                                split_hi(e + 1, c)
                        a.wait_ge(y_ready, g * 2 + 3)
                        a.wait_ge(y_out, g * 16 + 16)
                        a.activation(y[:, 0:TOK], yp[0][:, :], ACT.Copy).then_inc(y_taken, 1)

            @block.vector
            def _(v):
                def evacuate(hi_count):
                    for half in range(2):
                        v.wait_ge(t_hi, hi_count + half + 1)
                        part = slice(4 * half, 4 * half + 4)
                        v.tensor_tensor(xT_lo[:, part, :], tp[half][:, :].rearrange("p (k c) -> p k c", k=4),
                                        xT_hi[:, part, :].bitcast(FP32), ALU.subtract).then_inc(t_lo, 1)

                def split_lo(e, c):
                    v.wait_ge(*split_count(e, c, True))
                    v.tensor_tensor(w_lo[:, c, :], raw[:, c, :], w_hi[:, c, :].bitcast(FP32), ALU.subtract)\
                     .then_inc(split_count(e, c, False)[0], 1)

                v.sem_inc(up_ready, 1)
                v.sem_inc(act_ready, 1)
                v.sem_inc(t_ready, 2)
                v.sem_inc(y_ready, 2)
                v.sem_inc(y_taken, 2)
                v.sem_inc(y_out, 16)
                for c in range(2 * GC):
                    if c == GC:
                        evacuate(0)
                    split_lo(0, c)
                with v.Fori(0, E) as e:
                    lo, hi, swap = tiles_of(v, e, 3)
                    def splits(down, ahead):
                        if down:
                            with v.If(g == lo):
                                for c in down:
                                    split_lo(e, 2 * GC + c)
                        with v.If(g == swap):
                            for c in ahead:
                                split_lo(e + 1, c)

                    with v.Fori(lo, hi) as g:
                        splits((0, 1), (0, 1))
                        v.wait_ge(act_ready, g + 2)
                        for half in range(2):
                            if half:
                                splits((2,), (2,))
                            v.wait_ge(up_ready, g * 2 + half + 2)
                            for j in range(half * KF // 2, (half + 1) * KF // 2):
                                part = slice(j * P, (j + 1) * P)
                                v.tensor_tensor(prod[:, part], up_p[half][:, part], act[:, part], ALU.mult)\
                                 .then_inc(prod_ready, 1)
                        for j in range(KF):
                            if j == 2:
                                evacuate(g * 2 + 2)
                            if j == KF - 1:
                                splits((3,), (3,))
                            v.wait_ge(aT_himade, g * KF + j + 1)
                            v.tensor_tensor(aT_lo[:, j, :], aT_p[j % 2][:, 0:P], aT_hi[:, j, :].bitcast(FP32),
                                            ALU.subtract).then_inc(a_ready, 1)
                        splits((), range(GC, 2 * GC))
                        v.wait_ge(y_ready, g * 2 + 4)
                        v.wait_ge(y_out, g * 16 + 16)
                        v.tensor_copy(y[:, TOK:2 * TOK], yp[1][:, :]).then_inc(y_taken, 1)

            @block.tensor
            def _(pe):
                def product(out, hi, lo, x_hi, x_lo, first, last):
                    pe.matmul(out, hi, x_hi, start=first, stop=False)
                    pe.matmul(out, hi, x_lo, start=False, stop=False)
                    return pe.matmul(out, lo, x_hi, start=False, stop=last)

                def transposes(rows_count):
                    pe.wait_ge(rows_in, rows_count)
                    for half in range(2):
                        for k in range(4):
                            c = (4 * half + k) * P
                            mm = pe.transpose(tp[half][:, k * P:(k + 1) * P], rows[:, c:c + P], ident[:, :])
                        mm.then_inc(t_ready, 1)

                pe.wait_ge(ident_ready, 2)
                transposes(16)
                with pe.Fori(0, E) as e:
                    both = pe.value_load(bounds[0:1, 4, bass.ds(e, 1)], min_val=1, max_val=BOTH * MT - 1)
                    lo, hi = both % BOTH, both // BOTH
                    with pe.Fori(lo, hi) as g:
                        pe.wait_ge(t_lo, g * 2 + 2)
                        columns = slice(0, F)
                        for part, (out, c0, ready) in enumerate(((gate_p, 0, gate_ready), (up_p[0], GC, up_ready),
                                                                 (up_p[1], GC, up_ready))):
                            if part:
                                columns = slice((part - 1) * F // 2, part * F // 2)
                            if part == 2:
                                pe.wait_ge(act_ready, g + 2)
                            for k in range(KD):
                                c = c0 + k // KC
                                w = slice((k % KC) * F + columns.start, (k % KC) * F + columns.stop)
                                if k % KC == 0 and part < 2:
                                    pe.wait_ge(*split_count(e, c, False))
                                mm = product(out[:, columns], xT_hi[:, k, :], xT_lo[:, k, :], w_hi[:, c, w],
                                             w_lo[:, c, w], k == 0, k == KD - 1)
                            mm.then_inc(ready, 1)

                        def product_transposed(q):
                            pe.wait_ge(prod_ready, g * KF + q + 1)
                            if q >= 2:
                                pe.wait_ge(a_ready, g * KF + q - 1)
                            pe.transpose(aT_p[q % 2][:, 0:P], prod[:, q * P:(q + 1) * P], ident[:, :])\
                              .then_inc(aT_up, 1)

                        product_transposed(0)
                        product_transposed(1)
                        transposes(g * 16 + 32)
                        product_transposed(2)
                        pe.wait_ge(y_taken, g * 2 + 2)
                        for j in range(KF):
                            if j == 1:
                                product_transposed(3)
                            pe.wait_ge(*split_count(e, 2 * GC + j, False))
                            pe.wait_ge(a_ready, g * KF + j + 1)
                            for half in range(2):
                                w = slice(half * TOK, (half + 1) * TOK)
                                mm = product(yp[half][:, :], aT_hi[:, j, :], aT_lo[:, j, :],
                                             w_hi[:, 2 * GC + j, w], w_lo[:, 2 * GC + j, w], j == 0, j == KF - 1)
                                if j == KF - 1:
                                    mm.then_inc(y_ready, 1)


def combine(nc, t, h1, ys, out, keep):
    S, D = out.shape
    NT = S // P
    slot1, slot2, weight1, weight2, slot_token, bounds, MT = keep
    RING = 4

    with ExitStack() as ctx:
        def sb(name, shape, dt=FP32):
            return ctx.enter_context(nc.sbuf_tensor(name, shape, dt))

        def sem(name):
            return ctx.enter_context(nc.semaphore(name))

        y1, y2 = sb("c_y1", [P, RING, D]), sb("c_y2", [P, RING, D])
        h = sb("c_h", [P, RING, D])
        gain, shift = sb("c_gain", [P, D]), sb("c_bias", [P, D])
        stats, moments, rstd = sb("c_stats", [P, 2, 6]), sb("c_moments", [P, RING, 2]), sb("c_rstd", [P, RING, 1])
        minus_half = sb("c_minus_half", [P, 1])
        index = sb("c_index", [P, RING, 2], I32)
        consts_in = sem("c_consts_in")
        h_in = [sem(f"c_h_in{i}") for i in range(RING)]
        y_in = [sem(f"c_y_in{i}") for i in range(RING)]
        stored = [sem(f"c_stored{i}") for i in range(RING)]
        index_set, summed = sem("c_index_set"), sem("c_summed")
        scaled_h, sum1 = sem("c_scaled_h"), sem("c_sum1")
        ln_step, ln_moments, ln_rstd, ln_gained, ln_done = (
            sem("c_ln_step"), sem("c_ln_moments"), sem("c_ln_rstd"), sem("c_ln_gained"), sem("c_ln_done"))
        half_set = sem("c_half_set")

        with nc.Block() as block:
            @block.sync
            def _(sp):
                def load(i, u):
                    hold(sp, stored[u], i * 16 + 16)
                    sp.dma_start(h[:, u, :], h1[bass.ds(i * RING * P + TOK + u * P, P), :]).then_inc(h_in[u], 16)

                def store(i, u):
                    hold(sp, ln_done, i * RING + u + 1)
                    sp.dma_start(out[bass.ds(i * RING * P + u * P, P), :], h[:, u, :]).then_inc(stored[u], 16)

                for u in range(RING - 1):
                    load(0, u)
                    if u == 0:
                        for dst, row in ((gain, t["ln2_g"]), (shift, t["ln2_b"])):
                            sp.dma_start(dst[:, :], row.unsqueeze(0).to_broadcast([P, D])).then_inc(consts_in, 16)
                with sp.Fori(0, NT // RING - 1) as i:
                    load(i, RING - 1)
                    for u in range(RING - 1):
                        store(i, u)
                        load(i + 1, u)
                    store(i, RING - 1)
                load(NT // RING - 1, RING - 1)
                for u in range(RING):
                    store(NT // RING - 1, u)
                for u in range(RING):
                    sp.wait_ge(stored[u], (NT // RING + 1) * 16)

            @block.scalar
            def _(a):
                with a.Fori(0, NT // RING) as i:
                    for u in range(RING):
                        a.wait_ge(h_in[u], i * 16 + 16)
                        a.activation(h[:, u, :], h[:, u, :], ACT.Copy, scale=ALPHA).then_inc(scaled_h, 1)

            @block.gpsimd
            def _(po):
                def gather(i, u):
                    n = i * RING + u
                    hold(po, summed, n + 1)
                    for q, slot in enumerate((slot1, slot2)):
                        po.tensor_copy(index[:, u, q:q + 1], slot[:, bass.ds(n, 1)]).then_inc(index_set, 1)
                    hold(po, index_set, n * 2 + 2)
                    for q, y in enumerate((y1, y2)):
                        po.indirect_dma_start(out=y[:, u, :], out_offset=None, in_=ys[:, :],
                                              in_offset=bass.IndirectOffsetOnAxis(ap=index[:, u, q:q + 1], axis=0))\
                          .then_inc(y_in[u], 16)

                def deviation(i, u):
                    n = i * RING + u
                    hold(po, ln_moments, n + 1)
                    po.tensor_scalar(rstd[:, u, :], moments[:, u, 1:2], LN_EPS, None, ALU.add).then_inc(ln_rstd, 1)
                    po.wait_ge(ln_rstd, n * 2 + 1)
                    po.tensor_tensor(rstd[:, u, :], rstd[:, u, :], minus_half[:, :], ALU.pow).then_inc(ln_rstd, 1)

                po.memset(minus_half[:, :], -0.5).then_inc(half_set, 1)
                po.wait_ge(half_set, 1)
                for u in range(RING):
                    gather(0, u)
                with po.Fori(0, NT // RING - 1) as i:
                    for u in range(RING):
                        deviation(i, u)
                        gather(i + 1, u)
                for u in range(RING):
                    deviation(NT // RING - 1, u)

            @block.vector
            def _(v):
                v.sem_inc(summed, RING)
                for u in range(RING):
                    v.sem_inc(stored[u], 16)
                def sum1_of(n, i, u):
                    v.wait_ge(scaled_h, n + 1)
                    v.wait_ge(y_in[u], i * 32 + 32)
                    v.scalar_tensor_tensor(out=h[:, u, :], in0=y1[:, u, :], scalar=weight1[:, bass.ds(n, 1)],
                                           in1=h[:, u, :], op0=ALU.mult, op1=ALU.add).then_inc(sum1, 1)

                def sum2_of(n, i, u):
                    v.wait_ge(sum1, n + 1)
                    v.scalar_tensor_tensor(out=h[:, u, :], in0=y2[:, u, :], scalar=weight2[:, bass.ds(n, 1)],
                                           in1=h[:, u, :], op0=ALU.mult, op1=ALU.add).then_inc(summed, 1)

                def stats_of(n, i, u):
                    v.wait_ge(summed, n + RING + 1)
                    v.bn_stats(stats[:, 0, :], h[:, u, 0:D // 2])
                    v.bn_stats(stats[:, 1, :], h[:, u, D // 2:D]).then_inc(ln_step, 1)

                def tile(i, u, last):
                    n = i * RING + u
                    after = None if last else (n + 1, i + (u + 1) // RING, (u + 1) % RING)
                    if after:
                        sum1_of(*after)
                    hold(v, ln_step, n + 1)
                    v.bn_aggr(moments[:, u, :], stats[:, :, :]).then_inc(ln_moments, 1)
                    if after:
                        sum2_of(*after)
                    v.wait_ge(ln_moments, n + 1)
                    v.scalar_tensor_tensor(out=h[:, u, :], in0=h[:, u, :], scalar=moments[:, u, 0:1],
                                           in1=gain[:, :], op0=ALU.subtract, op1=ALU.mult).then_inc(ln_gained, 1)
                    if after:
                        stats_of(*after)
                    v.wait_ge(ln_gained, n + 1)
                    v.wait_ge(ln_rstd, n * 2 + 2)
                    v.scalar_tensor_tensor(out=h[:, u, :], in0=h[:, u, :], scalar=rstd[:, u, 0:1],
                                           in1=shift[:, :], op0=ALU.mult, op1=ALU.add).then_inc(ln_done, 1)

                for step_of in (sum1_of, sum2_of, stats_of):
                    step_of(0, 0, 0)
                v.wait_ge(consts_in, 32)
                with v.Fori(0, NT // RING - 1) as i:
                    for u in range(RING):
                        tile(i, u, last=False)
                for u in range(RING):
                    tile(NT // RING - 1, u, last=(u == RING - 1))


def encoder_block(nc, x, meta_tokens, ln0_g, ln0_b, w_in, attn_sinks, conv_w, w_attn_out, w_conv_out, w_o,
                  ln1_g, ln1_b, w_router_group, b_router_group, w_router_expert, b_router_expert,
                  w_exp_gate, w_exp_up, w_exp_down, ln2_g, ln2_b, out):
    x2, out2 = x[0], out[0]
    S, D = x2.shape
    E = w_router_expert.shape[2]
    NT = S // P
    slot_tiles = 2 * NT + E + 1
    slot_tiles += slot_tiles % 2
    t = dict(meta=meta_tokens, ln0_g=ln0_g, ln0_b=ln0_b, ln1_g=ln1_g[0], ln1_b=ln1_b[0], ln2_g=ln2_g[0],
             ln2_b=ln2_b[0], sinks=attn_sinks[0], conv_w=conv_w[0], w_rg=w_router_group[0],
             b_rg=b_router_group[0], w_re=w_router_expert[0], b_re=b_router_expert[0],
             w_gate=w_exp_gate[0], w_up=w_exp_up[0], w_down=w_exp_down[0])
    h1 = nc.dram_tensor("h1_rows", [TOK + S, D], FP32).ap()
    ys = nc.dram_tensor("expert_rows", [slot_tiles * P, D], FP32).ap()
    with ExitStack() as ctx:
        def sb(name, shape, dt=FP32):
            return ctx.enter_context(nc.sbuf_tensor(name, shape, dt))
        logits = sb("logits", [P, NT, w_router_group.shape[2] + E])
        mixer(nc, t, x2, w_in[0], w_attn_out[0], w_conv_out[0], w_o[0], h1, logits)
        keep = (sb("slot1", [P, NT], I32), sb("slot2", [P, NT], I32), sb("weight1", [P, NT]),
                sb("weight2", [P, NT]), sb("slot_token", [P, slot_tiles], I32), sb("bounds", [P, 5, E], I32),
                slot_tiles)
        route(nc, t, logits, keep)
        experts(nc, t, h1, ys, keep)
        combine(nc, t, h1, ys, out2, keep)


_INS = ["x", "meta_tokens", "ln0_g", "ln0_b", "w_in", "attn_sinks", "conv_w", "w_attn_out", "w_conv_out", "w_o",
        "ln1_g", "ln1_b", "w_router_group", "b_router_group", "w_router_expert", "b_router_expert",
        "w_exp_gate", "w_exp_up", "w_exp_down", "ln2_g", "ln2_b"]


def kernel(**inputs):
    import numpy as _np
    import concourse.bacc as _bacc
    from concourse import mybir as _mybir
    from concourse.bass_utils import run_bass_kernel_spmd as _run

    nc = _bacc.Bacc("TRN2", target_bir_lowering=False, num_devices=1)
    arrays, args = {}, []
    for name in _INS:
        a = _np.ascontiguousarray(inputs[name])
        arrays[f"in_{name}_dram"] = a
        args.append(nc.dram_tensor(f"in_{name}_dram", a.shape, _mybir.dt.from_np(a.dtype), kind="ExternalInput").ap())
    shape = arrays["in_x_dram"].shape
    args.append(nc.dram_tensor("out_0_dram", shape, _mybir.dt.float32, kind="ExternalOutput").ap())
    encoder_block(nc, *args)
    r = _run(nc, [arrays], core_ids=[0])
    return r.results[0]["out_0_dram"]
```
